# Optimizing a Trainium2 kernel written in Bass

```python
import jax, jax.numpy as jnp
from jax import lax
import numpy as np

D_MODEL = 1024
BATCH = 1
SEQ = 512
DEPTH = 1

HEAD_DIM = 64
FOX_HEADS = 8
SB_HEADS = 4
POOL_GROUPS = 4
POOL_WINDOWS = (2, 4, 8, 16)
POOL_GROUP_DIM = 64
FOX_W = FOX_HEADS * HEAD_DIM
SB_W = SB_HEADS * HEAD_DIM
POOL_W = POOL_GROUPS * POOL_GROUP_DIM
D_MIX = FOX_W + POOL_W + SB_W
Q_BLOCK = 128
EPS = 1e-6
NEG = -1e30

IN_SPLITS = (
    FOX_W, FOX_W, FOX_W, FOX_W,
    FOX_HEADS,
    POOL_W, POOL_W,
    SB_W, SB_W, SB_W, SB_W,
)
D_IN = sum(IN_SPLITS)


def rms_norm(x, g):
    xf = x.astype(jnp.float32)
    y = xf * lax.rsqrt(jnp.mean(xf * xf, axis=-1, keepdims=True) + EPS)
    return (y * g.astype(jnp.float32)).astype(x.dtype)

def to_heads(t, n_heads):
    b, s, _ = t.shape
    return t.reshape(b, s, n_heads, HEAD_DIM).transpose(0, 2, 1, 3)

def from_heads(t):
    b, h, s, d = t.shape
    return t.transpose(0, 2, 1, 3).reshape(b, s, h * d)

def split_blocks(t):
    b, h, s = t.shape[:3]
    nb = s // Q_BLOCK
    t = t.reshape((b, h, nb, Q_BLOCK) + t.shape[3:])
    return jnp.moveaxis(t, 2, 0)

def merge_blocks(o):
    nb, b, h, qb, d = o.shape
    return jnp.moveaxis(o, 0, 2).reshape(b, h, nb * qb, d)

def forgetting_attention(q, k, v, log_f):
    s_len, d = q.shape[2], q.shape[3]
    c = jnp.cumsum(log_f, axis=-1)
    kpos = jnp.arange(s_len)
    scale = d ** -0.5

    def one_block(args):
        qi, ci, i = args
        qpos = i * Q_BLOCK + jnp.arange(Q_BLOCK)
        sc = jnp.einsum('bhqd,bhkd->bhqk', qi, k).astype(jnp.float32) * scale
        sc = sc + (ci[..., :, None] - c[..., None, :])
        sc = jnp.where(kpos[None, :] <= qpos[:, None], sc, NEG)
        p = jax.nn.softmax(sc, axis=-1)
        return jnp.einsum('bhqk,bhkd->bhqd', p.astype(v.dtype), v)

    nb = s_len // Q_BLOCK
    o = lax.map(one_block, (split_blocks(q), split_blocks(c), jnp.arange(nb)))
    return merge_blocks(o)

def stick_breaking_attention(q, k, v):
    s_len, d = q.shape[2], q.shape[3]
    kpos = jnp.arange(s_len)
    scale = d ** -0.5

    def one_block(args):
        qi, i = args
        qpos = i * Q_BLOCK + jnp.arange(Q_BLOCK)
        z = jnp.einsum('bhqd,bhkd->bhqk', qi, k).astype(jnp.float32) * scale
        causal = kpos[None, :] < qpos[:, None]
        log_1m_beta = jnp.where(causal, -jax.nn.softplus(z), 0.0)
        rest = lax.cumsum(log_1m_beta, axis=3, reverse=True) - log_1m_beta
        a = jnp.where(causal, jnp.exp(jax.nn.log_sigmoid(z) + rest), 0.0)
        return jnp.einsum('bhqk,bhkd->bhqd', a.astype(v.dtype), v)

    nb = s_len // Q_BLOCK
    o = lax.map(one_block, (split_blocks(q), jnp.arange(nb)))
    return merge_blocks(o)

def causal_window_mean(x, w):
    s_len = x.shape[1]
    xf = x.astype(jnp.float32)
    cs = jnp.cumsum(xf, axis=1)
    cs_prev = jnp.pad(cs, ((0, 0), (w, 0), (0, 0)))[:, :s_len]
    count = jnp.minimum(jnp.arange(s_len) + 1, w).astype(jnp.float32)
    return ((cs - cs_prev) / count[None, :, None]).astype(x.dtype)

def multiscale_pool(x, w_pool, scale):
    b, s_len, _ = x.shape
    groups = jnp.split(x, POOL_GROUPS, axis=-1)
    pooled = jnp.stack([causal_window_mean(g, w) - g for g, w in zip(groups, POOL_WINDOWS)], axis=2)
    y = jnp.einsum('bsgc,gcd->bsgd', pooled, w_pool).reshape(b, s_len, POOL_W)
    return y * scale

def hybrid_layer(x, norm_g, w_in, b_f, q_norm_g, k_norm_g, w_pool, pool_scale, w_out):
    h = rms_norm(x, norm_g)
    proj = jnp.einsum('bsd,de->bse', h, w_in)
    idx = np.cumsum(IN_SPLITS)[:-1].tolist()
    (fq, fk, fv, fg, ff, px, pg, sq, sk, sv, sg) = jnp.split(proj, idx, axis=-1)

    fq = rms_norm(to_heads(fq, FOX_HEADS), q_norm_g)
    fk = rms_norm(to_heads(fk, FOX_HEADS), k_norm_g)
    fv = to_heads(fv, FOX_HEADS)
    log_f = jax.nn.log_sigmoid((ff + b_f).astype(jnp.float32)).transpose(0, 2, 1)
    fox_out = from_heads(forgetting_attention(fq, fk, fv, log_f)) * jax.nn.silu(fg)

    pool_out = multiscale_pool(px, w_pool, pool_scale) * jax.nn.silu(pg)

    sb = stick_breaking_attention(to_heads(sq, SB_HEADS), to_heads(sk, SB_HEADS), to_heads(sv, SB_HEADS))
    sb_out = from_heads(sb) * jax.nn.silu(sg)

    mixed = jnp.concatenate([fox_out, pool_out, sb_out], axis=-1)
    return x + jnp.einsum('bse,ed->bsd', mixed, w_out)

def first_inputs(seed: int = 0) -> dict:
    key = jax.random.key(seed)
    ks = jax.random.split(key, 10)
    x = jax.random.normal(ks[0], (BATCH, SEQ, D_MODEL), jnp.float32)
    norm_g = 1.0 + 0.02 * jax.random.normal(ks[1], (DEPTH, D_MODEL), jnp.float32)
    w_in = jax.random.normal(ks[2], (DEPTH, D_MODEL, D_IN), jnp.float32) * D_MODEL ** -0.5
    b_f = jax.random.uniform(ks[3], (DEPTH, FOX_HEADS), jnp.float32, 1.0, 4.0)
    q_norm_g = 1.0 + 0.02 * jax.random.normal(ks[4], (DEPTH, HEAD_DIM), jnp.float32)
    k_norm_g = 1.0 + 0.02 * jax.random.normal(ks[5], (DEPTH, HEAD_DIM), jnp.float32)
    w_pool = jax.random.normal(ks[6], (DEPTH, POOL_GROUPS, POOL_GROUP_DIM, POOL_GROUP_DIM), jnp.float32) * POOL_GROUP_DIM ** -0.5
    pool_scale = 1.0 + 0.02 * jax.random.normal(ks[7], (DEPTH, POOL_W), jnp.float32)
    w_out = jax.random.normal(ks[8], (DEPTH, D_MIX, D_MODEL), jnp.float32) * D_MIX ** -0.5
    return {"x": x, "norm_g": norm_g, "w_in": w_in, "b_f": b_f, "q_norm_g": q_norm_g,
            "k_norm_g": k_norm_g, "w_pool": w_pool, "pool_scale": pool_scale, "w_out": w_out}

def first_block(x, norm_g, w_in, b_f, q_norm_g, k_norm_g, w_pool, pool_scale, w_out):
    for l in range(DEPTH):
        x = hybrid_layer(x, norm_g[l], w_in[l], b_f[l], q_norm_g[l], k_norm_g[l],
                         w_pool[l], pool_scale[l], w_out[l])
    return x


PLE_DIM = 256
MIX_WIDTH = D_MODEL
ATTN_WIDTH = MIX_WIDTH // 2
CONV_WIDTH = MIX_WIDTH - ATTN_WIDTH
V_DIM = 64
NOPE_DIM = 64
ROPE_DIM = 32
N_ATTN_HEADS = ATTN_WIDTH // V_DIM
Q_RANK = D_MODEL // 4
KV_RANK = D_MODEL // 4
N_CONV_GROUPS = 8
CONV_K = 3
IN_COLS = Q_RANK + KV_RANK + ROPE_DIM + 3 * CONV_WIDTH
D_FF = ((8 * D_MODEL // 3 + 255) // 256) * 256
ROPE_THETA = 10000.0


def rmsnorm(x, g):
    xf = x.astype(jnp.float32)
    y = xf * lax.rsqrt(jnp.mean(xf * xf, axis=-1, keepdims=True) + EPS)
    return (y * g.astype(jnp.float32)).astype(x.dtype)

def rope_tables(positions, dtype):
    half = ROPE_DIM // 2
    inv_freq = 1.0 / (ROPE_THETA ** (jnp.arange(half, dtype=jnp.float32) / half))
    ang = positions.astype(jnp.float32)[..., None] * inv_freq
    return jnp.cos(ang).astype(dtype), jnp.sin(ang).astype(dtype)

def apply_rope(t, cos, sin):
    t1, t2 = jnp.split(t, 2, axis=-1)
    return jnp.concatenate([t1 * cos - t2 * sin, t2 * cos + t1 * sin], axis=-1)

def causal_block_attention(q, k, v):
    B, S, H, Dq = q.shape
    Dv = v.shape[-1]
    nb = S // Q_BLOCK
    scale = Dq ** -0.5
    qb = q.reshape(B, nb, Q_BLOCK, H, Dq).transpose(1, 0, 2, 3, 4)
    k_idx = jnp.arange(S)

    def one_block(args):
        q_blk, blk = args
        q_idx = blk * Q_BLOCK + jnp.arange(Q_BLOCK)
        s = jnp.einsum('bqhd,bkhd->bhqk', q_blk, k).astype(jnp.float32) * scale
        s = jnp.where(k_idx[None, :] <= q_idx[:, None], s, jnp.finfo(jnp.float32).min)
        pr = jax.nn.softmax(s, axis=-1)
        return jnp.einsum('bhqk,bkhd->bqhd', pr.astype(v.dtype), v)

    out = lax.map(one_block, (qb, jnp.arange(nb)))
    return out.transpose(1, 0, 2, 3, 4).reshape(B, S, H * Dv)

def mla(c_q_raw, c_kv_raw, k_rope_raw, positions, q_norm, kv_norm, w_uq, w_ukv):
    B, S, _ = c_q_raw.shape
    H = N_ATTN_HEADS
    q = (rmsnorm(c_q_raw, q_norm) @ w_uq).reshape(B, S, H, NOPE_DIM + ROPE_DIM)
    kv = (rmsnorm(c_kv_raw, kv_norm) @ w_ukv).reshape(B, S, H, NOPE_DIM + V_DIM)
    k_nope, v = kv[..., :NOPE_DIM], kv[..., NOPE_DIM:]
    cos, sin = rope_tables(positions, q.dtype)
    q_rope = apply_rope(q[..., NOPE_DIM:], cos[:, :, None, :], sin[:, :, None, :])
    k_rope = apply_rope(k_rope_raw, cos, sin)
    q_full = jnp.concatenate([q[..., :NOPE_DIM], q_rope], axis=-1)
    k_full = jnp.concatenate(
        [k_nope, jnp.broadcast_to(k_rope[:, :, None, :], (B, S, H, ROPE_DIM))], axis=-1)
    return causal_block_attention(q_full, k_full, v)

def short_gated_conv(b_gate, c_gate, xv, conv_w):
    S = xv.shape[1]
    u = c_gate * xv
    u_pad = jnp.pad(u, ((0, 0), (CONV_K - 1, 0), (0, 0)))
    y = conv_w[0] * u_pad[:, CONV_K - 1:CONV_K - 1 + S]
    for k in range(1, CONV_K):
        y = y + conv_w[k] * u_pad[:, CONV_K - 1 - k:CONV_K - 1 - k + S]
    return b_gate * y

def second_inputs(seed: int = 0) -> dict:
    key = jax.random.key(seed)
    ks = jax.random.split(key, 24)
    f32 = jnp.float32

    def w(k, shape, fan_in):
        return jax.random.normal(k, shape, f32) * (fan_in ** -0.5)

    def gain(k, shape):
        return 1.0 + 0.05 * jax.random.normal(k, shape, f32)

    L = DEPTH
    x = jax.random.normal(ks[0], (BATCH, SEQ, D_MODEL), f32)
    p = jax.random.normal(ks[1], (DEPTH, BATCH, SEQ, PLE_DIM), f32)
    offset = jax.random.randint(ks[2], (BATCH, 1), 0, 4096)
    positions = (offset + jnp.arange(SEQ, dtype=jnp.int32)[None, :]).astype(jnp.int32)
    return {
        "x": x,
        "p": p,
        "positions": positions,
        "mix_pre_norm": gain(ks[3], (L, D_MODEL)),
        "w_in": w(ks[4], (L, D_MODEL, IN_COLS), D_MODEL),
        "q_norm": gain(ks[5], (L, Q_RANK)),
        "kv_norm": gain(ks[6], (L, KV_RANK)),
        "w_uq": w(ks[7], (L, Q_RANK, N_ATTN_HEADS * (NOPE_DIM + ROPE_DIM)), Q_RANK),
        "w_ukv": w(ks[8], (L, KV_RANK, N_ATTN_HEADS * (NOPE_DIM + V_DIM)), KV_RANK),
        "conv_w": w(ks[9], (L, CONV_K, CONV_WIDTH), CONV_K),
        "attn_group_norm": gain(ks[10], (L, ATTN_WIDTH)),
        "conv_group_norm": gain(ks[11], (L, CONV_WIDTH)),
        "w_out": w(ks[12], (L, MIX_WIDTH, D_MODEL), MIX_WIDTH),
        "mix_post_norm": gain(ks[13], (L, D_MODEL)),
        "ffn_pre_norm": gain(ks[14], (L, D_MODEL)),
        "w_gate": w(ks[15], (L, D_MODEL, D_FF), D_MODEL),
        "w_up": w(ks[16], (L, D_MODEL, D_FF), D_MODEL),
        "w_down": w(ks[17], (L, D_FF, D_MODEL), D_FF),
        "ffn_post_norm": gain(ks[18], (L, D_MODEL)),
        "w_ple_proj": w(ks[19], (L, PLE_DIM, D_MODEL), PLE_DIM),
        "ple_norm": gain(ks[20], (L, D_MODEL)),
        "w_ple_gate": w(ks[21], (L, D_MODEL, D_MODEL), D_MODEL),
    }

def second_block(x, p, positions, mix_pre_norm, w_in, q_norm, kv_norm, w_uq, w_ukv,
              conv_w, attn_group_norm, conv_group_norm, w_out, mix_post_norm,
              ffn_pre_norm, w_gate, w_up, w_down, ffn_post_norm,
              w_ple_proj, ple_norm, w_ple_gate):
    o1 = Q_RANK
    o2 = o1 + KV_RANK
    o3 = o2 + ROPE_DIM
    o4 = o3 + CONV_WIDTH
    o5 = o4 + CONV_WIDTH
    for i in range(DEPTH):
        h = rmsnorm(x, mix_pre_norm[i])
        z = h @ w_in[i]
        a = mla(z[..., :o1], z[..., o1:o2], z[..., o2:o3], positions,
                q_norm[i], kv_norm[i], w_uq[i], w_ukv[i])
        c = short_gated_conv(z[..., o3:o4], z[..., o4:o5], z[..., o5:], conv_w[i])
        m = jnp.concatenate([rmsnorm(a, attn_group_norm[i]),
                             rmsnorm(c, conv_group_norm[i])], axis=-1)
        x = x + rmsnorm(m @ w_out[i], mix_post_norm[i])
        h = rmsnorm(x, ffn_pre_norm[i])
        f = (jax.nn.silu(h @ w_gate[i]) * (h @ w_up[i])) @ w_down[i]
        x = x + rmsnorm(f, ffn_post_norm[i])
        e = rmsnorm(p[i] @ w_ple_proj[i], ple_norm[i])
        x = x + jax.nn.sigmoid(x @ w_ple_gate[i]) * e
    return x


def setup_inputs(seed=0):
    out = dict(first_inputs(seed))
    for name, value in second_inputs(seed + 1).items():
        if name != "x":
            out[name + "_2"] = value
    return out


def reference(
    x, norm_g, w_in, b_f, q_norm_g, k_norm_g, w_pool, pool_scale, w_out, p_2, positions_2,
    mix_pre_norm_2, w_in_2, q_norm_2, kv_norm_2, w_uq_2, w_ukv_2, conv_w_2, attn_group_norm_2,
    conv_group_norm_2, w_out_2, mix_post_norm_2, ffn_pre_norm_2, w_gate_2, w_up_2, w_down_2,
    ffn_post_norm_2, w_ple_proj_2, ple_norm_2, w_ple_gate_2,
):
    x = first_block(
        x, norm_g, w_in, b_f, q_norm_g, k_norm_g, w_pool, pool_scale, w_out,
    )
    return second_block(
        x, p_2, positions_2, mix_pre_norm_2, w_in_2, q_norm_2, kv_norm_2, w_uq_2, w_ukv_2,
        conv_w_2, attn_group_norm_2, conv_group_norm_2, w_out_2, mix_post_norm_2,
        ffn_pre_norm_2, w_gate_2, w_up_2, w_down_2, ffn_post_norm_2, w_ple_proj_2, ple_norm_2,
        w_ple_gate_2,
    )


_drawn_inputs = setup_inputs


def setup_inputs(seed=0):
    import zlib

    import numpy as np

    out = dict(_drawn_inputs(seed))
    spreads = {}
    factors = {'norm_g': 3.305,
     'q_norm_g': 31.107,
     'k_norm_g': 28.742,
     'pool_scale': 21.964,
     'ple_norm_2': 121.162,
     'mix_pre_norm_2': 8.0,
     'q_norm_2': 8.0,
     'kv_norm_2': 8.0,
     'attn_group_norm_2': 64.0,
     'conv_group_norm_2': 64.0,
     'mix_post_norm_2': 61.913,
     'ffn_pre_norm_2': 45.378,
     'ffn_post_norm_2': 63.124}
    for name, (base, spread) in spreads.items():
        noise = np.random.default_rng([zlib.crc32(name.encode()), seed]).standard_normal(out[name].shape)
        drawn = base * np.exp(spread * noise) if base else spread * noise
        out[name] = __import__('jax').numpy.asarray(drawn.astype(out[name].dtype))
    for name, factor in factors.items():
        out[name] = (out[name] * factor).astype(out[name].dtype)
    return out
```

```python
from contextlib import ExitStack

import numpy as np

import concourse.bass as bass
from concourse import mybir

P = 128
F32 = mybir.dt.float32
F32R = mybir.dt.float32r
BF16 = mybir.dt.bfloat16
I32 = mybir.dt.int32
ALU = mybir.AluOpType
ACT = mybir.ActivationFunctionType
AX_X = mybir.AxisListType.X

LOG_EXP = "natural_log_exp_and_others"

S, D = 512, 1024
T = S // P
KD = D // P
HD = 64
FOX_H, SB_H, MLA_H = 8, 4, 8
ROPE, HALF = 32, 16
QK2 = HD + ROPE
RANK = 256
SF_W = SB_H * HD + FOX_H
LQ_W = RANK + ROPE
UQ_W = MLA_H * QK2
FF = 2816
NF = FF // P
EPS = 1e-6
NEG = -1e30
PAD = 16
WINDOWS = (2, 4, 8, 16)
KERNEL = 3

CW = 1024
SLOTS = 4
RAW = 2

CHUNKS = (("fq", 4), ("fv", 4), ("fk", 4), ("sf", 3), ("pg", 2), ("px", 2), ("fg", 4), ("sg", 2), ("sq", 2),
          ("sk", 2), ("out1", 8), ("lq", 3), ("lkv", 2), ("conv", 12), ("uq", 2), ("uk", 1), ("uv", 1),
          ("out2", 8), ("ffn", 2 * NF), ("down", NF), ("ple", 2), ("pgate", 8))
CH, NCH = {}, 0
for _name, _n in CHUNKS:
    CH[_name] = NCH
    NCH += _n

SHARED = (CH["ffn"] + 3, CH["ple"] + 3)

COLS, NCOL = {}, 0
for _name, _n in (("gq", 1), ("gk", 1), ("gq2", 2), ("gkv2", 2), ("conv", 4 * KERNEL), ("ga", 4), ("gc", 4), ("ps", 2),
                  ("bf", FOX_H), ("invf", HALF), ("rc", 2 * PAD), ("invw", 2)):
    COLS[_name] = NCOL
    NCOL += _n

PI_A = 6.28125
PI_B = float(np.round((2 * np.pi - PI_A) * 2.0**21) / 2.0**21)
PI_C = float(np.float32(2 * np.pi - PI_A - PI_B))
ROUND = 1.5 * 2.0**23


def psum_tiles():
    tiles = {}
    for n in range(2 * T):
        tiles["h1", n] = (n, "dve", None)

    def group(name, banks, drainer, width_chunks, n=T):
        for t in range(n):
            tiles[name, t] = (banks[t % len(banks)], drainer, CH[width_chunks[0]] + width_chunks[1] if t == n - 1 else None)

    group("fq", (0, 1, 2, 3), "act", ("fq", 3))
    group("fv", (4, 5, 6, 7), "act", ("fv", 3))
    for i in range(FOX_H):
        tiles["qT", i] = (i, "act", None)
    group("fk", (0, 1, 2, 3), "act", ("fk", 3))
    group("sf", (4, 5, 6, 7), "act", ("sf", 2))
    for i in range(FOX_H):
        tiles["kT", i] = (i, "act", None)
    n = 0
    for name in ("pg", "px", "lfT", "y", "fg", "sg", "sq", "sk"):
        for i in range({"lfT": 1, "fg": 4}.get(name, 2)):
            tiles[name, i] = (n % 8, "dve" if name in ("px", "lfT", "y") else "act", None if name in ("lfT", "y") else CH[name] + i)
            n += 1
    for g in range(2):
        for t in range(T):
            tiles["out1", g, t] = (4 * g + t, "dve", CH["out1"] + 4 * g + 3 if t == T - 1 else None)
    for n in range(2 * T):
        tiles["h2", n] = (n, "dve", None)
    group("lq", (0, 1, 2, 3), "act", ("lq", 2))
    group("lkv", (4, 5, 6, 7), "act", ("lkv", 1))
    n = 0
    for j in range(4):
        for i, name in enumerate(("c", "xv", "b")):
            tiles[name, j] = (n % 8, "act" if name == "c" else "dve", CH["conv"] + 3 * j + i)
            n += 1
    for i in range(4):
        tiles["latT", i] = (4 + i, "dve", None)
    tiles["krT", 0] = (0, "act", None)
    for t in range(T):
        for g in range(2):
            tiles["uq", t, g] = (2 * t + g, "act", CH["uq"] + 1 if (t, g) == (T - 1, 1) else None)
    for i in range(4):
        tiles["uk", i] = (i, "act", CH["uk"] if i == 3 else None)
    group("uv", (4, 5, 6, 7), "act", ("uv", 0))
    for i in range(MLA_H):
        tiles["q2T", i] = (i, "act", None)
    tiles["ss2", 0] = (0, "dve", None)
    for g in range(2):
        for half in range(2):
            for t in range(T):
                tiles["out2", g, half, t] = (4 * half + t, "act" if half == 0 else "dve",
                                             CH["out2"] + 4 * g + 2 * half + 1 if t == T - 1 else None)
    for n in range(2 * T):
        tiles["h3", n] = (n, "dve", None)
    for t in range(T):
        for g in range(2):
            tiles["down", t, g] = (2 * t + g, "dve", CH["down"] + NF - 1 if (t, g) == (T - 1, 1) else None)
    for g in range(2):
        for t in range(T):
            tiles["ple", g, t] = (2 * t + g, "act", CH["ple"] + g if t == T - 1 else None)
    for n in range(2 * T):
        tiles["xT", n] = (n, "dve", None)
    for g in range(2):
        for t in range(T):
            tiles["pgate", g, t] = (4 * g + t, "act", CH["pgate"] + 4 * g + 3 if t == T - 1 else None)
    return tiles


def tile_counts(tiles):
    full, drained, before, out = 0, {"act": 0, "dve": 0}, {}, {}
    for key, (bank, drainer, chunk) in tiles.items():
        if chunk is None:
            full += 1
        drained[drainer] += 1
        own = (drainer, drained[drainer])
        out[key] = (bank, ("tile", full) if chunk is None else ("chunk", chunk + 1), before.get(bank), own)
        before[bank] = own
    return out


def hybrid_kernel(nc, x_d, w_d, cols_d, pos_d, wpool_d, pt_d, gains_d, out_d):
    tiles = tile_counts(psum_tiles())
    with ExitStack() as ctx:
        def sb(name, shape, dt=F32):
            return ctx.enter_context(nc.sbuf_tensor(name, shape, dt))

        def sem(name):
            return ctx.enter_context(nc.semaphore(name))

        x = sb("x", [P, T, D])
        h = sb("h", [P, 2, D])
        aT_hi = sb("aT_hi", [P, KD, S], F32R)
        aT_lo = sb("aT_lo", [P, KD, S], F32R)
        raw = sb("raw", [P, RAW, CW])
        w_hi = sb("w_hi", [P, SLOTS, CW], F32R)
        w_lo = sb("w_lo", [P, SLOTS, CW], F32R)
        g_pre = sb("g_pre", [P, D])
        g_post = sb("g_post", [P, D])
        PT = sb("PT", [P, 2, T, S])
        arena = sb("arena", [P, 19488])
        ident = sb("ident", [P, P])
        ident_b = sb("ident_b", [P, P], BF16)
        mask_le = sb("mask_le", [P, P], BF16)
        mask_lt = sb("mask_lt", [P, P], BF16)
        neg_tri = sb("neg_tri", [P, P])
        neg_one = sb("neg_one", [P, P])
        ones = sb("ones", [P, 1])
        cols = sb("cols", [P, NCOL])
        wpool = sb("wpool", [P, 2, P])
        pos_i = sb("pos_i", [P, T], I32)
        pos_f = sb("pos_f", [P, T])
        cs = sb("cs", [P, 2, T, HALF])
        stat = sb("stat", [P, 4, 64])
        negmax = sb("negmax", [P, 8])
        esum = sb("esum", [P, 8])
        erec = sb("erec", [P, 8])
        bank = [ctx.enter_context(nc.psum_tensor(f"bank{i}", [P, 512], F32)) for i in range(8)]

        P_buf = h[:, :, :].rearrange("p a (b c) -> p (a b) c", c=S)
        PTf = PT[:, :, :, :].rearrange("p a b c -> p (a b c)")

        def view(base, at, *shape):
            v = base[:, at:at + int(np.prod(shape))]
            if len(shape) == 2:
                v = v.rearrange("p (a b) -> p a b", b=shape[1])
            elif len(shape) == 3:
                v = v.rearrange("p (a b c) -> p a b c", b=shape[1], c=shape[2])
            return v

        def ar(at, *shape):
            return view(arena, at, *shape)

        def col(name, i=0, n=1):
            return cols[:, COLS[name] + i:COLS[name] + i + n]

        qk_raw = ar(0, T, S)
        fv = ar(2048, T, S)
        sf = ar(4096, T, SF_W)
        gate = ar(5152, KD, S)
        sqT = ar(9248, 2, S)
        skT = ar(10272, 2, S)
        q_aug = ar(11296, FOX_H, S)
        k_aug = ar(15392, FOX_H, S)
        sq_tmp = view(PTf, 0, 2, S)
        xp = view(PTf, 1024, 3, S + PAD)
        pooled = view(PTf, 2608, 2, S)
        lf = view(PTf, 3632, 3, T * FOX_H)
        cum = ar(0, 2, S)[0:FOX_H]
        sp = [PT[:, 0, :, :], ar(11296, T, S)]
        az = [PT[:, 1, :, :], ar(13344, T, S)]
        ea = [ar(15392, T, S), ar(17440, T, S)]
        y = ar(0, 4, S)
        u = ar(2048, 2, S + KERNEL - 1)
        sqs = ar(3076, 2, S)
        sq2 = ar(4100, 2, S)
        q2 = ar(5124, T, UQ_W)
        q2T = ar(8196, MLA_H, S)
        k2T = ar(12292, MLA_H, S)
        v2 = ar(16388, T, S)
        lat_q = ar(16388, T, LQ_W)
        lat_kv = ar(5124, T, RANK)
        rope_t = view(PTf, 0, 4, MLA_H * HALF)
        y2 = ar(8196, T, D)
        act = ar(0, NF, S)
        sg_t = ar(11264, 2, S)
        emb = ar(12288, T, D)
        pe_raw = view(PTf, 0, 2, S)
        post_t = view(PTf, 1024, 2, D)
        gate_t = view(PTf, 3072, 2, S)

        x_in = [sem(f"x_in{t}") for t in range(T)]
        raw_in = [sem(f"raw_in{i}") for i in range(RAW)]
        const_in = sem("const_in")
        g_pre_in, g_post_in = sem("g_pre_in"), sem("g_post_in")
        pt_in = sem("pt_in")
        rows_laid, c_rows_in = sem("rows_laid"), sem("c_rows_in")
        out_stored = sem("out_stored")
        masks_made = sem("masks_made")
        hi_made, hi_shared, w_split, w_used = sem("hi_made"), sem("hi_shared"), sem("w_split"), sem("w_used")
        tile_full = sem("tile_full")
        drained = {"act": sem("drained_act"), "dve": sem("drained_dve")}
        sq_done = sem("sq_done")
        ms_made = sem("ms_made")
        rs_made = sem("rs_made")
        h_made, h_hi = sem("h_made"), sem("h_hi")
        act_step, dve_step = sem("act_step"), sem("dve_step")
        qk_squared, qk_reduced, qk_scaled = sem("qk_squared"), sem("qk_reduced"), sem("qk_scaled")
        gated = sem("gated")
        lf_abs, lf_exp, lf_made, cum_made = sem("lf_abs"), sem("lf_exp"), sem("lf_made"), sem("cum_made")
        pooled_made = sem("pooled_made")
        sines = sem("sines")
        angles = sem("angles")
        scored, maxed, exped, normed = sem("scored"), sem("maxed"), sem("exped"), sem("normed")
        turned, pt_made, pv_done, pv_drained = sem("turned"), sem("pt_made"), sem("pv_done"), sem("pv_drained")
        z_full, z_abs, z_exp, z_ln, sp_made = sem("z_full"), sem("z_abs"), sem("z_exp"), sem("z_ln"), sem("sp_made")
        rest_full, a_made, sb_full, sb_drained = sem("rest_full"), sem("a_made"), sem("sb_full"), sem("sb_drained")
        mix_hi, mix_lo = sem("mix_hi"), sem("mix_lo")
        x_new = sem("x_new")
        lat_scaled, roped, conv_c, conv_y, sq_y = (sem("lat_scaled"), sem("roped"), sem("conv_c"), sem("conv_y"),
                                                   sem("sq_y"))
        sqs_made = sem("sqs_made")
        group_rsqrt, y2_made = sem("group_rsqrt"), sem("y2_made")
        ffn_gate, ffn_act = sem("ffn_gate"), sem("ffn_act")
        stage_hi, staged = sem("stage_hi"), sem("staged")
        p_hi, p_split = sem("p_hi"), sem("p_split")
        pgate_made, out_made = sem("pgate_made"), sem("out_made")

        def full(eng, key):
            kind, n = tiles[key][1]
            eng.wait_ge(tile_full if kind == "tile" else w_used, n)

        def tbank(key):
            return bank[tiles[key][0]]

        block = ctx.enter_context(nc.Block())

        @block.sync
        def _(sp_):
            for t in range(T):
                sp_.dma_start(x[:, t, :], x_d[t * P:(t + 1) * P, :]).then_inc(x_in[t], 16)

            def load(c, first, r):
                if not first:
                    sp_.wait_ge(w_split, c - RAW + 1)
                src = w_d[bass.ds(c, 1), :, :].rearrange("a p c -> p (a c)")
                sp_.dma_start(raw[:, r, :], src).then_inc(raw_in[r], 16)

            for r in range(RAW):
                load(r, True, r)
            with sp_.Fori(1, NCH // RAW) as i:
                for r in range(RAW):
                    load(i * RAW + r, False, r)
            for n in range(2 * T):
                g, t = n // T, n % T
                sp_.wait_ge(out_made, n + 1)
                sp_.dma_start(out_d[t * P:(t + 1) * P, g * 512:(g + 1) * 512],
                              x[:, t, g * 512:(g + 1) * 512]).then_inc(out_stored, 16)
            sp_.wait_ge(out_stored, 2 * T * 16)

        @block.gpsimd
        def _(pool):
            nc.gpsimd.memset(ident[:, :], 0.0).then_inc(masks_made, 1)
            nc.gpsimd.memset(ident_b[:, :], 0.0).then_inc(masks_made, 1)
            nc.gpsimd.memset(mask_le[:, :], 0.0).then_inc(masks_made, 1)
            nc.gpsimd.memset(mask_lt[:, :], 0.0).then_inc(masks_made, 1)
            nc.gpsimd.memset(neg_tri[:, :], -1.0).then_inc(masks_made, 1)
            nc.gpsimd.memset(neg_one[:, :], -1.0).then_inc(masks_made, 1)
            nc.gpsimd.memset(ones[:, :], 1.0).then_inc(masks_made, 1)
            nc.gpsimd.memset(xp, 0.0).then_inc(masks_made, 1)
            pool.wait_ge(masks_made, 8)
            for m in (ident, ident_b):
                nc.gpsimd.affine_select(out=m[:, :], in_=m[:, :], compare_op=ALU.not_equal, fill=1.0, base=0,
                                        pattern=[[-1, P]], channel_multiplier=1).then_inc(masks_made, 1)
            nc.gpsimd.affine_select(out=mask_le[:, :], in_=mask_le[:, :], compare_op=ALU.is_ge, fill=NEG, base=0,
                                    pattern=[[-1, P]], channel_multiplier=1).then_inc(masks_made, 1)
            nc.gpsimd.affine_select(out=mask_lt[:, :], in_=mask_lt[:, :], compare_op=ALU.is_gt, fill=NEG, base=0,
                                    pattern=[[1, P]], channel_multiplier=-1).then_inc(masks_made, 1)
            nc.gpsimd.affine_select(out=neg_tri[:, :], in_=neg_tri[:, :], compare_op=ALU.is_ge, fill=0.0, base=0,
                                    pattern=[[-1, P]], channel_multiplier=1).then_inc(masks_made, 1)

            def split(c, s, shared, behind, first=False):
                r = s % RAW
                if not shared:
                    pool.wait_ge(raw_in[r], (c - r) * (16 // RAW) + 16)
                    if not first:
                        pool.wait_ge(w_used, c - SLOTS + 1)
                    nc.gpsimd.tensor_tensor(w_hi[:, s, :], raw[:, r, :], ones[:, :].broadcast_to([P, CW]),
                                            ALU.mult).then_inc(hi_made, 1)
                    pool.wait_ge(hi_made, c + (1 - behind))
                else:
                    pool.wait_ge(hi_shared, c + (1 - SHARED[0]))
                nc.gpsimd.tensor_tensor(w_lo[:, s, :], raw[:, r, :], w_hi[:, s, :].bitcast(F32),
                                        ALU.subtract).then_inc(w_split, 1)

            def splits(a, b, shared, behind=0):
                while a < b and (a % SLOTS or b - a < SLOTS or a < SLOTS):
                    split(a, a % SLOTS, shared, behind, first=(a < SLOTS))
                    a += 1
                if a < b:
                    with pool.Fori(a // SLOTS, b // SLOTS) as i:
                        for s in range(SLOTS):
                            split(i * SLOTS + s, s, shared, behind)
                for c in range(b // SLOTS * SLOTS if a < b else b, b):
                    split(c, c % SLOTS, shared, behind)

            splits(0, SHARED[0], False)
            splits(SHARED[0], SHARED[1], True)
            splits(SHARED[1], NCH, False, behind=SHARED[1] - SHARED[0])

        @block.tensor
        def _(pe):
            mm = nc.tensor.matmul

            def bank_free(key):
                before = tiles[key][2]
                if before is not None:
                    pe.wait_ge(drained[before[0]], before[1])

            def chunk(c):
                pe.wait_ge(w_split, c + 1)
                return w_hi[:, c % SLOTS, :], w_lo[:, c % SLOTS, :]

            def three(out, st_hi, st_lo, mv_hi, mv_lo, start, stop):
                mm(out, st_hi, mv_hi, start=start, stop=False)
                mm(out, st_hi, mv_lo, start=False, stop=False)
                return mm(out, st_lo, mv_hi, start=False, stop=stop)

            def left(k, t):
                return aT_hi[:, k, t * P:(t + 1) * P], aT_lo[:, k, t * P:(t + 1) * P]

            def weights_moving(keys, chunks, width, k0=0, cut=lambda kk: kk):
                for n, (c, ks) in enumerate(chunks):
                    hi, lo = chunk(c)
                    for t in range(T):
                        if n == 0:
                            bank_free(keys[t])
                        for kk, k in enumerate(ks):
                            at = slice(cut(kk) * width, (cut(kk) + 1) * width)
                            st = left(k0 + k, t)
                            end = n == len(chunks) - 1 and kk == len(ks) - 1
                            last = three(tbank(keys[t])[:, 0:width], st[0], st[1], hi[:, at], lo[:, at],
                                         start=(n == 0 and kk == 0), stop=end)
                        if t == T - 1:
                            last.then_inc(w_used, 1)
                        elif n == len(chunks) - 1:
                            last.then_inc(tile_full, 1)

            def weights_still(key, c):
                hi, lo = chunk(c)
                bank_free(key)
                for k in range(KD):
                    last = three(tbank(key)[:, :], hi[:, k * P:(k + 1) * P], lo[:, k * P:(k + 1) * P],
                                 aT_hi[:, k, :], aT_lo[:, k, :], start=(k == 0), stop=(k == KD - 1))
                last.then_inc(w_used, 1)

            def turn(out, in_):
                return nc.tensor.transpose(out, in_, ident[:, :])

            def turn_rows(name, src, ready, base):
                for n in range(2 * T):
                    t, half = n // 2, n % 2
                    if half == 0:
                        pe.wait_ge(ready, base + t + 1)
                    bank_free((name, n))
                    for b in range(4):
                        last = turn(tbank((name, n))[:, b * P:(b + 1) * P], src(t, 4 * half + b))
                    last.then_inc(tile_full, 1)

            def h_tile(t, k):
                return h[:, t % 2, k * P:(k + 1) * P]

            split_tiles = [0]

            def left_ready(n=2 * T):
                split_tiles[0] += n
                pe.wait_ge(mix_lo, split_tiles[0])

            pairs = [(0, (0, 1)), (1, (2, 3)), (2, (4, 5)), (3, (6, 7))]

            def group4(name):
                return [(CH[name] + i, ks) for i, ks in pairs]

            pe.wait_ge(masks_made, 13)
            turn_rows("h1", h_tile, h_made, 0)
            left_ready()
            weights_moving([("fq", t) for t in range(T)], group4("fq"), S)
            weights_moving([("fv", t) for t in range(T)], group4("fv"), S)

            def turn_heads(name, n, width, src, ready, count):
                pe.wait_ge(ready, count)
                for i in range(n):
                    bank_free((name, i))
                    for t in range(T):
                        last = turn(tbank((name, i))[0:width, t * P:(t + 1) * P], src(t, i))
                    last.then_inc(tile_full, 1)

            turn_heads("qT", FOX_H, HD, lambda t, i: qk_raw[:, t, i * HD:(i + 1) * HD], qk_scaled, 1)
            weights_moving([("fk", t) for t in range(T)], group4("fk"), S)
            weights_moving([("sf", t) for t in range(T)],
                           [(CH["sf"], (0, 1, 2)), (CH["sf"] + 1, (3, 4, 5)), (CH["sf"] + 2, (6, 7))], SF_W)
            turn_heads("kT", FOX_H, HD, lambda t, i: qk_raw[:, t, i * HD:(i + 1) * HD], qk_scaled, 2)
            for name in ("pg", "px"):
                for i in range(2):
                    weights_still((name, i), CH[name] + i)
            pe.wait_ge(lf_made, 1)
            bank_free(("lfT", 0))
            for t in range(T):
                last = turn(tbank(("lfT", 0))[0:FOX_H, t * P:(t + 1) * P], lf[:, 2, t * FOX_H:(t + 1) * FOX_H])
            last.then_inc(tile_full, 1)
            for i in range(2):
                pe.wait_ge(pooled_made, i + 1)
                bank_free(("y", i))
                mm(tbank(("y", i))[:, :], wpool[:, i, :], pooled[:, i, :], start=True, stop=True).then_inc(tile_full, 1)
            for name, n in (("fg", 4), ("sg", 2), ("sq", 2), ("sk", 2)):
                for i in range(n):
                    weights_still((name, i), CH[name] + i)

            LAG = 3

            def softmax_attention(base, heads, width, qT_, kT_, v_):
                steps = heads * T

                def scores(m):
                    i, qb = m // T, m % T
                    n = base + m
                    if m >= 3:
                        pe.wait_ge(exped, n - 2)
                    out = bank[n % 3]
                    kw = (qb + 1) * P
                    mm(out[:, 0:kw], qT_[0:width, i, qb * P:(qb + 1) * P], kT_[0:width, i, 0:kw], start=True,
                       stop=False)
                    mm(out[:, qb * P:kw], ident_b[:, :], mask_le[:, :], start=False, stop=True).then_inc(scored, 1)

                def turn_probs(m):
                    qb = m % T
                    n = base + m
                    pe.wait_ge(normed, n + 1)
                    if m >= 3:
                        pe.wait_ge(pt_made, n - 2)
                    for kb in range(qb + 1):
                        last = turn(bank[3 + n % 3][:, kb * P:(kb + 1) * P], P_buf[:, n % 4, kb * P:(kb + 1) * P])
                    last.then_inc(turned, 1)

                def values(i):
                    pe.wait_ge(pt_made, base + (i + 1) * T)
                    pair = (base // T + i) // 2
                    if i % 2 == 0 and i >= 4:
                        pe.wait_ge(pv_drained, pair - 1)
                    r0 = (i % 2) * HD
                    for kb in range(T):
                        last = mm(bank[6 + pair % 2][r0:r0 + HD, kb * P:S], v_[:, kb, i * HD:(i + 1) * HD],
                                  PT[:, i % 2, kb, kb * P:S], start=(kb == 0), stop=(kb == T - 1),
                                  skip_group_check=True)
                    last.then_inc(pv_done, 1)

                for m in range(steps + LAG + 1):
                    if m < steps:
                        scores(m)
                    if LAG <= m < steps + LAG:
                        turn_probs(m - LAG)
                    done = m - LAG - 1
                    if done >= 0 and done % T == T - 1:
                        values(done // T)

            pe.wait_ge(drained["act"], tiles["sk", 1][3][1])
            pe.wait_ge(drained["dve"], tiles["y", 1][3][1])
            pe.wait_ge(c_rows_in, 32)
            softmax_attention(0, FOX_H, HD + 2, q_aug, k_aug, fv)

            pe.wait_ge(exped, FOX_H * T)
            pe.wait_ge(pt_made, FOX_H * T)
            pe.wait_ge(pv_drained, FOX_H // 2)

            def z_scores(i, kb):
                n = i * T + kb
                if n >= 6:
                    pe.wait_ge(a_made, n - 5)
                r0, j = (i % 2) * HD, i // 2
                out = bank[n % 6]
                mm(out[:, kb * P:S], skT[r0:r0 + HD, j, kb * P:(kb + 1) * P], sqT[r0:r0 + HD, j, kb * P:S],
                   start=True, stop=False, skip_group_check=True)
                mm(out[:, kb * P:(kb + 1) * P], ident_b[:, :], mask_lt[:, :], start=False, stop=True,
                   skip_group_check=True).then_inc(z_full, 1)

            def rest(i):
                for kb in range(T):
                    if kb == 0:
                        pe.wait_ge(sp_made, (i + 1) * T)
                    for jb in range(kb, T):
                        last = mm(bank[(i * T + kb) % 6][:, jb * P:S], (neg_tri if jb == kb else neg_one)[:, :],
                                  sp[i % 2][:, jb, jb * P:S], start=False, stop=(jb == T - 1),
                                  skip_group_check=True)
                    last.then_inc(rest_full, 1)

            def sb_values(i):
                pe.wait_ge(a_made, (i + 1) * T)
                r0 = (i % 2) * HD
                for kb in range(T):
                    last = mm(bank[6 + i // 2][r0:r0 + HD, kb * P:S], sf[:, kb, i * HD:(i + 1) * HD],
                              az[i % 2][:, kb, kb * P:S], start=(kb == 0), stop=(kb == T - 1),
                              skip_group_check=True)
                last.then_inc(sb_full, 1)

            for kb in range(T):
                z_scores(0, kb)
            for i in range(SB_H):
                if i + 1 < SB_H:
                    z_scores(i + 1, 0)
                    z_scores(i + 1, 1)
                rest(i)
                if i + 1 < SB_H:
                    z_scores(i + 1, 2)
                    z_scores(i + 1, 3)
                sb_values(i)

            left_ready(KD)
            pe.wait_ge(a_made, SB_H * T)
            pe.wait_ge(sb_drained, SB_H // 2)
            for g in range(2):
                weights_moving([("out1", g, t) for t in range(T)],
                               [(CH["out1"] + 4 * g + i, ks) for i, ks in pairs], S)

            turn_rows("h2", h_tile, h_made, T)
            left_ready()
            weights_moving([("lq", t) for t in range(T)],
                           [(CH["lq"], (0, 1, 2)), (CH["lq"] + 1, (3, 4, 5)), (CH["lq"] + 2, (6, 7))], LQ_W)
            weights_moving([("lkv", t) for t in range(T)],
                           [(CH["lkv"], (0, 1, 2, 3)), (CH["lkv"] + 1, (4, 5, 6, 7))], RANK)
            for j in range(4):
                for i, name in enumerate(("c", "xv", "b")):
                    weights_still((name, j), CH["conv"] + 3 * j + i)
            pe.wait_ge(lat_scaled, 1)
            for i in range(4):
                bank_free(("latT", i))
                src = lat_q if i < 2 else lat_kv
                for t in range(T):
                    last = turn(tbank(("latT", i))[:, t * P:(t + 1) * P], src[:, t, (i % 2) * P:(i % 2 + 1) * P])
                last.then_inc(tile_full, 1)
            pe.wait_ge(roped, 1)
            bank_free(("krT", 0))
            for t in range(T):
                last = turn(tbank(("krT", 0))[0:ROPE, t * P:(t + 1) * P], lat_q[:, t, RANK:LQ_W])
            last.then_inc(tile_full, 1)
            left_ready(4)
            for k in range(2):
                hi, lo = chunk(CH["uq"] + k)
                for t in range(T):
                    for g in range(2):
                        key = ("uq", t, g)
                        if k == 0:
                            bank_free(key)
                        st = left(k, t)
                        w = UQ_W // 2
                        last = three(tbank(key)[:, 0:w], st[0], st[1], hi[:, g * w:(g + 1) * w],
                                     lo[:, g * w:(g + 1) * w], start=(k == 0), stop=(k == 1))
                        if (t, g) == (T - 1, 1):
                            last.then_inc(w_used, 1)
                        elif k == 1:
                            last.then_inc(tile_full, 1)
            hi, lo = chunk(CH["uk"])
            for i in range(4):
                bank_free(("uk", i))
                for k in range(2):
                    at = slice(k * 512 + i * P, k * 512 + (i + 1) * P)
                    last = three(tbank(("uk", i))[:, :], hi[:, at], lo[:, at], aT_hi[:, 2 + k, :], aT_lo[:, 2 + k, :],
                                 start=(k == 0), stop=(k == 1))
                last.then_inc(w_used if i == 3 else tile_full, 1)
            weights_moving([("uv", t) for t in range(T)], [(CH["uv"], (0, 1))], S, k0=2)
            turn_heads("q2T", MLA_H, QK2, lambda t, i: q2[:, t, i * QK2:(i + 1) * QK2], roped, 2)

            pe.wait_ge(drained["act"], tiles["q2T", MLA_H - 1][3][1])
            softmax_attention(FOX_H * T, MLA_H, QK2, q2T, k2T, v2)
            pe.wait_ge(exped, (FOX_H + MLA_H) * T)
            pe.wait_ge(pt_made, (FOX_H + MLA_H) * T)
            pe.wait_ge(pv_drained, (FOX_H + MLA_H) // 2)
            pe.wait_ge(sqs_made, 1)
            for half in range(2):
                for t in range(T):
                    last = mm(tbank(("ss2", 0))[:, half * T + t:half * T + t + 1],
                              sqs[:, half, t * P:(t + 1) * P], ones[:, :], start=True, stop=True)
            last.then_inc(tile_full, 1)
            left_ready(8)
            for g in range(2):
                for half in range(2):
                    weights_moving([("out2", g, half, t) for t in range(T)],
                                   [(CH["out2"] + 4 * g + 2 * half + i, (2 * i, 2 * i + 1)) for i in range(2)], S,
                                   k0=4 * half)

            turn_rows("h3", h_tile, h_made, 2 * T)
            left_ready()

            def ffn_block(f, c, first):
                for b in range(4):
                    s = (CH["ffn"] + b) % SLOTS
                    pe.wait_ge(w_split, c + b + 1)
                    if not first and b % 2 == 0:
                        pe.wait_ge(ffn_act, f + b // 2 - 1)
                    for k in range(KD):
                        at = slice(k * P, (k + 1) * P)
                        last = three(bank[b][:, :], w_hi[:, s, at], w_lo[:, s, at], aT_hi[:, k, :], aT_lo[:, k, :],
                                     start=(k == 0), stop=(k == KD - 1))
                    last.then_inc(w_used, 1)

            ffn_block(0, CH["ffn"], True)
            with pe.Fori(1, NF // 2) as i:
                ffn_block(i * 2, i * 4 + CH["ffn"], False)

            def down_block(k, slot, first, last_k):
                pe.wait_ge(staged, k + 1)
                pe.wait_ge(w_split, k + CH["down"] + 1)
                s = (CH["down"] + slot) % SLOTS
                for t in range(T):
                    st = aT_hi[:, slot, t * P:(t + 1) * P], aT_lo[:, slot, t * P:(t + 1) * P]
                    for g in range(2):
                        last = three(bank[2 * t + g][:, :], st[0], st[1], w_hi[:, s, g * 512:(g + 1) * 512],
                                     w_lo[:, s, g * 512:(g + 1) * 512], start=first, stop=last_k)
                        if (t, g) == (T - 1, 1):
                            last.then_inc(w_used, 1)
                        elif last_k:
                            last.then_inc(tile_full, 1)

            pe.wait_ge(ffn_act, NF)
            for k in range(4):
                down_block(k, k, k == 0, False)
            with pe.Fori(1, NF // 4) as i:
                for j in range(4):
                    down_block(i * 4 + j, j, False, False)
            for k in range(NF // 4 * 4, NF):
                down_block(k, k % 4, False, k == NF - 1)

            pe.wait_ge(p_split, 2)
            for g in range(2):
                weights_moving([("ple", g, t) for t in range(T)], [(CH["ple"] + g, (0, 1))], S, k0=4)
            turn_rows("xT", lambda t, k: x[:, t, k * P:(k + 1) * P], x_new, 3 * T)
            left_ready()
            for g in range(2):
                weights_moving([("pgate", g, t) for t in range(T)],
                               [(CH["pgate"] + 4 * g + i, ks) for i, ks in pairs], S)

        @block.scalar
        def _(act_):
            A = nc.scalar.activation
            steps, rsq, order, sq = [0], [0], [0], [0]
            junk = PTf[:, 3072:4096]

            def own(ins):
                steps[0] += 1
                ins.then_inc(act_step, 1)
                act_.wait_ge(act_step, steps[0])

            def drain(key, ins):
                order[0] += 1
                assert tiles[key][3] == ("act", order[0]), key
                ins.then_inc(drained["act"], 1)

            def copy(out, in_, scale=1.0):
                return A(out, in_, ACT.Copy, scale=scale)

            def rsqrt(at):
                rsq[0] += 1
                act_.wait_ge(ms_made, rsq[0])
                own(A(stat[:, 2, at], stat[:, 1, at], ACT.Ln))
                A(stat[:, 2, at], stat[:, 2, at], ACT.Exp, scale=-0.5).then_inc(rs_made, 1)

            def squares(in_, at):
                if sq[0]:
                    act_.wait_ge(sq_done, sq[0])
                sq[0] += 1
                A(junk[:, 0:in_.shape[-1]], in_, ACT.Square, accum_out=stat[:, 0, at:at + 1]).then_inc(sq_done, 1)

            def split_hi(out, in_, scale=1.0):
                copy(out, in_, scale).then_inc(mix_hi, 1)

            def norm_rows(name, ready, at0):
                for t in range(T + 1):
                    if t < T:
                        ready(t)
                        squares(x[:, t, :], at0 + t)
                    if t > 0:
                        rsqrt(slice(at0 + t - 1, at0 + t))
                for n in range(2 * T):
                    t, half = n // 2, n % 2
                    full(act_, (name, n))
                    split_hi(aT_hi[:, 4 * half:4 * half + 4, t * P:(t + 1) * P],
                             tbank((name, n))[:, :].rearrange("p (a b) -> p a b", b=P))

            act_.dma_start(cols[:, :], cols_d).then_inc(const_in, 16)
            act_.dma_start(wpool[:, :, :], wpool_d).then_inc(const_in, 16)
            act_.dma_start(pos_i[:, :], pos_d).then_inc(const_in, 16)
            act_.dma_start(g_pre[:, :], gains_d[0, :, :]).then_inc(g_pre_in, 16)
            act_.dma_start(g_post[:, :], gains_d[3, :, :]).then_inc(g_post_in, 16)

            act_.wait_ge(angles, 1)
            A(cs[:, 0, :, :], cs[:, 0, :, :], ACT.Sin).then_inc(sines, 1)
            A(cs[:, 1, :, :], cs[:, 1, :, :], ACT.Sin).then_inc(sines, 1)

            nc.scalar.preload_act_table_set(LOG_EXP)
            norm_rows("h1", lambda t: act_.wait_ge(x_in[t], 16), 0)

            def qk_rows(name, base):
                for t in range(T):
                    if base and t == 0:
                        act_.wait_ge(tile_full, tiles["qT", FOX_H - 1][1][1])
                    full(act_, (name, t))
                    copy(qk_raw[:, t, :], tbank((name, t))[:, :]).then_inc(act_step, 1)
                    steps[0] += 1
                    n = base + t
                    if n >= 2:
                        act_.wait_ge(qk_reduced, n - 1)
                    A(sq_tmp[:, n % 2, :], tbank((name, t))[:, :], ACT.Square).then_inc(qk_squared, 1)
                    act_.wait_ge(qk_squared, n + 1)
                    order[0] += 1
                    nc.scalar.sem_inc(drained["act"], 1)

            def heads_out(name, n, width, dst, scale=None):
                for i in range(n):
                    full(act_, (name, i))
                    drain((name, i), copy(dst[0:width, i, :], tbank((name, i))[0:width, :],
                                          1.0 if scale is None else scale))

            act_.wait_ge(const_in, 48)
            qk_rows("fq", 0)
            rsqrt(slice(16, 48))
            for t in range(T):
                full(act_, ("fv", t))
                drain(("fv", t), copy(fv[:, t, :], tbank(("fv", t))[:, :]))
            heads_out("qT", FOX_H, HD, q_aug, col("gq")[0:HD])
            qk_rows("fk", T)
            rsqrt(slice(16, 48))
            for t in range(T):
                full(act_, ("sf", t))
                drain(("sf", t), copy(sf[:, t, :], tbank(("sf", t))[:, 0:SF_W]))
            heads_out("kT", FOX_H, HD, k_aug, col("gk")[0:HD])
            act_.wait_ge(lf_abs, 1)
            own(A(lf[:, 1, :], lf[:, 1, :], ACT.Exp, scale=-1.0))
            A(lf[:, 1, :], lf[:, 1, :], ACT.Ln, bias=1.0).then_inc(lf_exp, 1)

            def gate_rows(name, n, b0):
                for i in range(n):
                    full(act_, (name, i))
                    drain((name, i), A(gate[:, b0 + i, :], tbank((name, i))[:, :], ACT.Silu))

            gate_rows("pg", 2, 4)
            gate_rows("fg", 4, 0)
            gate_rows("sg", 2, 6)
            for i in range(2):
                full(act_, ("sq", i))
                drain(("sq", i), copy(sqT[:, i, :], tbank(("sq", i))[:, :], HD ** -0.5))
            for i in range(2):
                full(act_, ("sk", i))
                drain(("sk", i), copy(skT[:, i, :], tbank(("sk", i))[:, :]))
            act_.wait_ge(rows_laid, 2)
            act_.wait_ge(cum_made, 1)
            act_.dma_start(q_aug[HD:HD + 1, :, :], cum[:, 0, :]).then_inc(c_rows_in, 16)
            act_.dma_start(k_aug[HD + 1:HD + 2, :, :], cum[:, 1, :]).then_inc(c_rows_in, 16)

            def softmax_attention(base, heads, pair_out):
                steps_ = heads * T
                for m in range(steps_ + 3):
                    if m < steps_:
                        n = base + m
                        kw = (m % T + 1) * P
                        act_.wait_ge(maxed, n + 1)
                        if m >= 4:
                            act_.wait_ge(turned, n - 3)
                        A(P_buf[:, n % 4, 0:kw], bank[n % 3][:, 0:kw], ACT.Exp, bias=negmax[:, n % 8:n % 8 + 1],
                          accum_out=esum[:, n % 8:n % 8 + 1]).then_inc(exped, 1)
                    if m >= 3:
                        n, i, qb = base + m - 3, (m - 3) // T, (m - 3) % T
                        act_.wait_ge(turned, n + 1)
                        if qb == 0 and i >= 2:
                            act_.wait_ge(pv_done, base // T + i - 1)
                        copy(PT[:, i % 2, 0:qb + 1, qb * P:(qb + 1) * P],
                             bank[3 + n % 3][:, 0:(qb + 1) * P].rearrange("p (a b) -> p a b", b=P))\
                            .then_inc(pt_made, 1)
                        if pair_out is not None and qb == 1 and i >= 2 and i % 2 == 0:
                            pair_out(i // 2 - 1)
                if pair_out is not None:
                    pair_out(heads // 2 - 1)

            nc.scalar.preload_act_table_set(LOG_EXP)
            act_.wait_ge(pooled_made, 2)
            act_.wait_ge(tile_full, tiles["y", 1][1][1])
            softmax_attention(0, FOX_H, None)

            act_.wait_ge(pv_done, FOX_H)

            def sb_logs(i):
                for kb in range(T):
                    n = i * T + kb
                    e = ea[i % 2][:, kb, kb * P:S]
                    act_.wait_ge(z_abs, n + 1)
                    own(A(e, e, ACT.Exp))
                    A(e, e, ACT.Ln, bias=1.0).then_inc(z_ln, 1)

            def sb_weights(i):
                for kb in range(T):
                    n = i * T + kb
                    act_.wait_ge(rest_full, n + 1)
                    if kb == 0 and i >= 2:
                        act_.wait_ge(sb_full, i - 1)
                    A(az[i % 2][:, kb, kb * P:S], bank[n % 6][:, kb * P:S], ACT.Exp).then_inc(a_made, 1)

            sb_logs(0)
            for i in range(SB_H):
                sb_weights(i)
                if i + 1 < SB_H:
                    sb_logs(i + 1)
            act_.wait_ge(gated, 1)
            for b in range(KD):
                split_hi(aT_hi[:, b, :], gate[:, b, :])

            act_.wait_ge(h_made, T)
            act_.dma_start(g_pre[:, :], gains_d[1, :, :]).then_inc(g_pre_in, 16)
            norm_rows("h2", lambda t: act_.wait_ge(x_new, T + t + 1), 4)
            for name, dst, w, at0 in (("lq", lat_q, LQ_W, 48), ("lkv", lat_kv, RANK, 52)):
                for t in range(T):
                    full(act_, (name, t))
                    own(copy(dst[:, t, :], tbank((name, t))[:, 0:w]))
                    drain((name, t), A(PTf[:, 3072:3072 + RANK], tbank((name, t))[:, 0:RANK], ACT.Square,
                                       accum_out=stat[:, 0, at0 + t:at0 + t + 1]))
            rsqrt(slice(48, 56))
            for j in range(4):
                full(act_, ("c", j))
                if j >= 2:
                    act_.wait_ge(conv_y, j - 1)
                drain(("c", j), copy(u[:, j % 2, KERNEL - 1:], tbank(("c", j))[:, :]))
                act_.wait_ge(conv_y, j + 1)
                A(sqs[:, 1, :] if j == 0 else sq2[:, j % 2, :], y[:, j, :], ACT.Square).then_inc(sq_y, 1)
            for i in range(4):
                full(act_, ("latT", i))
                split_hi(aT_hi[:, i, :], tbank(("latT", i))[:, :], col("gq2", i) if i < 2 else col("gkv2", i - 2))
            full(act_, ("krT", 0))
            drain(("krT", 0), copy(k2T[HD:QK2, :, :],
                                   tbank(("krT", 0))[0:ROPE, :].unsqueeze(1).broadcast_to([ROPE, MLA_H, S])))
            for t in range(T):
                for g in range(2):
                    full(act_, ("uq", t, g))
                    drain(("uq", t, g), copy(q2[:, t, g * 384:(g + 1) * 384], tbank(("uq", t, g))[:, 0:384],
                                             QK2 ** -0.5))
            for i in range(4):
                full(act_, ("uk", i))
                own(copy(k2T[0:HD, 2 * i, :], tbank(("uk", i))[0:HD, :]))
                drain(("uk", i), copy(k2T[0:HD, 2 * i + 1, :], tbank(("uk", i))[HD:P, :]))
            for t in range(T):
                full(act_, ("uv", t))
                drain(("uv", t), copy(v2[:, t, :], tbank(("uv", t))[:, :]))
            heads_out("q2T", MLA_H, QK2, q2T)
            for j in range(4):
                act_.wait_ge(w_used, CH["uv"] + 1)
                split_hi(aT_hi[:, 4 + j, :], y[:, j, :], col("gc", j))

            def pair_out(pair):
                act_.wait_ge(pv_done, FOX_H + 2 * pair + 2)
                out = bank[6 + pair % 2][:, :]
                split_hi(aT_hi[:, pair, :], out, col("ga", pair))
                A(sqs[:, 0, :] if pair == 0 else sq2[:, pair % 2, :], out, ACT.Square).then_inc(sq_y, 1)

            softmax_attention(FOX_H * T, MLA_H, pair_out)
            rsqrt(slice(56, 64))
            for g in range(2):
                for t in range(T):
                    full(act_, ("out2", g, 0, t))
                    if g == 0 and t == 0:
                        act_.wait_ge(group_rsqrt, 1)
                    drain(("out2", g, 0, t), copy(y2[:, t, g * 512:(g + 1) * 512], tbank(("out2", g, 0, t))[:, :],
                                                  stat[:, 3, 56 + t:57 + t]))
            for t in range(T):
                act_.wait_ge(y2_made, T + t + 1)
                squares(y2[:, t, :], 8 + t)
                if t > 0:
                    rsqrt(slice(7 + t, 8 + t))
            rsqrt(slice(11, 12))

            act_.wait_ge(h_made, 2 * T)
            act_.dma_start(g_pre[:, :], gains_d[2, :, :]).then_inc(g_pre_in, 16)
            norm_rows("h3", lambda t: act_.wait_ge(x_new, 2 * T + t + 1), 12)
            act_.dma_start(g_post[:, :], gains_d[4, :, :]).then_inc(g_post_in, 16)
            act_.dma_start(pe_raw, pt_d).then_inc(pt_in, 16)

            def weights_hi(c, s, used=None):
                act_.wait_ge(raw_in[s % RAW], (c - s % RAW) * (16 // RAW) + 16)
                if used is not None:
                    act_.wait_ge(w_used, used)
                copy(w_hi[:, s, :], raw[:, s % RAW, :]).then_inc(hi_shared, 1)

            def ffn_silu(f, slot, c, first):
                weights_hi(c + 3, (CH["ffn"] + 2 * slot + 3) % SLOTS, used=c)
                act_.wait_ge(w_used, c + 1)
                if not first:
                    act_.wait_ge(ffn_act, f - 1)
                A(sg_t[:, slot, :], bank[2 * slot][:, :], ACT.Silu).then_inc(ffn_gate, 1)
                weights_hi(c + 4, (CH["ffn"] + 2 * slot + 4) % SLOTS)

            for f in range(2):
                ffn_silu(f, f, CH["ffn"] + 2 * f, True)
            with act_.Fori(1, NF // 2) as i:
                for f in range(2):
                    ffn_silu(i * 2 + f, f, i * 4 + (CH["ffn"] + 2 * f), False)

            def stage(k, slot, used):
                act_.wait_ge(w_used, used)
                copy(aT_hi[:, slot, :].unsqueeze(1), act[:, bass.ds(k, 1), :]).then_inc(stage_hi, 1)

            def down_weights(k, slot):
                c = k + (CH["down"] + 3)
                weights_hi(c, (CH["down"] + 3 + slot) % SLOTS, used=c - 3)

            act_.wait_ge(ffn_act, NF)
            for k in range(4):
                stage(k, k, CH["down"])
            act_.wait_ge(pt_in, 16)
            for k in range(2):
                copy(aT_hi[:, 4 + k, :], pe_raw[:, k, :]).then_inc(p_hi, 1)
            for k in range(4):
                down_weights(k, k)
            with act_.Fori(1, NF // 4) as i:
                for j in range(4):
                    stage(i * 4 + j, j, i * 4 + (CH["down"] + j - 3))
                    down_weights(i * 4 + j, j)
            for k in range(NF // 4 * 4, NF):
                stage(k, k % 4, CH["down"] + k - 3)
                down_weights(k, k % 4)

            nc.scalar.preload_act_table_set(LOG_EXP)
            for t in range(T):
                for g in range(2):
                    full(act_, ("down", t, g))
                    squares(tbank(("down", t, g))[:, :], 16 + 2 * t + g)
                if t > 0:
                    rsqrt(slice(24 + t - 1, 24 + t))
            rsqrt(slice(27, 28))
            for g in range(2):
                for t in range(T):
                    full(act_, ("ple", g, t))
                    own(copy(emb[:, t, g * 512:(g + 1) * 512], tbank(("ple", g, t))[:, :]))
                    at = 32 + 4 * g + t
                    drain(("ple", g, t), A(gate_t[:, 0, :], tbank(("ple", g, t))[:, :], ACT.Square,
                                           accum_out=stat[:, 0, at:at + 1]))
            act_.wait_ge(x_new, 4 * T)
            act_.dma_start(g_post[:, :], gains_d[5, :, :]).then_inc(g_post_in, 16)
            for n in range(2 * T):
                t, half = n // 2, n % 2
                full(act_, ("xT", n))
                split_hi(aT_hi[:, 4 * half:4 * half + 4, t * P:(t + 1) * P],
                         tbank(("xT", n))[:, :].rearrange("p (a b) -> p a b", b=P))
            rsqrt(slice(40, 44))
            for g in range(2):
                for t in range(T):
                    n = g * T + t
                    full(act_, ("pgate", g, t))
                    if n >= 2:
                        act_.wait_ge(out_made, n - 1)
                    A(gate_t[:, n % 2, :], tbank(("pgate", g, t))[:, :], ACT.Sigmoid).then_inc(pgate_made, 1)

        @block.vector
        def _(dve):
            V = nc.vector
            steps, rsq, order, lows, sqn, hn, xn = [0], [0], [0], [0], [0], [0], [0]

            def own(ins):
                steps[0] += 1
                ins.then_inc(dve_step, 1)
                dve.wait_ge(dve_step, steps[0])

            def drain(key, ins):
                order[0] += 1
                assert tiles[key][3] == ("dve", order[0]), (key, order[0])
                ins.then_inc(drained["dve"], 1)

            def stt(out, in0, scalar, in1, op0, op1):
                return V.scalar_tensor_tensor(out=out, in0=in0, scalar=scalar, in1=in1, op0=op0, op1=op1)

            def rsqrt(at, width, ss=None):
                rsq[0] += 1
                V.tensor_scalar(stat[:, 1, at], stat[:, 0, at] if ss is None else ss, 1.0 / width, EPS, ALU.mult,
                                ALU.add).then_inc(ms_made, 1)
                dve.wait_ge(rs_made, rsq[0])
                own(V.tensor_tensor(stat[:, 3, at], stat[:, 2, at], stat[:, 2, at], ALU.mult))
                own(stt(stat[:, 3, at], stat[:, 3, at], -0.5, stat[:, 1, at], ALU.mult, ALU.mult))
                own(stt(stat[:, 3, at], stat[:, 3, at], 1.5, stat[:, 2, at], ALU.add, ALU.mult))

            def split_lo(key, out, in_, hi, scale=None):
                lows[0] += 1
                dve.wait_ge(mix_hi, lows[0])
                if scale is None:
                    ins = V.tensor_tensor(out, in_, hi, ALU.subtract)
                else:
                    ins = stt(out, in_, scale, hi, ALU.mult, ALU.subtract)
                ins.then_inc(mix_lo, 1)
                if key is not None:
                    order[0] += 1
                    assert tiles[key][3] == ("dve", order[0]), key
                    dve.wait_ge(mix_lo, lows[0])
                    V.sem_inc(drained["dve"], 1)

            def norm_rows(name, at0, gains):
                dve.wait_ge(g_pre_in, 16 * gains)
                for t in range(T):
                    sqn[0] += 1
                    dve.wait_ge(sq_done, sqn[0])
                    rsqrt(slice(at0 + t, at0 + t + 1), D)
                    if t >= 2:
                        full(dve, (name, 2 * (t - 2) + 1))
                    hn[0] += 1
                    stt(h[:, t % 2, :], x[:, t, :], stat[:, 3, at0 + t:at0 + t + 1], g_pre[:, :], ALU.mult,
                        ALU.mult).then_inc(h_made, 1)
                turned_lo(name)

            def turned_lo(name):
                for n in range(2 * T):
                    t, half = n // 2, n % 2
                    at = (slice(None), slice(4 * half, 4 * half + 4), slice(t * P, (t + 1) * P))
                    split_lo((name, n), aT_lo[at], tbank((name, n))[:, :].rearrange("p (a b) -> p a b", b=P),
                             aT_hi[at].bitcast(F32))

            dve.wait_ge(const_in, 48)
            own(V.tensor_copy(pos_f[:, :], pos_i[:, :]))
            for t in range(T):
                own(V.tensor_scalar(cs[:, 0, t, :], col("invf", 0, HALF), pos_f[:, t:t + 1], None, ALU.mult))
            ang = cs[:, 0, :, :].rearrange("p a b -> p (a b)")
            trn = cs[:, 1, :, :].rearrange("p a b -> p (a b)")
            own(V.tensor_scalar(trn, ang, float(1 / (2 * np.pi)), ROUND, ALU.mult, ALU.add))
            own(V.tensor_scalar(trn, trn, -ROUND, None, ALU.add))
            for part in (PI_A, PI_B, PI_C):
                own(stt(ang, trn, -part, ang, ALU.mult, ALU.add))
            own(V.tensor_scalar(ang, ang, 3.1415925, -3.1415925, ALU.min, ALU.max))
            own(stt(trn, ang, -1.0, ang, ALU.mult, ALU.max))
            V.tensor_scalar(trn, trn, -1.0, float(np.pi / 2), ALU.mult, ALU.add).then_inc(angles, 1)

            norm_rows("h1", 0, 1)
            own(V.tensor_scalar(col("gq"), col("gq"), HD ** -0.5, None, ALU.mult))
            V.memset(q_aug[HD:HD + 2, :, :], 1.0).then_inc(rows_laid, 1)
            V.memset(k_aug[HD:HD + 2, :, :], 1.0).then_inc(rows_laid, 1)

            def qk_norm(base):
                for t in range(T):
                    n = base + t
                    dve.wait_ge(qk_squared, n + 1)
                    V.reduce_sum(stat[:, 0, 16 + 8 * t:24 + 8 * t],
                                 sq_tmp[:, n % 2, :].rearrange("p (a b) -> p a b", b=HD), axis=AX_X)\
                        .then_inc(qk_reduced, 1)
                dve.wait_ge(qk_reduced, base + T)
                rsqrt(slice(16, 48), HD)
                v = qk_raw.rearrange("p a (b c) -> p (a b) c", c=HD)
                V.tensor_tensor(v, v, stat[:, 3, 16:48].unsqueeze(2).broadcast_to([P, T * FOX_H, HD]), ALU.mult)\
                    .then_inc(qk_scaled, 1)

            qk_norm(0)
            qk_norm(T)
            dve.wait_ge(drained["act"], tiles["sf", T - 1][3][1])
            v0 = lf[:, 0, :].rearrange("p (t h) -> p t h", h=FOX_H)
            own(V.tensor_tensor(v0, sf[:, :, SB_H * HD:SF_W],
                                col("bf", 0, FOX_H).unsqueeze(1).broadcast_to([P, T, FOX_H]), ALU.add))
            stt(lf[:, 1, :], lf[:, 0, :], -1.0, lf[:, 0, :], ALU.mult, ALU.max).then_inc(lf_abs, 1)
            dve.wait_ge(lf_exp, 1)
            stt(lf[:, 2, :], lf[:, 0, :], 0.0, lf[:, 1, :], ALU.min, ALU.subtract).then_inc(lf_made, 1)

            for i in range(2):
                full(dve, ("px", i))
                if i:
                    dve.wait_ge(pooled_made, i)
                a, b, c = xp[:, 0, :], xp[:, 1, :], xp[:, 2, :]
                ins = V.tensor_copy(a[:, PAD:], tbank(("px", i))[:, :])
                drain(("px", i), ins)
                dve.wait_ge(drained["dve"], order[0])
                src, dst, reach = a, b, 0
                w = 1
                halves = (WINDOWS[2 * i], WINDOWS[2 * i + 1])
                while w < halves[1]:
                    lo_p = 0 if w < halves[0] else HD
                    at = reach + w
                    own(V.tensor_tensor(dst[lo_p:, at:], src[lo_p:, at:], src[lo_p:, at - w:S + PAD - w], ALU.add))
                    if 2 * w == halves[0]:
                        own(V.tensor_copy(pooled[0:HD, i, :], dst[0:HD, PAD:]))
                    reach = at
                    w *= 2
                    src, dst = dst, (c if dst is b else b)
                own(V.tensor_copy(pooled[HD:, i, :], src[HD:, PAD:]))
                own(V.tensor_tensor(xp[:, 1, 0:PAD], pooled[:, i, 0:PAD], col("rc", i * PAD, PAD), ALU.mult))
                own(stt(pooled[:, i, :], pooled[:, i, :], col("invw", i), a[:, PAD:], ALU.mult, ALU.subtract))
                V.tensor_tensor(pooled[:, i, 0:PAD], xp[:, 1, 0:PAD], a[:, PAD:2 * PAD], ALU.subtract)\
                    .then_inc(pooled_made, 1)
            full(dve, ("lfT", 0))
            one_row = xp[0:FOX_H, 2, 0:S]
            own(V.memset(one_row, 1.0))
            ins = V.tensor_tensor_scan(cum[:, 0, :], one_row, tbank(("lfT", 0))[0:FOX_H, :], 0.0, ALU.mult, ALU.add)
            drain(("lfT", 0), ins)
            dve.wait_ge(drained["dve"], order[0])
            V.tensor_scalar(cum[:, 1, :], cum[:, 0, :], -1.0, None, ALU.mult).then_inc(cum_made, 1)
            dve.wait_ge(drained["act"], tiles["pg", 1][3][1])
            for i in range(2):
                full(dve, ("y", i))
                drain(("y", i), stt(gate[:, 4 + i, :], tbank(("y", i))[:, :], col("ps", i), gate[:, 4 + i, :],
                                    ALU.mult, ALU.mult))

            def softmax_attention(base, heads, pair_out):
                steps_ = heads * T
                for m in range(steps_ + 1):
                    if m < steps_:
                        n = base + m
                        kw = (m % T + 1) * P
                        dve.wait_ge(scored, n + 1)
                        V.tensor_reduce(negmax[:, n % 8:n % 8 + 1], bank[n % 3][:, 0:kw], AX_X, ALU.max, negate=True)\
                            .then_inc(maxed, 1)
                    if m > 0:
                        n = base + m - 1
                        kw = ((m - 1) % T + 1) * P
                        dve.wait_ge(exped, n + 1)
                        own(V.reciprocal(erec[:, n % 8:n % 8 + 1], esum[:, n % 8:n % 8 + 1]))
                        V.tensor_scalar(P_buf[:, n % 4, 0:kw], P_buf[:, n % 4, 0:kw], erec[:, n % 8:n % 8 + 1],
                                        None, ALU.mult).then_inc(normed, 1)
                    if m % (2 * T) == T + 1 and m > 2 * T:
                        pair_out(m // (2 * T) - 1)
                pair_out(heads // 2 - 1)

            def fox_pair(pair):
                dve.wait_ge(pv_done, 2 * pair + 2)
                V.tensor_tensor(gate[:, pair, :], bank[6 + pair % 2][:, :], gate[:, pair, :], ALU.mult)\
                    .then_inc(pv_drained, 1)

            softmax_attention(0, FOX_H, fox_pair)
            dve.wait_ge(pv_drained, FOX_H // 2)

            def sb_abs(i, kbs):
                for kb in kbs:
                    n = i * T + kb
                    dve.wait_ge(z_full, n + 1)
                    if kb == 0 and i >= 2:
                        dve.wait_ge(rest_full, (i - 1) * T)
                    r, z = sp[i % 2][:, kb, kb * P:S], bank[n % 6][:, kb * P:S]
                    own(V.tensor_scalar(r, z, 0.0, None, ALU.max))
                    stt(ea[i % 2][:, kb, kb * P:S], r, -2.0, z, ALU.mult, ALU.add).then_inc(z_abs, 1)

            def sb_softplus(i):
                for kb in range(T):
                    n = i * T + kb
                    dve.wait_ge(z_ln, n + 1)
                    r = sp[i % 2][:, kb, kb * P:S]
                    V.tensor_tensor(r, r, ea[i % 2][:, kb, kb * P:S], ALU.add).then_inc(sp_made, 1)

            def sb_out(pair):
                dve.wait_ge(sb_full, 2 * pair + 2)
                V.tensor_tensor(gate[:, 6 + pair, :], bank[6 + pair][:, :], gate[:, 6 + pair, :], ALU.mult)\
                    .then_inc(sb_drained, 1)

            dve.wait_ge(pv_done, FOX_H)
            sb_abs(0, range(T))
            sb_softplus(0)
            for i in range(1, SB_H):
                sb_abs(i, range(T))
                sb_softplus(i)
                if i % 2 == 0:
                    sb_out(i // 2 - 1)
            sb_out(SB_H // 2 - 1)
            dve.wait_ge(sb_drained, SB_H // 2)
            V.sem_inc(gated, 1)
            for b in range(KD):
                split_lo(None, aT_lo[:, b, :], gate[:, b, :], aT_hi[:, b, :].bitcast(F32))
            for g in range(2):
                for t in range(T):
                    full(dve, ("out1", g, t))
                    at = x[:, t, g * 512:(g + 1) * 512]
                    xn[0] += 1
                    V.tensor_tensor(at, at, tbank(("out1", g, t))[:, :], ALU.add).then_inc(x_new, 1)
                    dve.wait_ge(x_new, xn[0])
                    order[0] += 1
                    V.sem_inc(drained["dve"], 1)

            norm_rows("h2", 4, 2)
            dve.wait_ge(drained["act"], tiles["lkv", T - 1][3][1])
            rsqrt(slice(48, 56), RANK)
            for t in range(T):
                own(V.tensor_scalar(lat_q[:, t, 0:RANK], lat_q[:, t, 0:RANK], stat[:, 3, 48 + t:49 + t], None,
                                    ALU.mult))
                own(V.tensor_scalar(lat_kv[:, t, :], lat_kv[:, t, :], stat[:, 3, 52 + t:53 + t], None, ALU.mult))
            V.sem_inc(lat_scaled, 1)

            def rotate(t1, t2, sn, cn, w):
                own(V.tensor_tensor(w[0], t1, cn, ALU.mult))
                own(V.tensor_tensor(w[1], t2, sn, ALU.mult))
                own(V.tensor_tensor(w[2], t2, cn, ALU.mult))
                own(V.tensor_tensor(w[3], t1, sn, ALU.mult))
                own(V.tensor_tensor(t1, w[0], w[1], ALU.subtract))
                own(V.tensor_tensor(t2, w[2], w[3], ALU.add))

            dve.wait_ge(sines, 2)
            w = [rope_t[:, j, 0:T * HALF].rearrange("p (a b) -> p a b", b=HALF) for j in range(4)]
            rotate(lat_q[:, :, RANK:RANK + HALF], lat_q[:, :, RANK + HALF:LQ_W], cs[:, 0, :, :], cs[:, 1, :, :], w)
            V.sem_inc(roped, 1)

            own(V.memset(u[:, :, 0:KERNEL - 1], 0.0))
            for j in range(4):
                dve.wait_ge(drained["act"], tiles["c", j][3][1])
                full(dve, ("xv", j))
                uj = u[:, j % 2, :]
                ins = V.tensor_tensor(uj[:, KERNEL - 1:], uj[:, KERNEL - 1:], tbank(("xv", j))[:, :], ALU.mult)
                drain(("xv", j), ins)
                dve.wait_ge(drained["dve"], order[0])
                own(V.tensor_scalar(y[:, j, :], uj[:, KERNEL - 1:], col("conv", j * KERNEL), None, ALU.mult))
                for tap in range(1, KERNEL):
                    own(stt(y[:, j, :], uj[:, KERNEL - 1 - tap:KERNEL - 1 - tap + S], col("conv", j * KERNEL + tap),
                            y[:, j, :], ALU.mult, ALU.add))
                full(dve, ("b", j))
                ins = V.tensor_tensor(y[:, j, :], y[:, j, :], tbank(("b", j))[:, :], ALU.mult)
                drain(("b", j), ins)
                dve.wait_ge(drained["dve"], order[0])
                V.sem_inc(conv_y, 1)
                dve.wait_ge(sq_y, j + 1)
                if j > 0:
                    own(V.tensor_tensor(sqs[:, 1, :], sqs[:, 1, :], sq2[:, j % 2, :], ALU.add))
            for i in range(4):
                split_lo(("latT", i), aT_lo[:, i, :], tbank(("latT", i))[:, :], aT_hi[:, i, :].bitcast(F32),
                         col("gq2", i) if i < 2 else col("gkv2", i - 2))
            dve.wait_ge(drained["act"], tiles["uq", T - 1, 1][3][1])
            for t in range(T):
                qt = q2[:, t, :].rearrange("p (h c) -> p h c", c=QK2)
                w = [rope_t[:, j, :].rearrange("p (a b) -> p a b", b=HALF) for j in range(4)]
                sn, cn = (cs[:, j, t, :].unsqueeze(1).broadcast_to([P, MLA_H, HALF]) for j in (0, 1))
                rotate(qt[:, :, HD:HD + HALF], qt[:, :, HD + HALF:], sn, cn, w)
            V.sem_inc(roped, 1)
            for j in range(4):
                split_lo(None, aT_lo[:, 4 + j, :], y[:, j, :], aT_hi[:, 4 + j, :].bitcast(F32), col("gc", j))

            def mla_pair(pair):
                out = bank[6 + pair % 2][:, :]
                dve.wait_ge(sq_y, 4 + pair + 1)
                split_lo(None, aT_lo[:, pair, :], out, aT_hi[:, pair, :].bitcast(F32), col("ga", pair))
                if pair > 0:
                    own(V.tensor_tensor(sqs[:, 0, :], sqs[:, 0, :], sq2[:, pair % 2, :], ALU.add))
                dve.wait_ge(mix_lo, lows[0])
                V.sem_inc(pv_drained, 1)

            softmax_attention(FOX_H * T, MLA_H, mla_pair)
            V.sem_inc(sqs_made, 1)
            full(dve, ("ss2", 0))
            rsqrt(slice(56, 64), 512, ss=tbank(("ss2", 0))[:, 0:2 * T])
            order[0] += 1
            V.sem_inc(drained["dve"], 1)
            V.sem_inc(group_rsqrt, 1)
            ny = 0
            for g in range(2):
                for t in range(T):
                    full(dve, ("out2", g, 1, t))
                    dve.wait_ge(drained["act"], tiles["out2", g, 0, t][3][1])
                    at = y2[:, t, g * 512:(g + 1) * 512]
                    stt(at, tbank(("out2", g, 1, t))[:, :], stat[:, 3, 60 + t:61 + t], at, ALU.mult, ALU.add)\
                        .then_inc(y2_made, 1)
                    ny += 1
                    dve.wait_ge(y2_made, ny)
                    order[0] += 1
                    V.sem_inc(drained["dve"], 1)

            def add_post(t, halves, at):
                for n, (lo_c, hi_c, value) in enumerate(halves):
                    w = post_t[:, t % 2, lo_c:hi_c]
                    own(stt(w, value, stat[:, 3, at:at + 1], g_post[:, lo_c:hi_c], ALU.mult, ALU.mult))
                xn[0] += 1
                V.tensor_tensor(x[:, t, :], x[:, t, :], post_t[:, t % 2, :], ALU.add).then_inc(x_new, 1)

            dve.wait_ge(g_post_in, 16)
            for t in range(T):
                sqn[0] += 1
                dve.wait_ge(sq_done, sqn[0])
                rsqrt(slice(8 + t, 9 + t), D)
                add_post(t, [(0, D, y2[:, t, :])], 8 + t)
            dve.wait_ge(x_new, xn[0])

            norm_rows("h3", 12, 3)

            def ffn_rows(f, slot, c):
                dve.wait_ge(ffn_gate, f + 1)
                dve.wait_ge(w_used, c + 2)
                V.tensor_tensor(act[:, bass.ds(f, 1), :], sg_t[:, slot, :].unsqueeze(1),
                                bank[2 * slot + 1][:, :].unsqueeze(1), ALU.mult).then_inc(ffn_act, 1)

            for f in range(2):
                ffn_rows(f, f, CH["ffn"] + 2 * f)
            with dve.Fori(1, NF // 2) as i:
                for f in range(2):
                    ffn_rows(i * 2 + f, f, i * 4 + (CH["ffn"] + 2 * f))

            def stage(k, slot):
                dve.wait_ge(stage_hi, k + 1)
                V.tensor_tensor(aT_lo[:, slot, :].unsqueeze(1), act[:, bass.ds(k, 1), :],
                                aT_hi[:, slot, :].bitcast(F32).unsqueeze(1), ALU.subtract).then_inc(staged, 1)

            dve.wait_ge(ffn_act, NF)
            for k in range(4):
                stage(k, k)
            for k in range(2):
                dve.wait_ge(p_hi, k + 1)
                V.tensor_tensor(aT_lo[:, 4 + k, :], pe_raw[:, k, :], aT_hi[:, 4 + k, :].bitcast(F32), ALU.subtract)\
                    .then_inc(p_split, 1)
            with dve.Fori(1, NF // 4) as i:
                for j in range(4):
                    stage(i * 4 + j, j)
            for k in range(NF // 4 * 4, NF):
                stage(k, k % 4)

            dve.wait_ge(g_post_in, 32)
            dve.wait_ge(p_split, 2)
            for t in range(T):
                sqn[0] += 2
                dve.wait_ge(sq_done, sqn[0])
                own(V.tensor_tensor(stat[:, 0, 24 + t:25 + t], stat[:, 0, 16 + 2 * t:17 + 2 * t],
                                    stat[:, 0, 17 + 2 * t:18 + 2 * t], ALU.add))
                rsqrt(slice(24 + t, 25 + t), D)
                add_post(t, [(g * 512, (g + 1) * 512, tbank(("down", t, g))[:, :]) for g in range(2)], 24 + t)
                for g in range(2):
                    order[0] += 1
                    V.sem_inc(drained["dve"], 1)

            turned_lo("xT")
            dve.wait_ge(drained["act"], tiles["ple", 1, T - 1][3][1])
            dve.wait_ge(g_post_in, 48)
            own(V.tensor_tensor(stat[:, 0, 40:44], stat[:, 0, 32:36], stat[:, 0, 36:40], ALU.add))
            rsqrt(slice(40, 44), D)
            for t in range(T):
                own(stt(emb[:, t, :], emb[:, t, :], stat[:, 3, 40 + t:41 + t], g_post[:, :], ALU.mult, ALU.mult))
            for g in range(2):
                for t in range(T):
                    n = g * T + t
                    dve.wait_ge(pgate_made, n + 1)
                    s = gate_t[:, n % 2, :]
                    own(V.tensor_tensor(s, s, emb[:, t, g * 512:(g + 1) * 512], ALU.mult))
                    at = x[:, t, g * 512:(g + 1) * 512]
                    V.tensor_tensor(at, at, s, ALU.add).then_inc(out_made, 1)


def cut_moving(w, ks, at=slice(None)):
    c = np.concatenate([w[k * P:(k + 1) * P, at] for k in ks], axis=1)
    return np.pad(c, ((0, 0), (0, CW - c.shape[1])))


def cut_still(w, at):
    return w[:, at].reshape(KD, P, P).transpose(1, 0, 2).reshape(P, CW)


def lay_out_weights(w_in, w_out, w_in2, w_uq, w_ukv, w_out2, w_gate, w_up, w_down, w_ple, w_pgate):
    c = []
    pairs = [(0, 1), (2, 3), (4, 5), (6, 7)]
    threes = [(0, 1, 2), (3, 4, 5), (6, 7)]
    fq, fk, fv, fg, ff, px, pg, sq, sk, sv, sg = (
        0, 512, 1024, 1536, 2048, 2056, 2312, 2568, 2824, 3080, 3336)

    def moving(w, at, groups):
        c.extend(cut_moving(w, ks, at) for ks in groups)

    def still(w, at, n):
        c.extend(cut_still(w, slice(at + i * P, at + (i + 1) * P)) for i in range(n))

    for at in (fq, fv, fk):
        moving(w_in, slice(at, at + S), pairs)
    moving(np.concatenate([w_in[:, sv:sv + SB_H * HD], w_in[:, ff:ff + FOX_H]], axis=1), slice(None), threes)
    for at, n in ((pg, 2), (px, 2), (fg, 4), (sg, 2), (sq, 2), (sk, 2)):
        still(w_in, at, n)
    for g in range(2):
        moving(w_out, slice(g * 512, (g + 1) * 512), pairs)
    kr, cb, cc, cx = 2 * RANK, 2 * RANK + ROPE, 2 * RANK + ROPE + 512, 2 * RANK + ROPE + 1024
    moving(np.concatenate([w_in2[:, :RANK], w_in2[:, kr:kr + ROPE]], axis=1), slice(None), threes)
    moving(w_in2, slice(RANK, 2 * RANK), [(0, 1, 2, 3), (4, 5, 6, 7)])
    for j in range(4):
        for at in (cc, cx, cb):
            still(w_in2, at + j * P, 1)
    moving(w_uq, slice(None), [(0,), (1,)])
    by_head = w_ukv.reshape(RANK, MLA_H, 2, HD)
    for part in range(2):
        moving(by_head[:, :, part, :].reshape(RANK, 512), slice(None), [(0, 1)])
    for g in range(2):
        moving(w_out2, slice(g * 512, (g + 1) * 512), pairs)
    for f in range(NF):
        still(w_gate, f * P, 1)
        still(w_up, f * P, 1)
    moving(w_down, slice(None), [(k,) for k in range(NF)])
    for g in range(2):
        moving(w_ple, slice(g * 512, (g + 1) * 512), [(0, 1)])
    for g in range(2):
        moving(w_pgate, slice(g * 512, (g + 1) * 512), pairs)
    return np.ascontiguousarray(np.stack(c))


def by_partition(v):
    return v.reshape(-1, P).T


def kernel(**inputs):
    import concourse.bacc as _bacc
    from concourse.bass_utils import run_bass_kernel_spmd as _run

    a = {k: np.asarray(v) for k, v in inputs.items()}
    w = lay_out_weights(a["w_in"][0], a["w_out"][0], a["w_in_2"][0], a["w_uq_2"][0], a["w_ukv_2"][0], a["w_out_2"][0],
                        a["w_gate_2"][0], a["w_up_2"][0], a["w_down_2"][0], a["w_ple_proj_2"][0], a["w_ple_gate_2"][0])
    f32 = np.float32
    halves = np.repeat(np.array(WINDOWS, f32).reshape(2, 2), HD, axis=1)
    rc = 1 / np.minimum(np.arange(1, PAD + 1, dtype=f32)[None, None, :], halves[:, :, None])
    invf = (1.0 / (f32(10000.0) ** (np.arange(HALF, dtype=f32) / f32(HALF)))).astype(f32)
    cols = np.concatenate([
        np.tile(a["q_norm_g"][0], 2)[:, None], np.tile(a["k_norm_g"][0], 2)[:, None],
        by_partition(a["q_norm_2"][0]), by_partition(a["kv_norm_2"][0]),
        a["conv_w_2"][0].reshape(KERNEL, 4, P).transpose(2, 1, 0).reshape(P, 4 * KERNEL),
        by_partition(a["attn_group_norm_2"][0]), by_partition(a["conv_group_norm_2"][0]),
        by_partition(a["pool_scale"][0]),
        np.broadcast_to(a["b_f"][0][None, :], (P, FOX_H)), np.broadcast_to(invf[None, :], (P, HALF)),
        rc.transpose(1, 0, 2).reshape(P, 2 * PAD).astype(f32), (1 / halves).T.astype(f32),
    ], axis=1)
    pos = a["positions_2"].reshape(T, P).T
    wpool = np.zeros((P, 2, P), f32)
    for g in range(4):
        r = slice((g % 2) * HD, (g % 2 + 1) * HD)
        wpool[r, g // 2, r] = a["w_pool"][0, g]
    pt = a["p_2"][0, 0].T.reshape(2, P, S).transpose(1, 0, 2)
    gains = np.stack([np.broadcast_to(a[n][0][None, :], (P, D)) for n in (
        "norm_g", "mix_pre_norm_2", "ffn_pre_norm_2", "mix_post_norm_2", "ffn_post_norm_2", "ple_norm_2")])
    arrays = {"x": a["x"].reshape(S, D), "weights": w, "cols": cols, "pos": pos, "wpool": wpool, "pt": pt,
              "gains": gains}
    arrays = {k: np.ascontiguousarray(v) for k, v in arrays.items()}
    nc = _bacc.Bacc("TRN2", target_bir_lowering=False, num_devices=1)
    args = [nc.dram_tensor("in_" + k, v.shape, mybir.dt.from_np(v.dtype), kind="ExternalInput").ap() for k, v in arrays.items()]
    out = nc.dram_tensor("y_out", (S, D), F32, kind="ExternalOutput").ap()
    hybrid_kernel(nc, *args, out)
    r = _run(nc, [{"in_" + k: v for k, v in arrays.items()}], core_ids=[0])
    return r.results[0]["y_out"].reshape(1, S, D)
```

```python
from contextlib import ExitStack

import numpy as np

import concourse.bass as bass
from concourse import mybir

P = 128
F32 = mybir.dt.float32
F32R = mybir.dt.float32r
BF16 = mybir.dt.bfloat16
I32 = mybir.dt.int32
ALU = mybir.AluOpType
ACT = mybir.ActivationFunctionType
AX_X = mybir.AxisListType.X

LOG_EXP = "natural_log_exp_and_others"

S, D = 512, 1024
T = S // P
KD = D // P
HD = 64
FOX_H, SB_H, MLA_H = 8, 4, 8
ROPE, HALF = 32, 16
QK2 = HD + ROPE
RANK = 256
SF_W = SB_H * HD + FOX_H
LQ_W = RANK + ROPE
UQ_W = MLA_H * QK2
FF = 2816
NF = FF // P
EPS = 1e-6
NEG = -1e30
PAD = 16
WINDOWS = (2, 4, 8, 16)
KERNEL = 3

CW = 1024
SLOTS = 4
RAW = 2
SPARE = 5

CHUNKS = (("fq", 4), ("fv", 4), ("fk", 4), ("sf", 3), ("pg", 2), ("px", 2), ("fg", 4), ("sg", 2), ("sq", 2),
          ("sk", 2), ("out1", 8), ("lq", 3), ("lkv", 2), ("conv", 12), ("uq", 2), ("uk", 1), ("uv", 1),
          ("out2c", 4), ("out2a", 4), ("ple", 2), ("ffn", 2 * NF), ("down", NF), ("pgate", 8))
CH, NCH = {}, 0
for _name, _n in CHUNKS:
    CH[_name] = NCH
    NCH += _n

SHARED = CH["ffn"] + 3

COLS, NCOL = {}, 0
for _name, _n in (("gq", 1), ("gk", 1), ("gq2", 2), ("gkv2", 2), ("conv", 4 * KERNEL), ("ga", 4), ("gc", 4), ("ps", 2),
                  ("bf", FOX_H), ("invf", HALF), ("rc", 2 * PAD), ("invw", 2)):
    COLS[_name] = NCOL
    NCOL += _n

PI_A = 6.28125
PI_B = float(np.round((2 * np.pi - PI_A) * 2.0**21) / 2.0**21)
PI_C = float(np.float32(2 * np.pi - PI_A - PI_B))
ROUND = 1.5 * 2.0**23


def psum_tiles():
    tiles = {}
    for n in range(2 * T):
        tiles["h1", n] = (n, "dve", None)

    def group(name, banks, drainer, width_chunks, n=T):
        for t in range(n):
            tiles[name, t] = (banks[t % len(banks)], drainer, CH[width_chunks[0]] + width_chunks[1] if t == n - 1 else None)

    group("fq", (0, 1, 2, 3), "act", ("fq", 3))
    group("fv", (4, 5, 6, 7), "act", ("fv", 3))
    for i in range(FOX_H):
        tiles["qT", i] = (i, "act", None)
    group("fk", (0, 1, 2, 3), "act", ("fk", 3))
    group("sf", (4, 5, 6, 7), "act", ("sf", 2))
    n = 0
    for name in ("pg", "kT", "lfT", "px", "fg", "y", "sg"):
        for i in range({"kT": FOX_H, "lfT": 1, "fg": 4}.get(name, 2)):
            tiles[name, i] = (n % 8, "dve" if name in ("px", "lfT", "y") else "act",
                              None if name in ("lfT", "y", "kT") else CH[name] + i)
            n += 1
    for name in ("sq", "sk"):
        for i in range(2):
            tiles[name, i] = (SPARE, "act", CH[name] + i)
    for g in range(2):
        for t in range(T):
            tiles["out1", g, t] = (4 * g + t, "dve", CH["out1"] + 4 * g + 3 if t == T - 1 else None)
    for n in range(2 * T):
        tiles["h2", n] = (n, "dve", None)
    group("lq", (0, 1, 2, 3), "act", ("lq", 2))
    group("lkv", (4, 5, 6, 7), "act", ("lkv", 1))
    n = 0
    for j in range(4):
        for i, name in enumerate(("c", "xv", "b")):
            tiles[name, j] = (n % 8, "act" if name == "c" else "dve", CH["conv"] + 3 * j + i)
            n += 1
    for i in range(4):
        tiles["latT", i] = (4 + i, "dve", None)
    tiles["krT", 0] = (0, "act", None)
    for t in range(T):
        for g in range(2):
            tiles["uq", t, g] = (2 * t + g, "act", CH["uq"] + 1 if (t, g) == (T - 1, 1) else None)
    for i in range(4):
        tiles["uk", i] = (i, "act", CH["uk"] if i == 3 else None)
    group("uv", (4, 5, 6, 7), "act", ("uv", 0))
    for i in range(MLA_H):
        tiles["q2T", i] = (i, "act", None)
    tiles["ssc", 0] = (0, "dve", None)
    for g in range(2):
        for t in range(T):
            tiles["out2c", g, t] = (SPARE, "act", CH["out2c"] + 2 * g + 1 if t == T - 1 else None)
    for t in range(T):
        for g in range(2):
            tiles["out2a", t, g] = (2 * t + g, "dve", CH["out2a"] + 2 * g + 1 if t == T - 1 else None)
        if t == 0:
            tiles["ssa", 0] = (7, "dve", None)
    for g in range(2):
        for t in range(T):
            tiles["ple", g, t] = (4 * g + t, "act", CH["ple"] + g if t == T - 1 else None)
    for n in range(2 * T):
        tiles["h3", n] = (n, "dve", None)
    for t in range(T):
        for g in range(2):
            tiles["down", t, g] = (2 * t + g, "dve" if t < T - 1 else "dve_last",
                                   CH["down"] + NF - 1 if (t, g) == (T - 1, 1) else None)
        if t == T - 2:
            for n in range(2):
                tiles["xT", n] = (n, "dve", None)
    for n in range(2, 2 * T):
        tiles["xT", n] = (n, "dve", None)
    for t in range(T - 1):
        tiles["pgate", 0, t] = (t, "act", None)
    tiles["pgate", 0, T - 1] = (T - 1, "act", CH["pgate"] + 3)
    for t in range(T):
        tiles["pgate", 1, t] = (4 + t, "act", CH["pgate"] + 7 if t == T - 1 else None)
    return tiles


def tile_counts(tiles):
    full, drained, before, out = 0, {"act": 0, "dve": 0, "dve_last": 0}, {}, {}
    for key, (bank, drainer, chunk) in tiles.items():
        if chunk is None:
            full += 1
        drained[drainer] += 1
        own = (drainer, drained[drainer])
        out[key] = (bank, ("tile", full) if chunk is None else ("chunk", chunk + 1), before.get(bank), own)
        before[bank] = own
    return out


def hybrid_kernel(nc, x_d, w_d, cols_d, pos_d, wpool_d, pt_d, gains_d, out_d):
    tiles = tile_counts(psum_tiles())
    with ExitStack() as ctx:
        def sb(name, shape, dt=F32):
            return ctx.enter_context(nc.sbuf_tensor(name, shape, dt))

        def sem(name):
            return ctx.enter_context(nc.semaphore(name))

        x = sb("x", [P, T, D])
        h = sb("h", [P, 2, D])
        aT_hi = sb("aT_hi", [P, KD, S], F32R)
        aT_lo = sb("aT_lo", [P, KD, S], F32R)
        raw = sb("raw", [P, RAW, CW])
        w_hi = sb("w_hi", [P, SLOTS, CW], F32R)
        w_lo = sb("w_lo", [P, SLOTS, CW], F32R)
        g_pre = sb("g_pre", [P, D])
        g_post = sb("g_post", [P, D])
        PT = sb("PT", [P, 2, T, S])
        arena = sb("arena", [P, 19488])
        ident = sb("ident", [P, P])
        ident_b = sb("ident_b", [P, P], BF16)
        mask_le = sb("mask_le", [P, P], BF16)
        mask_lt = sb("mask_lt", [P, P], BF16)
        neg_tri = sb("neg_tri", [P, P])
        neg_one = sb("neg_one", [P, P])
        ones = sb("ones", [P, 1])
        cols = sb("cols", [P, NCOL])
        wpool = sb("wpool", [P, 2, P])
        pos_i = sb("pos_i", [P, T], I32)
        pos_f = sb("pos_f", [P, T])
        cs = sb("cs", [P, 2, T, HALF])
        stat = sb("stat", [P, 4, 64])
        negmax = sb("negmax", [P, 8])
        esum = sb("esum", [P, 8])
        erec = sb("erec", [P, 8])
        bank = [ctx.enter_context(nc.psum_tensor(f"bank{i}", [P, 512], F32)) for i in range(8)]

        P_buf = h[:, :, :].rearrange("p a (b c) -> p (a b) c", c=S)
        PTf = PT[:, :, :, :].rearrange("p a b c -> p (a b c)")

        def view(base, at, *shape):
            v = base[:, at:at + int(np.prod(shape))]
            if len(shape) == 2:
                v = v.rearrange("p (a b) -> p a b", b=shape[1])
            elif len(shape) == 3:
                v = v.rearrange("p (a b c) -> p a b c", b=shape[1], c=shape[2])
            return v

        def ar(at, *shape):
            return view(arena, at, *shape)

        def col(name, i=0, n=1):
            return cols[:, COLS[name] + i:COLS[name] + i + n]

        qk_raw = ar(0, T, S)
        fv = ar(2048, T, S)
        sf = ar(4096, T, SF_W)
        gate = ar(5152, KD, S)
        sqT = ar(9248, 2, S)
        skT = ar(10272, 2, S)
        q_aug = ar(11296, FOX_H, S)
        k_aug = ar(15392, FOX_H, S)
        sq_tmp = view(PTf, 0, 2, S)
        xp = view(PTf, 1024, 3, S + PAD)
        pooled = view(PTf, 2608, 2, S)
        lf = view(PTf, 3632, 3, T * FOX_H)
        cum = ar(0, 2, S)[0:FOX_H]
        sp = [PT[:, 0, :, :], ar(11296, T, S)]
        az = [PT[:, 1, :, :], ar(13344, T, S)]
        ea = [ar(15392, T, S), ar(17440, T, S)]
        y = ar(0, 4, S)
        u = ar(2048, 2, S + KERNEL - 1)
        sqs = ar(3076, 2, S)
        sq2 = ar(4100, 2, S)
        q2 = ar(5124, T, UQ_W)
        q2T = ar(8196, MLA_H, S)
        k2T = ar(12292, MLA_H, S)
        v2 = ar(16388, T, S)
        lat_q = ar(16388, T, LQ_W)
        lat_kv = ar(5124, T, RANK)
        rope_t = view(PTf, 0, 4, MLA_H * HALF)
        y2 = [ar(5124 + t * D, D) for t in range(T - 1)] + [ar(18436, D)]
        act = ar(0, NF, S)
        sg_t = ar(11264, 2, S)
        emb = ar(12288, T, D)
        pe_raw = view(PTf, 0, 2, S)
        post_t = view(PTf, 1024, 2, D)
        gate_t = view(PTf, 3072, 2, S)

        x_in = [sem(f"x_in{t}") for t in range(T)]
        raw_in = [sem(f"raw_in{i}") for i in range(RAW)]
        const_in = sem("const_in")
        g_pre_in, g_post_in = sem("g_pre_in"), sem("g_post_in")
        pt_in = sem("pt_in")
        rows_laid, c_rows_in = sem("rows_laid"), sem("c_rows_in")
        out_stored = sem("out_stored")
        masks_made = sem("masks_made")
        hi_made, hi_shared, w_split, w_used = sem("hi_made"), sem("hi_shared"), sem("w_split"), sem("w_used")
        tile_full = sem("tile_full")
        drained = {"act": sem("drained_act"), "dve": sem("drained_dve"), "dve_last": sem("drained_dve_last")}
        sq_done = sem("sq_done")
        ms_made = sem("ms_made")
        rs_made = sem("rs_made")
        h_made, h_hi = sem("h_made"), sem("h_hi")
        act_step, dve_step = sem("act_step"), sem("dve_step")
        qk_squared, qk_reduced, qk_scaled = sem("qk_squared"), sem("qk_reduced"), sem("qk_scaled")
        gated = sem("gated")
        lf_abs, lf_exp, lf_made, cum_made = sem("lf_abs"), sem("lf_exp"), sem("lf_made"), sem("cum_made")
        pooled_made = sem("pooled_made")
        sines = sem("sines")
        angles = sem("angles")
        scored, maxed, exped, normed = sem("scored"), sem("maxed"), sem("exped"), sem("normed")
        turned, pt_made, pv_done, pv_drained = sem("turned"), sem("pt_made"), sem("pv_done"), sem("pv_drained")
        z_full, z_abs, z_exp, z_ln, sp_made = sem("z_full"), sem("z_abs"), sem("z_exp"), sem("z_ln"), sem("sp_made")
        rest_full, a_made, sb_full, sb_drained = sem("rest_full"), sem("a_made"), sem("sb_full"), sem("sb_drained")
        mix_hi, mix_lo = sem("mix_hi"), sem("mix_lo")
        x_new = sem("x_new")
        lat_scaled, roped, conv_c, conv_y, sq_y = (sem("lat_scaled"), sem("roped"), sem("conv_c"), sem("conv_y"),
                                                   sem("sq_y"))
        sqs_made = sem("sqs_made")
        group_rsqrt, y2_made = sem("group_rsqrt"), sem("y2_made")
        ffn_gate, ffn_act = sem("ffn_gate"), sem("ffn_act")
        stage_hi, staged = sem("stage_hi"), sem("staged")
        p_hi, p_split, emb_made = sem("p_hi"), sem("p_split"), sem("emb_made")
        pgate_made, out_made = sem("pgate_made"), sem("out_made")

        def full(eng, key):
            kind, n = tiles[key][1]
            eng.wait_ge(tile_full if kind == "tile" else w_used, n)

        def tbank(key):
            return bank[tiles[key][0]]

        block = ctx.enter_context(nc.Block())

        @block.sync
        def _(sp_):
            for t in range(T):
                sp_.dma_start(x[:, t, :], x_d[t * P:(t + 1) * P, :]).then_inc(x_in[t], 16)

            def load(c, first, r):
                if not first:
                    sp_.wait_ge(w_split, c - RAW + 1)
                src = w_d[bass.ds(c, 1), :, :].rearrange("a p c -> p (a c)")
                sp_.dma_start(raw[:, r, :], src).then_inc(raw_in[r], 16)

            for r in range(RAW):
                load(r, True, r)
            with sp_.Fori(1, NCH // RAW) as i:
                for r in range(RAW):
                    load(i * RAW + r, False, r)
            for n in range(2 * T):
                g, t = n // T, n % T
                sp_.wait_ge(out_made, n + 1)
                sp_.dma_start(out_d[t * P:(t + 1) * P, g * 512:(g + 1) * 512],
                              x[:, t, g * 512:(g + 1) * 512]).then_inc(out_stored, 16)
            sp_.wait_ge(out_stored, 2 * T * 16)

        @block.gpsimd
        def _(pool):
            nc.gpsimd.memset(ident[:, :], 0.0).then_inc(masks_made, 1)
            nc.gpsimd.memset(ident_b[:, :], 0.0).then_inc(masks_made, 1)
            nc.gpsimd.memset(mask_le[:, :], 0.0).then_inc(masks_made, 1)
            nc.gpsimd.memset(mask_lt[:, :], 0.0).then_inc(masks_made, 1)
            nc.gpsimd.memset(neg_tri[:, :], -1.0).then_inc(masks_made, 1)
            nc.gpsimd.memset(neg_one[:, :], -1.0).then_inc(masks_made, 1)
            nc.gpsimd.memset(ones[:, :], 1.0).then_inc(masks_made, 1)
            nc.gpsimd.memset(xp, 0.0).then_inc(masks_made, 1)
            pool.wait_ge(masks_made, 8)
            for m in (ident, ident_b):
                nc.gpsimd.affine_select(out=m[:, :], in_=m[:, :], compare_op=ALU.not_equal, fill=1.0, base=0,
                                        pattern=[[-1, P]], channel_multiplier=1).then_inc(masks_made, 1)
            nc.gpsimd.affine_select(out=mask_le[:, :], in_=mask_le[:, :], compare_op=ALU.is_ge, fill=NEG, base=0,
                                    pattern=[[-1, P]], channel_multiplier=1).then_inc(masks_made, 1)
            nc.gpsimd.affine_select(out=mask_lt[:, :], in_=mask_lt[:, :], compare_op=ALU.is_gt, fill=NEG, base=0,
                                    pattern=[[1, P]], channel_multiplier=-1).then_inc(masks_made, 1)
            nc.gpsimd.affine_select(out=neg_tri[:, :], in_=neg_tri[:, :], compare_op=ALU.is_ge, fill=0.0, base=0,
                                    pattern=[[-1, P]], channel_multiplier=1).then_inc(masks_made, 1)

            def split(c, s, shared, first=False):
                r = s % RAW
                if not shared:
                    pool.wait_ge(raw_in[r], (c - r) * (16 // RAW) + 16)
                    if not first:
                        pool.wait_ge(w_used, c - SLOTS + 1)
                    nc.gpsimd.tensor_tensor(w_hi[:, s, :], raw[:, r, :], ones[:, :].broadcast_to([P, CW]),
                                            ALU.mult).then_inc(hi_made, 1)
                    pool.wait_ge(hi_made, c + 1)
                else:
                    pool.wait_ge(hi_shared, c + (1 - SHARED))
                nc.gpsimd.tensor_tensor(w_lo[:, s, :], raw[:, r, :], w_hi[:, s, :].bitcast(F32),
                                        ALU.subtract).then_inc(w_split, 1)

            def splits(a, b, shared):
                while a % SLOTS or a < SLOTS:
                    split(a, a % SLOTS, shared, first=(a < SLOTS))
                    a += 1
                with pool.Fori(a // SLOTS, b // SLOTS) as i:
                    for s in range(SLOTS):
                        split(i * SLOTS + s, s, shared)
                for c in range(b // SLOTS * SLOTS, b):
                    split(c, c % SLOTS, shared)

            splits(0, SHARED, False)
            splits(SHARED, NCH, True)

        @block.tensor
        def _(pe):
            mm = nc.tensor.matmul

            def bank_free(key):
                before = tiles[key][2]
                if before is not None:
                    pe.wait_ge(drained[before[0]], before[1])

            def chunk(c):
                pe.wait_ge(w_split, c + 1)
                return w_hi[:, c % SLOTS, :], w_lo[:, c % SLOTS, :]

            def three(out, st_hi, st_lo, mv_hi, mv_lo, start, stop):
                mm(out, st_hi, mv_hi, start=start, stop=False)
                mm(out, st_hi, mv_lo, start=False, stop=False)
                return mm(out, st_lo, mv_hi, start=False, stop=stop)

            def left(k, t):
                return aT_hi[:, k, t * P:(t + 1) * P], aT_lo[:, k, t * P:(t + 1) * P]

            def weights_moving(keys, chunks, width, k0=0, rows=0, ready=None, late=None):
                def step(n, t, parts):
                    c, ks = chunks[n]
                    hi, lo = parts
                    if n == 0:
                        bank_free(keys[t])
                        if ready:
                            ready(t)
                    for kk, k in enumerate(ks):
                        at = slice(kk * width, (kk + 1) * width)
                        st = left(k0 + k, t)
                        end = n == len(chunks) - 1 and kk == len(ks) - 1
                        last = three(tbank(keys[t])[:, 0:width], st[0], st[1], hi[:, at], lo[:, at],
                                     start=(n == 0 and kk == 0), stop=end)
                    if t == T - 1:
                        last.then_inc(w_used, 1)
                    elif n == len(chunks) - 1:
                        last.then_inc(tile_full, 1)

                whole = len(chunks) - rows
                together = T - 1 if late else T
                for n in range(whole):
                    parts = chunk(chunks[n][0])
                    if late and n == whole - 1:
                        late()
                    for t in range(together):
                        step(n, t, parts)
                if late:
                    for n in range(whole):
                        step(n, T - 1, chunk(chunks[n][0]))
                for t in range(T if rows else 0):
                    for n in range(whole, len(chunks)):
                        step(n, t, chunk(chunks[n][0]))

            def weights_still(key, c):
                hi, lo = chunk(c)
                bank_free(key)
                for k in range(KD):
                    last = three(tbank(key)[:, :], hi[:, k * P:(k + 1) * P], lo[:, k * P:(k + 1) * P],
                                 aT_hi[:, k, :], aT_lo[:, k, :], start=(k == 0), stop=(k == KD - 1))
                last.then_inc(w_used, 1)

            def turn(out, in_):
                return nc.tensor.transpose(out, in_, ident[:, :])

            def turn_rows(name, src, ready, base, tiles_of=range(T)):
                for n in range(2 * tiles_of[0], 2 * tiles_of[-1] + 2):
                    t, half = n // 2, n % 2
                    if half == 0:
                        pe.wait_ge(ready, base + t + 1)
                    bank_free((name, n))
                    for b in range(4):
                        last = turn(tbank((name, n))[:, b * P:(b + 1) * P], src(t, 4 * half + b))
                    last.then_inc(tile_full, 1)

            def h_tile(t, k):
                return h[:, t % 2, k * P:(k + 1) * P]

            split_tiles = [0]

            def left_row():
                base = split_tiles[0]
                split_tiles[0] += 2 * T
                return lambda t: pe.wait_ge(mix_lo, base + 2 * (t + 1))

            def left_ready(n=2 * T):
                split_tiles[0] += n
                pe.wait_ge(mix_lo, split_tiles[0])

            pairs = [(0, (0, 1)), (1, (2, 3)), (2, (4, 5)), (3, (6, 7))]

            def group4(name):
                return [(CH[name] + i, ks) for i, ks in pairs]

            pe.wait_ge(masks_made, 13)
            turn_rows("h1", h_tile, h_made, 0)
            left_ready()
            weights_moving([("fq", t) for t in range(T)], group4("fq"), S)
            weights_moving([("fv", t) for t in range(T)], group4("fv"), S)

            def turn_heads(name, n, width, src, ready, count):
                pe.wait_ge(ready, count)
                for i in range(n):
                    bank_free((name, i))
                    for t in range(T):
                        last = turn(tbank((name, i))[0:width, t * P:(t + 1) * P], src(t, i))
                    last.then_inc(tile_full, 1)

            turn_heads("qT", FOX_H, HD, lambda t, i: qk_raw[:, t, i * HD:(i + 1) * HD], qk_scaled, 1)
            weights_moving([("fk", t) for t in range(T)], group4("fk"), S)
            weights_moving([("sf", t) for t in range(T)],
                           [(CH["sf"], (0, 1, 2)), (CH["sf"] + 1, (3, 4, 5)), (CH["sf"] + 2, (6, 7))], SF_W)
            for i in range(2):
                weights_still(("pg", i), CH["pg"] + i)
            turn_heads("kT", FOX_H, HD, lambda t, i: qk_raw[:, t, i * HD:(i + 1) * HD], qk_scaled, 2)
            pe.wait_ge(lf_made, 1)
            bank_free(("lfT", 0))
            for t in range(T):
                last = turn(tbank(("lfT", 0))[0:FOX_H, t * P:(t + 1) * P], lf[:, 2, t * FOX_H:(t + 1) * FOX_H])
            last.then_inc(tile_full, 1)
            for name, n in (("px", 2), ("fg", 4)):
                for i in range(n):
                    weights_still((name, i), CH[name] + i)
            for i in range(2):
                pe.wait_ge(pooled_made, i + 1)
                bank_free(("y", i))
                mm(tbank(("y", i))[:, :], wpool[:, i, :], pooled[:, i, :], start=True, stop=True).then_inc(tile_full, 1)
            for i in range(2):
                weights_still(("sg", i), CH["sg"] + i)

            LAG = 3

            def softmax_attention(base, heads, width, qT_, kT_, v_, beside):
                steps = heads * T

                def scores(m):
                    i, qb = m // T, m % T
                    n = base + m
                    if m >= 3:
                        pe.wait_ge(exped, n - 2)
                    out = bank[n % 3]
                    kw = (qb + 1) * P
                    mm(out[:, 0:kw], qT_[0:width, i, qb * P:(qb + 1) * P], kT_[0:width, i, 0:kw], start=True,
                       stop=False)
                    mm(out[:, qb * P:kw], ident_b[:, :], mask_le[:, :], start=False, stop=True).then_inc(scored, 1)

                def turn_probs(m):
                    qb = m % T
                    n = base + m
                    pe.wait_ge(normed, n + 1)
                    if m >= 2:
                        pe.wait_ge(pt_made, n - 1)
                    for kb in range(qb + 1):
                        last = turn(bank[3 + n % 2][:, kb * P:(kb + 1) * P], P_buf[:, n % 4, kb * P:(kb + 1) * P])
                    last.then_inc(turned, 1)

                def values(i):
                    pe.wait_ge(pt_made, base + (i + 1) * T)
                    pair = (base // T + i) // 2
                    if i % 2 == 0 and i >= 4:
                        pe.wait_ge(pv_drained, pair - 1)
                    r0 = (i % 2) * HD
                    for kb in range(T):
                        last = mm(bank[6 + pair % 2][r0:r0 + HD, kb * P:S], v_[:, kb, i * HD:(i + 1) * HD],
                                  PT[:, i % 2, kb, kb * P:S], start=(kb == 0), stop=(kb == T - 1),
                                  skip_group_check=True)
                    last.then_inc(pv_done, 1)

                for m in range(steps + LAG + 1):
                    if m < steps:
                        scores(m)
                    if LAG <= m < steps + LAG:
                        turn_probs(m - LAG)
                    if m < steps:
                        beside(m)
                    done = m - LAG - 1
                    if done >= 0 and done % T == T - 1:
                        values(done // T)

            def sqk_piece(m):
                key = (("sq", 0), ("sq", 1), ("sk", 0), ("sk", 1))[m // KD]
                k = m % KD
                hi, lo = chunk(CH["sq"] + m // KD)
                if k == 0:
                    bank_free(key)
                last = three(tbank(key)[:, :], hi[:, k * P:(k + 1) * P], lo[:, k * P:(k + 1) * P], aT_hi[:, k, :],
                             aT_lo[:, k, :], start=(k == 0), stop=(k == KD - 1))
                if k == KD - 1:
                    last.then_inc(w_used, 1)

            pe.wait_ge(drained["act"], tiles["sg", 1][3][1])
            pe.wait_ge(drained["dve"], tiles["y", 1][3][1])
            pe.wait_ge(c_rows_in, 32)
            softmax_attention(0, FOX_H, HD + 2, q_aug, k_aug, fv, sqk_piece)

            pe.wait_ge(exped, FOX_H * T)
            pe.wait_ge(pt_made, FOX_H * T)
            pe.wait_ge(pv_drained, FOX_H // 2)
            pe.wait_ge(drained["act"], tiles["sk", 1][3][1])

            def z_scores(i, kb):
                n = i * T + kb
                if n >= 6:
                    pe.wait_ge(a_made, n - 5)
                r0, j = (i % 2) * HD, i // 2
                out = bank[n % 6]
                mm(out[:, kb * P:S], skT[r0:r0 + HD, j, kb * P:(kb + 1) * P], sqT[r0:r0 + HD, j, kb * P:S],
                   start=True, stop=False, skip_group_check=True)
                mm(out[:, kb * P:(kb + 1) * P], ident_b[:, :], mask_lt[:, :], start=False, stop=True,
                   skip_group_check=True).then_inc(z_full, 1)

            def rest(i):
                for kb in range(T):
                    if kb == 0:
                        pe.wait_ge(sp_made, (i + 1) * T)
                    for jb in range(kb, T):
                        last = mm(bank[(i * T + kb) % 6][:, jb * P:S], (neg_tri if jb == kb else neg_one)[:, :],
                                  sp[i % 2][:, jb, jb * P:S], start=False, stop=(jb == T - 1),
                                  skip_group_check=True)
                    last.then_inc(rest_full, 1)

            def sb_values(i):
                pe.wait_ge(a_made, (i + 1) * T)
                r0 = (i % 2) * HD
                for kb in range(T):
                    last = mm(bank[6 + i // 2][r0:r0 + HD, kb * P:S], sf[:, kb, i * HD:(i + 1) * HD],
                              az[i % 2][:, kb, kb * P:S], start=(kb == 0), stop=(kb == T - 1),
                              skip_group_check=True)
                last.then_inc(sb_full, 1)

            for kb in range(T):
                z_scores(0, kb)
            for i in range(SB_H):
                if i + 1 < SB_H:
                    z_scores(i + 1, 0)
                    z_scores(i + 1, 1)
                rest(i)
                if i + 1 < SB_H:
                    z_scores(i + 1, 2)
                    z_scores(i + 1, 3)
                sb_values(i)

            left_ready(KD)
            pe.wait_ge(a_made, SB_H * T)
            pe.wait_ge(sb_drained, SB_H // 2)
            for g in range(2):
                weights_moving([("out1", g, t) for t in range(T)],
                               [(CH["out1"] + 4 * g + i, ks) for i, ks in pairs], S, rows=3 * g)

            turn_rows("h2", h_tile, h_made, T)
            left_ready()
            weights_moving([("lq", t) for t in range(T)],
                           [(CH["lq"], (0, 1, 2)), (CH["lq"] + 1, (3, 4, 5)), (CH["lq"] + 2, (6, 7))], LQ_W)
            weights_moving([("lkv", t) for t in range(T)],
                           [(CH["lkv"], (0, 1, 2, 3)), (CH["lkv"] + 1, (4, 5, 6, 7))], RANK)
            for j in range(4):
                for i, name in enumerate(("c", "xv", "b")):
                    weights_still((name, j), CH["conv"] + 3 * j + i)
            pe.wait_ge(lat_scaled, 1)
            for i in range(4):
                bank_free(("latT", i))
                src = lat_q if i < 2 else lat_kv
                for t in range(T):
                    last = turn(tbank(("latT", i))[:, t * P:(t + 1) * P], src[:, t, (i % 2) * P:(i % 2 + 1) * P])
                last.then_inc(tile_full, 1)
            pe.wait_ge(roped, 1)
            bank_free(("krT", 0))
            for t in range(T):
                last = turn(tbank(("krT", 0))[0:ROPE, t * P:(t + 1) * P], lat_q[:, t, RANK:LQ_W])
            last.then_inc(tile_full, 1)
            left_ready(4)
            for k in range(2):
                hi, lo = chunk(CH["uq"] + k)
                for t in range(T):
                    for g in range(2):
                        key = ("uq", t, g)
                        if k == 0:
                            bank_free(key)
                        st = left(k, t)
                        w = UQ_W // 2
                        last = three(tbank(key)[:, 0:w], st[0], st[1], hi[:, g * w:(g + 1) * w],
                                     lo[:, g * w:(g + 1) * w], start=(k == 0), stop=(k == 1))
                        if (t, g) == (T - 1, 1):
                            last.then_inc(w_used, 1)
                        elif k == 1:
                            last.then_inc(tile_full, 1)
            hi, lo = chunk(CH["uk"])
            for i in range(4):
                bank_free(("uk", i))
                for k in range(2):
                    at = slice(k * 512 + i * P, k * 512 + (i + 1) * P)
                    last = three(tbank(("uk", i))[:, :], hi[:, at], lo[:, at], aT_hi[:, 2 + k, :], aT_lo[:, 2 + k, :],
                                 start=(k == 0), stop=(k == 1))
                last.then_inc(w_used if i == 3 else tile_full, 1)
            weights_moving([("uv", t) for t in range(T)], [(CH["uv"], (0, 1))], S, k0=2)
            turn_heads("q2T", MLA_H, QK2, lambda t, i: q2[:, t, i * QK2:(i + 1) * QK2], roped, 2)

            pe.wait_ge(sqs_made, 1)
            bank_free(("ssc", 0))
            for t in range(T):
                last = mm(tbank(("ssc", 0))[:, t:t + 1], sqs[:, 1, t * P:(t + 1) * P], ones[:, :], start=True,
                          stop=True)
            last.then_inc(tile_full, 1)

            left_ready(4)

            def out2c_piece(m):
                g, t, kk = m // 16, m // 4 % 4, m % 4
                key = ("out2c", g, t)
                hi, lo = chunk(CH["out2c"] + 2 * g + kk // 2)
                if kk == 0:
                    bank_free(key)
                st = left(4 + kk, t)
                at = slice(kk % 2 * 512, (kk % 2 + 1) * 512)
                last = three(tbank(key)[:, :], st[0], st[1], hi[:, at], lo[:, at], start=(kk == 0), stop=(kk == 3))
                if t == T - 1 and kk % 2:
                    last.then_inc(w_used, 1)
                elif kk == 3:
                    last.then_inc(tile_full, 1)

            pe.wait_ge(drained["act"], tiles["q2T", MLA_H - 1][3][1])
            pe.wait_ge(drained["dve"], tiles["ssc", 0][3][1])
            softmax_attention(FOX_H * T, MLA_H, QK2, q2T, k2T, v2, out2c_piece)
            pe.wait_ge(exped, (FOX_H + MLA_H) * T)
            pe.wait_ge(pt_made, (FOX_H + MLA_H) * T)
            left_ready(4)
            pe.wait_ge(pv_drained, (FOX_H + MLA_H) // 2)
            for t in range(T):
                for g in range(2):
                    key = ("out2a", t, g)
                    bank_free(key)
                    for k in range(4):
                        hi, lo = chunk(CH["out2a"] + 2 * g + k // 2)
                        st = left(k, t)
                        at = slice(k % 2 * 512, (k % 2 + 1) * 512)
                        last = three(tbank(key)[:, :], st[0], st[1], hi[:, at], lo[:, at], start=(k == 0),
                                     stop=(k == 3))
                        if t == T - 1 and k % 2:
                            last.then_inc(w_used, 1)
                    if t < T - 1:
                        last.then_inc(tile_full, 1)
                if t == 0:
                    pe.wait_ge(sqs_made, 2)
                    for b in range(T):
                        last = mm(tbank(("ssa", 0))[:, b:b + 1], sqs[:, 0, b * P:(b + 1) * P], ones[:, :],
                                  start=True, stop=True)
                    last.then_inc(tile_full, 1)
            pe.wait_ge(p_split, 2)
            for g in range(2):
                weights_moving([("ple", g, t) for t in range(T)], [(CH["ple"] + g, (0, 1))], S)

            turn_rows("h3", h_tile, h_made, 2 * T)
            left_ready()

            def ffn_block(f, c, first):
                for b in range(4):
                    s = (CH["ffn"] + b) % SLOTS
                    pe.wait_ge(w_split, c + b + 1)
                    if not first and b % 2 == 0:
                        pe.wait_ge(ffn_act, f + b // 2 - 1)
                    for k in range(KD):
                        at = slice(k * P, (k + 1) * P)
                        last = three(bank[b][:, :], w_hi[:, s, at], w_lo[:, s, at], aT_hi[:, k, :], aT_lo[:, k, :],
                                     start=(k == 0), stop=(k == KD - 1))
                    last.then_inc(w_used, 1)

            ffn_block(0, CH["ffn"], True)
            with pe.Fori(1, NF // 2) as i:
                ffn_block(i * 2, i * 4 + CH["ffn"], False)

            def down_step(t, slot, first=False, end=False):
                s = (CH["down"] + slot) % SLOTS
                for g in range(2):
                    at = slice(g * 512, (g + 1) * 512)
                    last = three(bank[2 * t + g][:, :], aT_hi[:, slot, t * P:(t + 1) * P],
                                 aT_lo[:, slot, t * P:(t + 1) * P], w_hi[:, s, at], w_lo[:, s, at], start=first,
                                 stop=end)
                    if t == T - 1 and g == 1:
                        last.then_inc(w_used, 1)
                    elif end:
                        last.then_inc(tile_full, 1)

            def down_block(k, slot, first=False):
                pe.wait_ge(staged, k + 1)
                pe.wait_ge(w_split, k + (CH["down"] + 1))
                for t in range(T):
                    down_step(t, slot, first)

            pe.wait_ge(ffn_act, NF)
            for k in range(4):
                down_block(k, k, k == 0)
            rounds = (NF - 4) // 4
            with pe.Fori(1, rounds) as i:
                for j in range(4):
                    down_block(i * 4 + j, j)
            for k in range(4 * rounds, NF - 4):
                down_block(k, k % 4)

            def turn_x(tiles_of):
                turn_rows("xT", lambda t, k: x[:, t, k * P:(k + 1) * P], x_new, 3 * T, tiles_of)

            for t in range(T):
                for k in range(NF - 4, NF):
                    if t == 0:
                        pe.wait_ge(staged, k + 1)
                        pe.wait_ge(w_split, k + CH["down"] + 1)
                    down_step(t, k % 4, end=(k == NF - 1))
                if t == T - 2:
                    turn_x(range(0, 1))

            turn_x(range(1, T - 1))
            weights_moving([("pgate", 0, t) for t in range(T)], group4("pgate"), S, ready=left_row(),
                           late=lambda: turn_x(range(T - 1, T)))
            weights_moving([("pgate", 1, t) for t in range(T)],
                           [(CH["pgate"] + 4 + i, ks) for i, ks in pairs], S, rows=3)

        @block.scalar
        def _(act_):
            A = nc.scalar.activation
            steps, rsq, order, sq = [0], [0], [0], [0]
            junk = PTf[:, 3072:4096]

            def own(ins):
                steps[0] += 1
                ins.then_inc(act_step, 1)
                act_.wait_ge(act_step, steps[0])

            def drain(key, ins):
                order[0] += 1
                assert tiles[key][3] == ("act", order[0]), key
                ins.then_inc(drained["act"], 1)

            def copy(out, in_, scale=1.0):
                return A(out, in_, ACT.Copy, scale=scale)

            def rsqrt(at):
                rsq[0] += 1
                act_.wait_ge(ms_made, rsq[0])
                own(A(stat[:, 2, at], stat[:, 1, at], ACT.Ln))
                A(stat[:, 2, at], stat[:, 2, at], ACT.Exp, scale=-0.5).then_inc(rs_made, 1)

            def squares(in_, at):
                if sq[0]:
                    act_.wait_ge(sq_done, sq[0])
                sq[0] += 1
                A(junk[:, 0:in_.shape[-1]], in_, ACT.Square, accum_out=stat[:, 0, at:at + 1]).then_inc(sq_done, 1)

            def split_hi(out, in_, scale=1.0):
                copy(out, in_, scale).then_inc(mix_hi, 1)

            def norm_rows(name, ready, at0):
                for t in range(T + 1):
                    if t < T:
                        ready(t)
                        squares(x[:, t, :], at0 + t)
                    if t > 0:
                        rsqrt(slice(at0 + t - 1, at0 + t))
                turned_hi(name)

            def turned_hi(name, tiles_of=range(T)):
                for n in range(2 * tiles_of[0], 2 * tiles_of[-1] + 2):
                    t, half = n // 2, n % 2
                    full(act_, (name, n))
                    split_hi(aT_hi[:, 4 * half:4 * half + 4, t * P:(t + 1) * P],
                             tbank((name, n))[:, :].rearrange("p (a b) -> p a b", b=P))

            act_.dma_start(cols[:, :], cols_d).then_inc(const_in, 16)
            act_.dma_start(wpool[:, :, :], wpool_d).then_inc(const_in, 16)
            act_.dma_start(pos_i[:, :], pos_d).then_inc(const_in, 16)
            act_.dma_start(g_pre[:, :], gains_d[0, :, :]).then_inc(g_pre_in, 16)
            act_.dma_start(g_post[:, :], gains_d[3, :, :]).then_inc(g_post_in, 16)

            nc.scalar.preload_act_table_set(LOG_EXP)
            norm_rows("h1", lambda t: act_.wait_ge(x_in[t], 16), 0)

            def qk_rows(name, base):
                for t in range(T):
                    if base and t == 0:
                        act_.wait_ge(tile_full, tiles["qT", FOX_H - 1][1][1])
                    full(act_, (name, t))
                    copy(qk_raw[:, t, :], tbank((name, t))[:, :]).then_inc(act_step, 1)
                    steps[0] += 1
                    n = base + t
                    if n >= 2:
                        act_.wait_ge(qk_reduced, n - 1)
                    A(sq_tmp[:, n % 2, :], tbank((name, t))[:, :], ACT.Square).then_inc(qk_squared, 1)
                    act_.wait_ge(qk_squared, n + 1)
                    order[0] += 1
                    nc.scalar.sem_inc(drained["act"], 1)

            def heads_out(name, n, width, dst, scale=None):
                for i in range(n):
                    full(act_, (name, i))
                    drain((name, i), copy(dst[0:width, i, :], tbank((name, i))[0:width, :],
                                          1.0 if scale is None else scale))

            act_.wait_ge(const_in, 48)
            qk_rows("fq", 0)
            rsqrt(slice(16, 48))
            for t in range(T):
                full(act_, ("fv", t))
                drain(("fv", t), copy(fv[:, t, :], tbank(("fv", t))[:, :]))
            heads_out("qT", FOX_H, HD, q_aug, col("gq")[0:HD])
            qk_rows("fk", T)
            rsqrt(slice(16, 48))
            for t in range(T):
                full(act_, ("sf", t))
                drain(("sf", t), copy(sf[:, t, :], tbank(("sf", t))[:, 0:SF_W]))
            act_.wait_ge(lf_abs, 1)
            own(A(lf[:, 1, :], lf[:, 1, :], ACT.Exp, scale=-1.0))
            A(lf[:, 1, :], lf[:, 1, :], ACT.Ln, bias=1.0).then_inc(lf_exp, 1)
            act_.wait_ge(angles, 1)
            A(cs[:, 0, :, :], cs[:, 0, :, :], ACT.Sin).then_inc(sines, 1)
            A(cs[:, 1, :, :], cs[:, 1, :, :], ACT.Sin).then_inc(sines, 1)

            def gate_rows(name, n, b0):
                for i in range(n):
                    full(act_, (name, i))
                    drain((name, i), A(gate[:, b0 + i, :], tbank((name, i))[:, :], ACT.Silu))

            gate_rows("pg", 2, 4)
            heads_out("kT", FOX_H, HD, k_aug, col("gk")[0:HD])
            gate_rows("fg", 4, 0)
            gate_rows("sg", 2, 6)
            act_.wait_ge(rows_laid, 2)
            act_.wait_ge(cum_made, 1)
            act_.dma_start(q_aug[HD:HD + 1, :, :], cum[:, 0, :]).then_inc(c_rows_in, 16)
            act_.dma_start(k_aug[HD + 1:HD + 2, :, :], cum[:, 1, :]).then_inc(c_rows_in, 16)

            def softmax_attention(base, heads, pair_out, beside):
                steps_ = heads * T
                for m in range(steps_ + 3):
                    beside(m)
                    if m < steps_:
                        n = base + m
                        kw = (m % T + 1) * P
                        act_.wait_ge(maxed, n + 1)
                        if m >= 4:
                            act_.wait_ge(turned, n - 3)
                        A(P_buf[:, n % 4, 0:kw], bank[n % 3][:, 0:kw], ACT.Exp, bias=negmax[:, n % 8:n % 8 + 1],
                          accum_out=esum[:, n % 8:n % 8 + 1]).then_inc(exped, 1)
                    if m >= 3:
                        n, i, qb = base + m - 3, (m - 3) // T, (m - 3) % T
                        act_.wait_ge(turned, n + 1)
                        if qb == 0 and i >= 2:
                            act_.wait_ge(pv_done, base // T + i - 1)
                        copy(PT[:, i % 2, 0:qb + 1, qb * P:(qb + 1) * P],
                             bank[3 + n % 2][:, 0:(qb + 1) * P].rearrange("p (a b) -> p a b", b=P))\
                            .then_inc(pt_made, 1)
                        if pair_out is not None and qb == 1 and i >= 2 and i % 2 == 0:
                            pair_out(i // 2 - 1)
                if pair_out is not None:
                    pair_out(heads // 2 - 1)

            nc.scalar.preload_act_table_set(LOG_EXP)
            act_.wait_ge(pooled_made, 2)
            act_.wait_ge(tile_full, tiles["y", 1][1][1])

            def sqk_out(m):
                if m % KD == 0 and 0 < m <= 4 * KD:
                    i = m // KD - 1
                    key = ("sq" if i < 2 else "sk", i % 2)
                    full(act_, key)
                    drain(key, copy((sqT if i < 2 else skT)[:, i % 2, :], tbank(key)[:, :],
                                    HD ** -0.5 if i < 2 else 1.0))

            softmax_attention(0, FOX_H, None, sqk_out)

            act_.wait_ge(pv_done, FOX_H)

            def sb_logs(i):
                for kb in range(T):
                    n = i * T + kb
                    e = ea[i % 2][:, kb, kb * P:S]
                    act_.wait_ge(z_abs, n + 1)
                    own(A(e, e, ACT.Exp))
                    A(e, e, ACT.Ln, bias=1.0).then_inc(z_ln, 1)

            def sb_weights(i):
                for kb in range(T):
                    n = i * T + kb
                    act_.wait_ge(rest_full, n + 1)
                    if kb == 0 and i >= 2:
                        act_.wait_ge(sb_full, i - 1)
                    A(az[i % 2][:, kb, kb * P:S], bank[n % 6][:, kb * P:S], ACT.Exp).then_inc(a_made, 1)

            sb_logs(0)
            for i in range(SB_H):
                sb_weights(i)
                if i + 1 < SB_H:
                    sb_logs(i + 1)
            act_.wait_ge(gated, 1)
            for b in range(KD):
                split_hi(aT_hi[:, b, :], gate[:, b, :])

            act_.wait_ge(h_made, T)
            act_.dma_start(g_pre[:, :], gains_d[1, :, :]).then_inc(g_pre_in, 16)
            norm_rows("h2", lambda t: act_.wait_ge(x_new, T + t + 1), 4)
            for name, dst, w, at0 in (("lq", lat_q, LQ_W, 48), ("lkv", lat_kv, RANK, 52)):
                for t in range(T):
                    full(act_, (name, t))
                    own(copy(dst[:, t, :], tbank((name, t))[:, 0:w]))
                    drain((name, t), A(PTf[:, 3072:3072 + RANK], tbank((name, t))[:, 0:RANK], ACT.Square,
                                       accum_out=stat[:, 0, at0 + t:at0 + t + 1]))
            rsqrt(slice(48, 56))
            for j in range(4):
                full(act_, ("c", j))
                if j >= 2:
                    act_.wait_ge(conv_y, j - 1)
                drain(("c", j), copy(u[:, j % 2, KERNEL - 1:], tbank(("c", j))[:, :]))
                act_.wait_ge(conv_y, j + 1)
                A(sqs[:, 1, :] if j == 0 else sq2[:, j % 2, :], y[:, j, :], ACT.Square).then_inc(sq_y, 1)
            for i in range(4):
                full(act_, ("latT", i))
                split_hi(aT_hi[:, i, :], tbank(("latT", i))[:, :], col("gq2", i) if i < 2 else col("gkv2", i - 2))
            full(act_, ("krT", 0))
            drain(("krT", 0), copy(k2T[HD:QK2, :, :],
                                   tbank(("krT", 0))[0:ROPE, :].unsqueeze(1).broadcast_to([ROPE, MLA_H, S])))
            for t in range(T):
                for g in range(2):
                    full(act_, ("uq", t, g))
                    drain(("uq", t, g), copy(q2[:, t, g * 384:(g + 1) * 384], tbank(("uq", t, g))[:, 0:384],
                                             QK2 ** -0.5))
            for i in range(4):
                full(act_, ("uk", i))
                own(copy(k2T[0:HD, 2 * i, :], tbank(("uk", i))[0:HD, :]))
                drain(("uk", i), copy(k2T[0:HD, 2 * i + 1, :], tbank(("uk", i))[HD:P, :]))
            for t in range(T):
                full(act_, ("uv", t))
                drain(("uv", t), copy(v2[:, t, :], tbank(("uv", t))[:, :]))
            heads_out("q2T", MLA_H, QK2, q2T)
            rsqrt(slice(60, 64))
            for j in range(4):
                act_.wait_ge(w_used, CH["uv"] + 1)
                split_hi(aT_hi[:, 4 + j, :], y[:, j, :], col("gc", j))

            def pair_out(pair):
                act_.wait_ge(pv_done, FOX_H + 2 * pair + 2)
                out = bank[6 + pair % 2][:, :]
                split_hi(aT_hi[:, pair, :], out, col("ga", pair))
                A(sqs[:, 0, :] if pair == 0 else sq2[:, pair % 2, :], out, ACT.Square).then_inc(sq_y, 1)

            def out2c_out(m):
                if m % 4 == 0 and 0 < m <= 32:
                    g, t = (m // 4 - 1) // T, (m // 4 - 1) % T
                    if m == 4:
                        act_.wait_ge(group_rsqrt, 1)
                    full(act_, ("out2c", g, t))
                    drain(("out2c", g, t), copy(y2[t][:, g * 512:(g + 1) * 512], tbank(("out2c", g, t))[:, :],
                                                stat[:, 3, 60 + t:61 + t]))

            softmax_attention(FOX_H * T, MLA_H, pair_out, out2c_out)
            act_.dma_start(pe_raw, pt_d).then_inc(pt_in, 16)
            act_.wait_ge(h_made, 2 * T)
            act_.dma_start(g_pre[:, :], gains_d[2, :, :]).then_inc(g_pre_in, 16)
            rsqrt(slice(56, 60))

            def ple_hi():
                act_.wait_ge(pt_in, 16)
                act_.wait_ge(w_used, CH["out2a"] + 4)
                for k in range(2):
                    copy(aT_hi[:, k, :], pe_raw[:, k, :]).then_inc(p_hi, 1)


            def ple_out(g):
                for t in range(T):
                    full(act_, ("ple", g, t))
                    drain(("ple", g, t), copy(emb[:, t, g * 512:(g + 1) * 512], tbank(("ple", g, t))[:, :]))

            for t in range(T + 1):
                if t == T - 1:
                    ple_hi()
                if t < T:
                    act_.wait_ge(y2_made, 2 * (t + 1))
                    squares(y2[t], 8 + t)
                    rsqrt(slice(8 + t, 9 + t))
                else:
                    ple_out(0)
                if t > 0:
                    act_.wait_ge(x_new, 2 * T + t)
                    squares(x[:, t - 1, :], 12 + t - 1)
                    rsqrt(slice(12 + t - 1, 12 + t))
            ple_out(1)

            turned_hi("h3")
            act_.wait_ge(x_new, 3 * T)
            act_.dma_start(g_post[:, :], gains_d[5, :, :]).then_inc(g_post_in, 16)
            for t in range(T):
                squares(emb[:, t, :], 40 + t)
            rsqrt(slice(40, 44))
            act_.wait_ge(emb_made, 1)
            act_.dma_start(g_post[:, :], gains_d[4, :, :]).then_inc(g_post_in, 16)

            def weights_hi(c, s, used=None):
                act_.wait_ge(raw_in[s % RAW], (c - s % RAW) * (16 // RAW) + 16)
                if used is not None:
                    act_.wait_ge(w_used, used)
                copy(w_hi[:, s, :], raw[:, s % RAW, :]).then_inc(hi_shared, 1)

            def ffn_silu(f, slot, c, first):
                weights_hi(c + 3, (CH["ffn"] + 2 * slot + 3) % SLOTS, used=c)
                act_.wait_ge(w_used, c + 1)
                if not first:
                    act_.wait_ge(ffn_act, f - 1)
                A(sg_t[:, slot, :], bank[2 * slot][:, :], ACT.Silu).then_inc(ffn_gate, 1)
                weights_hi(c + 4, (CH["ffn"] + 2 * slot + 4) % SLOTS)

            for f in range(2):
                ffn_silu(f, f, CH["ffn"] + 2 * f, True)
            with act_.Fori(1, NF // 2) as i:
                for f in range(2):
                    ffn_silu(i * 2 + f, f, i * 4 + (CH["ffn"] + 2 * f), False)

            def stage(k, slot, used):
                act_.wait_ge(w_used, used)
                copy(aT_hi[:, slot, :].unsqueeze(1), act[:, bass.ds(k, 1), :]).then_inc(stage_hi, 1)

            def down_weights(k, slot):
                c = k + (CH["down"] + 3)
                weights_hi(c, (CH["down"] + 3 + slot) % SLOTS, used=c - 3)

            act_.wait_ge(ffn_act, NF)
            for k in range(4):
                stage(k, k, CH["down"])
            for k in range(4):
                down_weights(k, k)
            rounds = (NF - 4) // 4
            with act_.Fori(1, rounds) as i:
                for j in range(4):
                    stage(i * 4 + j, j, i * 4 + (CH["down"] + j - 3))
                    down_weights(i * 4 + j, j)
            for k in range(4 * rounds, NF - 3):
                stage(k, k % 4, CH["down"] + k - 3)
                down_weights(k, k % 4)
            for k in range(NF - 3, NF):
                stage(k, k % 4, CH["down"] + k - 3)

            nc.scalar.preload_act_table_set(LOG_EXP)
            for t in range(T):
                if t == T - 1:
                    turned_hi("xT", range(0, 1))
                    for k in range(NF - 3, NF - 1):
                        down_weights(k, k % 4)
                for g in range(2):
                    full(act_, ("down", t, g))
                    squares(tbank(("down", t, g))[:, :], 16 + 2 * t + g)
                if t == T - 1:
                    turned_hi("xT", range(1, 2))
                rsqrt(slice(24 + t, 25 + t))
            turned_hi("xT", range(2, T - 1))
            for k in range(NF - 1, NF + 1):
                down_weights(k, k % 4)
            turned_hi("xT", range(T - 1, T))
            for g in range(2):
                for t in range(T):
                    n = g * T + t
                    if (g, t) == (0, T - 1):
                        for k in range(NF + 1, NF + 4):
                            down_weights(k, k % 4)
                    full(act_, ("pgate", g, t))
                    if n >= 2:
                        act_.wait_ge(out_made, n - 1)
                    A(gate_t[:, n % 2, :], tbank(("pgate", g, t))[:, :], ACT.Sigmoid).then_inc(pgate_made, 1)
                    if (g, t) == (0, T - 1):
                        down_weights(NF + 4, (NF + 4) % 4)

        @block.vector
        def _(dve):
            V = nc.vector
            steps, rsq, order, lows, sqn, hn, xn = [0], [0], [0], [0], [0], [0], [0]

            def own(ins):
                steps[0] += 1
                ins.then_inc(dve_step, 1)
                dve.wait_ge(dve_step, steps[0])

            def drain(key, ins):
                order[0] += 1
                assert tiles[key][3] == ("dve", order[0]), (key, order[0])
                ins.then_inc(drained["dve"], 1)

            def stt(out, in0, scalar, in1, op0, op1):
                return V.scalar_tensor_tensor(out=out, in0=in0, scalar=scalar, in1=in1, op0=op0, op1=op1)

            def rsqrt(at, width, ss=None):
                rsq[0] += 1
                V.tensor_scalar(stat[:, 1, at], stat[:, 0, at] if ss is None else ss, 1.0 / width, EPS, ALU.mult,
                                ALU.add).then_inc(ms_made, 1)
                dve.wait_ge(rs_made, rsq[0])
                own(V.tensor_tensor(stat[:, 3, at], stat[:, 2, at], stat[:, 2, at], ALU.mult))
                own(stt(stat[:, 3, at], stat[:, 3, at], -0.5, stat[:, 1, at], ALU.mult, ALU.mult))
                own(stt(stat[:, 3, at], stat[:, 3, at], 1.5, stat[:, 2, at], ALU.add, ALU.mult))

            def split_lo(key, out, in_, hi, scale=None):
                lows[0] += 1
                dve.wait_ge(mix_hi, lows[0])
                if scale is None:
                    ins = V.tensor_tensor(out, in_, hi, ALU.subtract)
                else:
                    ins = stt(out, in_, scale, hi, ALU.mult, ALU.subtract)
                ins.then_inc(mix_lo, 1)
                if key is not None:
                    order[0] += 1
                    assert tiles[key][3] == ("dve", order[0]), key
                    dve.wait_ge(mix_lo, lows[0])
                    V.sem_inc(drained["dve"], 1)

            def norm_row(name, at0, t):
                sqn[0] += 1
                dve.wait_ge(sq_done, sqn[0])
                rsqrt(slice(at0 + t, at0 + t + 1), D)
                if t >= 2:
                    full(dve, (name, 2 * (t - 2) + 1))
                stt(h[:, t % 2, :], x[:, t, :], stat[:, 3, at0 + t:at0 + t + 1], g_pre[:, :], ALU.mult,
                    ALU.mult).then_inc(h_made, 1)

            def turned_lo(name, tiles_of=range(T)):
                for n in range(2 * tiles_of[0], 2 * tiles_of[-1] + 2):
                    t, half = n // 2, n % 2
                    at = (slice(None), slice(4 * half, 4 * half + 4), slice(t * P, (t + 1) * P))
                    split_lo((name, n), aT_lo[at], tbank((name, n))[:, :].rearrange("p (a b) -> p a b", b=P),
                             aT_hi[at].bitcast(F32))

            dve.wait_ge(g_pre_in, 16)
            for t in range(T):
                norm_row("h1", 0, t)
            turned_lo("h1")
            dve.wait_ge(const_in, 48)
            own(V.tensor_copy(pos_f[:, :], pos_i[:, :]))
            for t in range(T):
                own(V.tensor_scalar(cs[:, 0, t, :], col("invf", 0, HALF), pos_f[:, t:t + 1], None, ALU.mult))
            ang = cs[:, 0, :, :].rearrange("p a b -> p (a b)")
            trn = cs[:, 1, :, :].rearrange("p a b -> p (a b)")
            own(V.tensor_scalar(trn, ang, float(1 / (2 * np.pi)), ROUND, ALU.mult, ALU.add))
            own(V.tensor_scalar(trn, trn, -ROUND, None, ALU.add))
            for part in (PI_A, PI_B, PI_C):
                own(stt(ang, trn, -part, ang, ALU.mult, ALU.add))
            own(V.tensor_scalar(ang, ang, 3.1415925, -3.1415925, ALU.min, ALU.max))
            own(stt(trn, ang, -1.0, ang, ALU.mult, ALU.max))
            V.tensor_scalar(trn, trn, -1.0, float(np.pi / 2), ALU.mult, ALU.add).then_inc(angles, 1)

            own(V.tensor_scalar(col("gq"), col("gq"), HD ** -0.5, None, ALU.mult))
            V.memset(q_aug[HD:HD + 2, :, :], 1.0).then_inc(rows_laid, 1)
            V.memset(k_aug[HD:HD + 2, :, :], 1.0).then_inc(rows_laid, 1)

            def qk_norm(base):
                for t in range(T):
                    n = base + t
                    dve.wait_ge(qk_squared, n + 1)
                    V.reduce_sum(stat[:, 0, 16 + 8 * t:24 + 8 * t],
                                 sq_tmp[:, n % 2, :].rearrange("p (a b) -> p a b", b=HD), axis=AX_X)\
                        .then_inc(qk_reduced, 1)
                dve.wait_ge(qk_reduced, base + T)
                rsqrt(slice(16, 48), HD)
                v = qk_raw.rearrange("p a (b c) -> p (a b) c", c=HD)
                V.tensor_tensor(v, v, stat[:, 3, 16:48].unsqueeze(2).broadcast_to([P, T * FOX_H, HD]), ALU.mult)\
                    .then_inc(qk_scaled, 1)

            qk_norm(0)
            qk_norm(T)
            dve.wait_ge(drained["act"], tiles["sf", T - 1][3][1])
            v0 = lf[:, 0, :].rearrange("p (t h) -> p t h", h=FOX_H)
            own(V.tensor_tensor(v0, sf[:, :, SB_H * HD:SF_W],
                                col("bf", 0, FOX_H).unsqueeze(1).broadcast_to([P, T, FOX_H]), ALU.add))
            stt(lf[:, 1, :], lf[:, 0, :], -1.0, lf[:, 0, :], ALU.mult, ALU.max).then_inc(lf_abs, 1)
            dve.wait_ge(lf_exp, 1)
            stt(lf[:, 2, :], lf[:, 0, :], 0.0, lf[:, 1, :], ALU.min, ALU.subtract).then_inc(lf_made, 1)

            full(dve, ("lfT", 0))
            one_row = xp[0:FOX_H, 2, 0:S]
            own(V.memset(one_row, 1.0))
            ins = V.tensor_tensor_scan(cum[:, 0, :], one_row, tbank(("lfT", 0))[0:FOX_H, :], 0.0, ALU.mult, ALU.add)
            drain(("lfT", 0), ins)
            dve.wait_ge(drained["dve"], order[0])
            V.tensor_scalar(cum[:, 1, :], cum[:, 0, :], -1.0, None, ALU.mult).then_inc(cum_made, 1)
            for i in range(2):
                full(dve, ("px", i))
                if i:
                    dve.wait_ge(pooled_made, i)
                a, b, c = xp[:, 0, :], xp[:, 1, :], xp[:, 2, :]
                ins = V.tensor_copy(a[:, PAD:], tbank(("px", i))[:, :])
                drain(("px", i), ins)
                dve.wait_ge(drained["dve"], order[0])
                src, dst, reach = a, b, 0
                w = 1
                halves = (WINDOWS[2 * i], WINDOWS[2 * i + 1])
                while w < halves[1]:
                    lo_p = 0 if w < halves[0] else HD
                    at = reach + w
                    own(V.tensor_tensor(dst[lo_p:, at:], src[lo_p:, at:], src[lo_p:, at - w:S + PAD - w], ALU.add))
                    if 2 * w == halves[0]:
                        own(V.tensor_copy(pooled[0:HD, i, :], dst[0:HD, PAD:]))
                    reach = at
                    w *= 2
                    src, dst = dst, (c if dst is b else b)
                own(V.tensor_copy(pooled[HD:, i, :], src[HD:, PAD:]))
                own(V.tensor_tensor(xp[:, 1, 0:PAD], pooled[:, i, 0:PAD], col("rc", i * PAD, PAD), ALU.mult))
                own(stt(pooled[:, i, :], pooled[:, i, :], col("invw", i), a[:, PAD:], ALU.mult, ALU.subtract))
                V.tensor_tensor(pooled[:, i, 0:PAD], xp[:, 1, 0:PAD], a[:, PAD:2 * PAD], ALU.subtract)\
                    .then_inc(pooled_made, 1)
            dve.wait_ge(drained["act"], tiles["pg", 1][3][1])
            for i in range(2):
                full(dve, ("y", i))
                drain(("y", i), stt(gate[:, 4 + i, :], tbank(("y", i))[:, :], col("ps", i), gate[:, 4 + i, :],
                                    ALU.mult, ALU.mult))

            def softmax_attention(base, heads, pair_out):
                steps_ = heads * T
                for m in range(steps_ + 1):
                    if m < steps_:
                        n = base + m
                        kw = (m % T + 1) * P
                        dve.wait_ge(scored, n + 1)
                        V.tensor_reduce(negmax[:, n % 8:n % 8 + 1], bank[n % 3][:, 0:kw], AX_X, ALU.max, negate=True)\
                            .then_inc(maxed, 1)
                    if m > 0:
                        n = base + m - 1
                        kw = ((m - 1) % T + 1) * P
                        dve.wait_ge(exped, n + 1)
                        own(V.reciprocal(erec[:, n % 8:n % 8 + 1], esum[:, n % 8:n % 8 + 1]))
                        V.tensor_scalar(P_buf[:, n % 4, 0:kw], P_buf[:, n % 4, 0:kw], erec[:, n % 8:n % 8 + 1],
                                        None, ALU.mult).then_inc(normed, 1)
                    if m % (2 * T) == T + 1 and m > 2 * T:
                        pair_out(m // (2 * T) - 1)
                pair_out(heads // 2 - 1)

            def fox_pair(pair):
                dve.wait_ge(pv_done, 2 * pair + 2)
                V.tensor_tensor(gate[:, pair, :], bank[6 + pair % 2][:, :], gate[:, pair, :], ALU.mult)\
                    .then_inc(pv_drained, 1)

            softmax_attention(0, FOX_H, fox_pair)
            dve.wait_ge(pv_drained, FOX_H // 2)

            def sb_abs(i, kbs):
                for kb in kbs:
                    n = i * T + kb
                    dve.wait_ge(z_full, n + 1)
                    if kb == 0 and i >= 2:
                        dve.wait_ge(rest_full, (i - 1) * T)
                    r, z = sp[i % 2][:, kb, kb * P:S], bank[n % 6][:, kb * P:S]
                    own(V.tensor_scalar(r, z, 0.0, None, ALU.max))
                    stt(ea[i % 2][:, kb, kb * P:S], r, -2.0, z, ALU.mult, ALU.add).then_inc(z_abs, 1)

            def sb_softplus(i):
                for kb in range(T):
                    n = i * T + kb
                    dve.wait_ge(z_ln, n + 1)
                    r = sp[i % 2][:, kb, kb * P:S]
                    V.tensor_tensor(r, r, ea[i % 2][:, kb, kb * P:S], ALU.add).then_inc(sp_made, 1)

            def sb_out(pair):
                dve.wait_ge(sb_full, 2 * pair + 2)
                V.tensor_tensor(gate[:, 6 + pair, :], bank[6 + pair][:, :], gate[:, 6 + pair, :], ALU.mult)\
                    .then_inc(sb_drained, 1)

            dve.wait_ge(pv_done, FOX_H)
            sb_abs(0, range(T))
            sb_softplus(0)
            for i in range(1, SB_H):
                sb_abs(i, range(T))
                sb_softplus(i)
                if i % 2 == 0:
                    sb_out(i // 2 - 1)
            sb_out(SB_H // 2 - 1)
            dve.wait_ge(sb_drained, SB_H // 2)
            V.sem_inc(gated, 1)
            for b in range(KD):
                split_lo(None, aT_lo[:, b, :], gate[:, b, :], aT_hi[:, b, :].bitcast(F32))

            def add_out1(g, t):
                full(dve, ("out1", g, t))
                at = x[:, t, g * 512:(g + 1) * 512]
                xn[0] += 1
                V.tensor_tensor(at, at, tbank(("out1", g, t))[:, :], ALU.add).then_inc(x_new, 1)
                dve.wait_ge(x_new, xn[0])
                order[0] += 1
                V.sem_inc(drained["dve"], 1)

            for t in range(T):
                add_out1(0, t)
            dve.wait_ge(g_pre_in, 32)
            for t in range(T + 1):
                if t < T:
                    add_out1(1, t)
                if t > 0:
                    norm_row("h2", 4, t - 1)
            turned_lo("h2")
            dve.wait_ge(drained["act"], tiles["lkv", T - 1][3][1])
            rsqrt(slice(48, 56), RANK)
            for t in range(T):
                own(V.tensor_scalar(lat_q[:, t, 0:RANK], lat_q[:, t, 0:RANK], stat[:, 3, 48 + t:49 + t], None,
                                    ALU.mult))
                own(V.tensor_scalar(lat_kv[:, t, :], lat_kv[:, t, :], stat[:, 3, 52 + t:53 + t], None, ALU.mult))
            V.sem_inc(lat_scaled, 1)

            def rotate(t1, t2, sn, cn, w):
                own(V.tensor_tensor(w[0], t1, cn, ALU.mult))
                own(V.tensor_tensor(w[1], t2, sn, ALU.mult))
                own(V.tensor_tensor(w[2], t2, cn, ALU.mult))
                own(V.tensor_tensor(w[3], t1, sn, ALU.mult))
                own(V.tensor_tensor(t1, w[0], w[1], ALU.subtract))
                own(V.tensor_tensor(t2, w[2], w[3], ALU.add))

            dve.wait_ge(sines, 2)
            w = [rope_t[:, j, 0:T * HALF].rearrange("p (a b) -> p a b", b=HALF) for j in range(4)]
            rotate(lat_q[:, :, RANK:RANK + HALF], lat_q[:, :, RANK + HALF:LQ_W], cs[:, 0, :, :], cs[:, 1, :, :], w)
            V.sem_inc(roped, 1)

            own(V.memset(u[:, :, 0:KERNEL - 1], 0.0))
            for j in range(4):
                dve.wait_ge(drained["act"], tiles["c", j][3][1])
                full(dve, ("xv", j))
                uj = u[:, j % 2, :]
                ins = V.tensor_tensor(uj[:, KERNEL - 1:], uj[:, KERNEL - 1:], tbank(("xv", j))[:, :], ALU.mult)
                drain(("xv", j), ins)
                dve.wait_ge(drained["dve"], order[0])
                own(V.tensor_scalar(y[:, j, :], uj[:, KERNEL - 1:], col("conv", j * KERNEL), None, ALU.mult))
                for tap in range(1, KERNEL):
                    own(stt(y[:, j, :], uj[:, KERNEL - 1 - tap:KERNEL - 1 - tap + S], col("conv", j * KERNEL + tap),
                            y[:, j, :], ALU.mult, ALU.add))
                full(dve, ("b", j))
                ins = V.tensor_tensor(y[:, j, :], y[:, j, :], tbank(("b", j))[:, :], ALU.mult)
                drain(("b", j), ins)
                dve.wait_ge(drained["dve"], order[0])
                V.sem_inc(conv_y, 1)
                dve.wait_ge(sq_y, j + 1)
                if j > 0:
                    own(V.tensor_tensor(sqs[:, 1, :], sqs[:, 1, :], sq2[:, j % 2, :], ALU.add))
            V.sem_inc(sqs_made, 1)
            for i in range(4):
                split_lo(("latT", i), aT_lo[:, i, :], tbank(("latT", i))[:, :], aT_hi[:, i, :].bitcast(F32),
                         col("gq2", i) if i < 2 else col("gkv2", i - 2))
            dve.wait_ge(drained["act"], tiles["uq", T - 1, 1][3][1])
            for t in range(T):
                qt = q2[:, t, :].rearrange("p (h c) -> p h c", c=QK2)
                w = [rope_t[:, j, :].rearrange("p (a b) -> p a b", b=HALF) for j in range(4)]
                sn, cn = (cs[:, j, t, :].unsqueeze(1).broadcast_to([P, MLA_H, HALF]) for j in (0, 1))
                rotate(qt[:, :, HD:HD + HALF], qt[:, :, HD + HALF:], sn, cn, w)
            V.sem_inc(roped, 1)

            def group_rms(key, at):
                full(dve, (key, 0))
                rsqrt(at, 512, ss=tbank((key, 0))[:, 0:T])
                order[0] += 1
                assert tiles[key, 0][3] == ("dve", order[0]), key
                V.sem_inc(drained["dve"], 1)
                V.sem_inc(group_rsqrt, 1)

            group_rms("ssc", slice(60, 64))
            for j in range(4):
                split_lo(None, aT_lo[:, 4 + j, :], y[:, j, :], aT_hi[:, 4 + j, :].bitcast(F32), col("gc", j))

            def mla_pair(pair):
                out = bank[6 + pair % 2][:, :]
                dve.wait_ge(sq_y, 4 + pair + 1)
                split_lo(None, aT_lo[:, pair, :], out, aT_hi[:, pair, :].bitcast(F32), col("ga", pair))
                if pair > 0:
                    own(V.tensor_tensor(sqs[:, 0, :], sqs[:, 0, :], sq2[:, pair % 2, :], ALU.add))
                dve.wait_ge(mix_lo, lows[0])
                V.sem_inc(pv_drained, 1)

            softmax_attention(FOX_H * T, MLA_H, mla_pair)
            V.sem_inc(sqs_made, 1)

            def add_post(t, halves, at):
                for n, (lo_c, hi_c, value) in enumerate(halves):
                    w = post_t[:, t % 2, lo_c:hi_c]
                    own(stt(w, value, stat[:, 3, at:at + 1], g_post[:, lo_c:hi_c], ALU.mult, ALU.mult))
                xn[0] += 1
                V.tensor_tensor(x[:, t, :], x[:, t, :], post_t[:, t % 2, :], ALU.add).then_inc(x_new, 1)

            def out2_row(t):
                for g in range(2):
                    key = ("out2a", t, g)
                    full(dve, key)
                    at = y2[t][:, g * 512:(g + 1) * 512]
                    if (t, g) == (0, 0):
                        full(dve, ("ssa", 0))
                        rsqrt(slice(56, 60), 512, ss=tbank(("ssa", 0))[:, 0:T])
                    stt(at, tbank(key)[:, :], stat[:, 3, 56 + t:57 + t], at, ALU.mult, ALU.add).then_inc(y2_made, 1)
                    dve.wait_ge(y2_made, 2 * t + g + 1)
                    order[0] += 1
                    assert tiles[key][3] == ("dve", order[0]), key
                    V.sem_inc(drained["dve"], 1)
                if t == 0:
                    order[0] += 1
                    V.sem_inc(drained["dve"], 1)
                sqn[0] += 1
                dve.wait_ge(sq_done, sqn[0])
                rsqrt(slice(8 + t, 9 + t), D)
                add_post(t, [(0, D, y2[t])], 8 + t)

            dve.wait_ge(g_post_in, 16)
            dve.wait_ge(g_pre_in, 48)
            for t in range(T + 1):
                if t == T - 1:
                    for k in range(2):
                        dve.wait_ge(p_hi, k + 1)
                        V.tensor_tensor(aT_lo[:, k, :], pe_raw[:, k, :], aT_hi[:, k, :].bitcast(F32), ALU.subtract)\
                            .then_inc(p_split, 1)
                if t < T:
                    out2_row(t)
                if t > 0:
                    norm_row("h3", 12, t - 1)

            turned_lo("h3")
            dve.wait_ge(g_post_in, 32)
            sqn[0] += T
            dve.wait_ge(sq_done, sqn[0])
            rsqrt(slice(40, 44), D)
            for t in range(T):
                own(stt(emb[:, t, :], emb[:, t, :], stat[:, 3, 40 + t:41 + t], g_post[:, :], ALU.mult, ALU.mult))
            V.sem_inc(emb_made, 1)

            def ffn_rows(f, slot, c):
                dve.wait_ge(ffn_gate, f + 1)
                dve.wait_ge(w_used, c + 2)
                V.tensor_tensor(act[:, bass.ds(f, 1), :], sg_t[:, slot, :].unsqueeze(1),
                                bank[2 * slot + 1][:, :].unsqueeze(1), ALU.mult).then_inc(ffn_act, 1)

            for f in range(2):
                ffn_rows(f, f, CH["ffn"] + 2 * f)
            with dve.Fori(1, NF // 2) as i:
                for f in range(2):
                    ffn_rows(i * 2 + f, f, i * 4 + (CH["ffn"] + 2 * f))

            def stage(k, slot):
                dve.wait_ge(stage_hi, k + 1)
                V.tensor_tensor(aT_lo[:, slot, :].unsqueeze(1), act[:, bass.ds(k, 1), :],
                                aT_hi[:, slot, :].bitcast(F32).unsqueeze(1), ALU.subtract).then_inc(staged, 1)

            dve.wait_ge(ffn_act, NF)
            for k in range(4):
                stage(k, k)
            with dve.Fori(1, NF // 4) as i:
                for j in range(4):
                    stage(i * 4 + j, j)
            for k in range(NF // 4 * 4, NF):
                stage(k, k % 4)

            dve.wait_ge(g_post_in, 48)
            for t in range(T):
                if t == T - 1:
                    turned_lo("xT", range(0, 1))
                sqn[0] += 2
                dve.wait_ge(sq_done, sqn[0])
                own(V.tensor_tensor(stat[:, 0, 24 + t:25 + t], stat[:, 0, 16 + 2 * t:17 + 2 * t],
                                    stat[:, 0, 17 + 2 * t:18 + 2 * t], ALU.add))
                rsqrt(slice(24 + t, 25 + t), D)
                if t == T - 1:
                    turned_lo("xT", range(1, T - 1))
                add_post(t, [(g * 512, (g + 1) * 512, tbank(("down", t, g))[:, :]) for g in range(2)], 24 + t)
                for g in range(2):
                    if t < T - 1:
                        order[0] += 1
                    V.sem_inc(drained[tiles["down", t, g][3][0]], 1)

            turned_lo("xT", range(T - 1, T))
            for g in range(2):
                for t in range(T):
                    n = g * T + t
                    dve.wait_ge(pgate_made, n + 1)
                    s = gate_t[:, n % 2, :]
                    own(V.tensor_tensor(s, s, emb[:, t, g * 512:(g + 1) * 512], ALU.mult))
                    at = x[:, t, g * 512:(g + 1) * 512]
                    V.tensor_tensor(at, at, s, ALU.add).then_inc(out_made, 1)


def cut_moving(w, ks, at=slice(None)):
    c = np.concatenate([w[k * P:(k + 1) * P, at] for k in ks], axis=1)
    return np.pad(c, ((0, 0), (0, CW - c.shape[1])))


def cut_still(w, at):
    return w[:, at].reshape(KD, P, P).transpose(1, 0, 2).reshape(P, CW)


def lay_out_weights(w_in, w_out, w_in2, w_uq, w_ukv, w_out2, w_gate, w_up, w_down, w_ple, w_pgate):
    c = []
    pairs = [(0, 1), (2, 3), (4, 5), (6, 7)]
    threes = [(0, 1, 2), (3, 4, 5), (6, 7)]
    fq, fk, fv, fg, ff, px, pg, sq, sk, sv, sg = (
        0, 512, 1024, 1536, 2048, 2056, 2312, 2568, 2824, 3080, 3336)

    def moving(w, at, groups):
        c.extend(cut_moving(w, ks, at) for ks in groups)

    def still(w, at, n):
        c.extend(cut_still(w, slice(at + i * P, at + (i + 1) * P)) for i in range(n))

    for at in (fq, fv, fk):
        moving(w_in, slice(at, at + S), pairs)
    moving(np.concatenate([w_in[:, sv:sv + SB_H * HD], w_in[:, ff:ff + FOX_H]], axis=1), slice(None), threes)
    for at, n in ((pg, 2), (px, 2), (fg, 4), (sg, 2), (sq, 2), (sk, 2)):
        still(w_in, at, n)
    for g in range(2):
        moving(w_out, slice(g * 512, (g + 1) * 512), pairs)
    kr, cb, cc, cx = 2 * RANK, 2 * RANK + ROPE, 2 * RANK + ROPE + 512, 2 * RANK + ROPE + 1024
    moving(np.concatenate([w_in2[:, :RANK], w_in2[:, kr:kr + ROPE]], axis=1), slice(None), threes)
    moving(w_in2, slice(RANK, 2 * RANK), [(0, 1, 2, 3), (4, 5, 6, 7)])
    for j in range(4):
        for at in (cc, cx, cb):
            still(w_in2, at + j * P, 1)
    moving(w_uq, slice(None), [(0,), (1,)])
    by_head = w_ukv.reshape(RANK, MLA_H, 2, HD)
    for part in range(2):
        moving(by_head[:, :, part, :].reshape(RANK, 512), slice(None), [(0, 1)])
    for half in (pairs[2:], pairs[:2]):
        for g in range(2):
            moving(w_out2, slice(g * 512, (g + 1) * 512), half)
    for g in range(2):
        moving(w_ple, slice(g * 512, (g + 1) * 512), [(0, 1)])
    for f in range(NF):
        still(w_gate, f * P, 1)
        still(w_up, f * P, 1)
    moving(w_down, slice(None), [(k,) for k in range(NF)])
    for g in range(2):
        moving(w_pgate, slice(g * 512, (g + 1) * 512), pairs)
    return np.ascontiguousarray(np.stack(c))


def by_partition(v):
    return v.reshape(-1, P).T


def kernel(**inputs):
    import concourse.bacc as _bacc
    from concourse.bass_utils import run_bass_kernel_spmd as _run

    a = {k: np.asarray(v) for k, v in inputs.items()}
    w = lay_out_weights(a["w_in"][0], a["w_out"][0], a["w_in_2"][0], a["w_uq_2"][0], a["w_ukv_2"][0], a["w_out_2"][0],
                        a["w_gate_2"][0], a["w_up_2"][0], a["w_down_2"][0], a["w_ple_proj_2"][0], a["w_ple_gate_2"][0])
    f32 = np.float32
    halves = np.repeat(np.array(WINDOWS, f32).reshape(2, 2), HD, axis=1)
    rc = 1 / np.minimum(np.arange(1, PAD + 1, dtype=f32)[None, None, :], halves[:, :, None])
    invf = (1.0 / (f32(10000.0) ** (np.arange(HALF, dtype=f32) / f32(HALF)))).astype(f32)
    cols = np.concatenate([
        np.tile(a["q_norm_g"][0], 2)[:, None], np.tile(a["k_norm_g"][0], 2)[:, None],
        by_partition(a["q_norm_2"][0]), by_partition(a["kv_norm_2"][0]),
        a["conv_w_2"][0].reshape(KERNEL, 4, P).transpose(2, 1, 0).reshape(P, 4 * KERNEL),
        by_partition(a["attn_group_norm_2"][0]), by_partition(a["conv_group_norm_2"][0]),
        by_partition(a["pool_scale"][0]),
        np.broadcast_to(a["b_f"][0][None, :], (P, FOX_H)), np.broadcast_to(invf[None, :], (P, HALF)),
        rc.transpose(1, 0, 2).reshape(P, 2 * PAD).astype(f32), (1 / halves).T.astype(f32),
    ], axis=1)
    pos = a["positions_2"].reshape(T, P).T
    wpool = np.zeros((P, 2, P), f32)
    for g in range(4):
        r = slice((g % 2) * HD, (g % 2 + 1) * HD)
        wpool[r, g // 2, r] = a["w_pool"][0, g]
    pt = a["p_2"][0, 0].T.reshape(2, P, S).transpose(1, 0, 2)
    gains = np.stack([np.broadcast_to(a[n][0][None, :], (P, D)) for n in (
        "norm_g", "mix_pre_norm_2", "ffn_pre_norm_2", "mix_post_norm_2", "ffn_post_norm_2", "ple_norm_2")])
    arrays = {"x": a["x"].reshape(S, D), "weights": w, "cols": cols, "pos": pos, "wpool": wpool, "pt": pt,
              "gains": gains}
    arrays = {k: np.ascontiguousarray(v) for k, v in arrays.items()}
    nc = _bacc.Bacc("TRN2", target_bir_lowering=False, num_devices=1)
    args = [nc.dram_tensor("in_" + k, v.shape, mybir.dt.from_np(v.dtype), kind="ExternalInput").ap() for k, v in arrays.items()]
    out = nc.dram_tensor("y_out", (S, D), F32, kind="ExternalOutput").ap()
    hybrid_kernel(nc, *args, out)
    r = _run(nc, [{"in_" + k: v for k, v in arrays.items()}], core_ids=[0])
    return r.results[0]["y_out"].reshape(1, S, D)
```

```python
from contextlib import ExitStack

import numpy as np

import concourse.bass as bass
from concourse import mybir

P = 128
F32 = mybir.dt.float32
F32R = mybir.dt.float32r
BF16 = mybir.dt.bfloat16
I32 = mybir.dt.int32
ALU = mybir.AluOpType
ACT = mybir.ActivationFunctionType
AX_X = mybir.AxisListType.X

LOG_EXP = "natural_log_exp_and_others"

S, D = 512, 1024
T = S // P
KD = D // P
HD = 64
FOX_H, SB_H, MLA_H = 8, 4, 8
ROPE, HALF = 32, 16
QK2 = HD + ROPE
RANK = 256
SF_W = SB_H * HD + FOX_H
LQ_W = RANK + ROPE
UQ_W = MLA_H * QK2
FF = 2816
NF = FF // P
EPS = 1e-6
NEG = -1e30
PAD = 16
WINDOWS = (2, 4, 8, 16)
KERNEL = 3

CW = 1024
SLOTS = 4
RAW = 2
SB_ORDER = (0, 1, 3, 2)
SPARE = 5

CHUNKS = (("fq", 4), ("fv", 4), ("fk", 4), ("sf", 3), ("pg", 2), ("px", 2), ("fg", 4), ("sg", 2), ("sq", 2),
          ("sk", 2), ("out1", 8), ("lq", 3), ("lkv", 2), ("conv", 12), ("uq", 2), ("uk", 1), ("uv", 1),
          ("out2c", 4), ("out2a", 4), ("ple", 2), ("ffn", 2 * NF), ("down", NF), ("pgate", 8))
CH, NCH = {}, 0
for _name, _n in CHUNKS:
    CH[_name] = NCH
    NCH += _n

SHARED = CH["ple"]

COLS, NCOL = {}, 0
for _name, _n in (("gq", 1), ("gk", 1), ("gq2", 2), ("gkv2", 2), ("conv", 4 * KERNEL), ("ga", 4), ("gc", 4), ("ps", 2),
                  ("bf", FOX_H), ("invf", HALF), ("rc", 2 * PAD), ("invw", 2)):
    COLS[_name] = NCOL
    NCOL += _n

PI_A = 6.28125
PI_B = float(np.round((2 * np.pi - PI_A) * 2.0**21) / 2.0**21)
PI_C = float(np.float32(2 * np.pi - PI_A - PI_B))
ROUND = 1.5 * 2.0**23


def psum_tiles():
    tiles = {}
    for n in range(2 * T):
        tiles["h1", n] = (n, "dve", None)

    def group(name, banks, drainer, width_chunks, n=T):
        for t in range(n):
            chunk = CH[width_chunks[0]] + width_chunks[1] if t == n - 1 else None
            tiles[name, t] = (banks[t % len(banks)], drainer, chunk)

    group("fq", (0, 1, 2, 3), "act", ("fq", 3))
    group("fv", (4, 5, 6, 7), "act", ("fv", 3))
    for i in range(FOX_H):
        tiles["qT", i] = (i, "act", None)
    group("fk", (0, 1, 2, 3), "act", ("fk", 3))
    group("sf", (4, 5, 6, 7), "act", ("sf", 2))
    n = 0
    for name in ("pg", "kT", "lfT", "px", "fg", "y", "sg"):
        for i in range({"kT": FOX_H, "lfT": 1, "fg": 4}.get(name, 2)):
            tiles[name, i] = (n % 8, "dve" if name in ("px", "lfT", "y") else "act",
                              None if name in ("lfT", "y", "kT") else CH[name] + i)
            n += 1
    for name in ("sq", "sk"):
        for i in range(2):
            tiles[name, i] = (SPARE, "act", CH[name] + i)
    for t in range(T):
        tiles["out1a", t] = (7, "dve", CH["out1"] + 2 if t == T - 1 else None)
    for t in range(T):
        if t == T - 1:
            for half in range(2):
                tiles["h2", half] = (4 * half, "dve", None)
        tiles["out1b", t] = (4 + t, "dve", CH["out1"] + 6 if t == T - 1 else None)
        tiles["out1c", t] = (t, "dve", CH["out1"] + 7 if t == T - 1 else None)
    for n in range(2, 2 * T):
        tiles["h2", n] = (n // 2 + 4 * (n % 2), "dve", None)
    group("lq", (0, 1, 2, 3), "act", ("lq", 2))
    group("lkv", (4, 5, 6, 7), "act", ("lkv", 1))
    n = 0
    for j in range(4):
        for i, name in enumerate(("c", "xv", "b")):
            tiles[name, j] = (n % 8, "act" if name == "c" else "dve", CH["conv"] + 3 * j + i)
            n += 1
    for i in range(4):
        tiles["latT", i] = (4 + i, "dve", None)
    tiles["krT", 0] = (0, "act", None)
    for t in range(T):
        for g in range(2):
            tiles["uq", t, g] = (2 * t + g, "act", CH["uq"] + 1 if (t, g) == (T - 1, 1) else None)
    for i in range(4):
        tiles["uk", i] = (i, "act", CH["uk"] if i == 3 else None)
    tiles["ssc", 0] = (7, "dve", None)
    group("uv", (4, 5, 6, 7), "act", ("uv", 0))
    for i in range(MLA_H):
        tiles["q2T", i] = ((2, 0, 1, SPARE, 3, 4, 6, 7)[i], "act", None)
    for g in range(2):
        for t in range(T):
            tiles["out2c", g, t] = (SPARE, "act", CH["out2c"] + 2 * g + 1 if t == T - 1 else None)
    for t in range(T):
        for g in range(2):
            tiles["out2a", t, g] = (2 * t + g, "dve" if t < T - 1 else "dve_last",
                                    CH["out2a"] + 2 * g + 1 if t == T - 1 else None)
        if t == 0:
            tiles["ssa", 0] = (7, "dve", None)
    for t in range(T):
        for g in range(2):
            tiles["ple", g, t] = (2 * (t % 2) + g, "act", CH["ple"] + g if t == T - 1 else None)
        if t < 2:
            for n in range(2):
                tiles["h3", 2 * t + n] = (4 + n, "dve", None)
    for n in range(4, 2 * T):
        tiles["h3", n] = (n, "dve", None)
    for t in range(T):
        for g in range(2):
            tiles["down", t, g] = (2 * t + g, "dve" if t < T - 1 else "dve_last",
                                   CH["down"] + NF - 1 if (t, g) == (T - 1, 1) else None)
        if t == T - 2:
            for n in range(2):
                tiles["xT", n] = (n, "dve", None)
    for n in range(2, 2 * T):
        tiles["xT", n] = (n, "dve", None)
    for t in range(T - 1):
        tiles["pgate", 0, t] = (t, "act", None)
    tiles["pgate", 0, T - 1] = (T - 1, "act", CH["pgate"] + 3)
    for t in range(T):
        tiles["pgate", 1, t] = (4 + t, "act", CH["pgate"] + 7 if t == T - 1 else None)
    return tiles


def tile_counts(tiles):
    full, drained, before, out = 0, {"act": 0, "dve": 0, "dve_last": 0}, {}, {}
    for key, (bank, drainer, chunk) in tiles.items():
        if chunk is None:
            full += 1
        drained[drainer] += 1
        own = (drainer, drained[drainer])
        out[key] = (bank, ("tile", full) if chunk is None else ("chunk", chunk + 1), before.get(bank), own)
        before[bank] = own
    return out


def hybrid_kernel(nc, x_d, w_d, cols_d, pos_d, wpool_d, pt_d, gains_d, out_d):
    tiles = tile_counts(psum_tiles())
    with ExitStack() as ctx:
        def sb(name, shape, dt=F32):
            return ctx.enter_context(nc.sbuf_tensor(name, shape, dt))

        def sem(name):
            return ctx.enter_context(nc.semaphore(name))

        x = sb("x", [P, T, D])
        h = sb("h", [P, 2, D])
        aT_hi = sb("aT_hi", [P, KD, S], F32R)
        aT_lo = sb("aT_lo", [P, KD, S], F32R)
        raw = sb("raw", [P, RAW, CW])
        w_hi = sb("w_hi", [P, SLOTS, CW], F32R)
        w_lo = sb("w_lo", [P, SLOTS, CW], F32R)
        g_pre = sb("g_pre", [P, D])
        g_post = sb("g_post", [P, D])
        PT = sb("PT", [P, 2, T, S])
        arena = sb("arena", [P, 19488])
        ident = sb("ident", [P, P])
        ident_b = sb("ident_b", [P, P], BF16)
        mask_le = sb("mask_le", [P, P], BF16)
        mask_lt = sb("mask_lt", [P, P], BF16)
        neg_tri = sb("neg_tri", [P, P])
        neg_one = sb("neg_one", [P, P])
        ones = sb("ones", [P, 1])
        cols = sb("cols", [P, NCOL])
        wpool = sb("wpool", [P, 2, P])
        pos_i = sb("pos_i", [P, T], I32)
        pos_f = sb("pos_f", [P, T])
        cs = sb("cs", [P, 2, T, HALF])
        stat = sb("stat", [P, 4, 64])
        negmax = sb("negmax", [P, 8])
        esum = sb("esum", [P, 8])
        erec = sb("erec", [P, 8])
        bank = [ctx.enter_context(nc.psum_tensor(f"bank{i}", [P, 512], F32)) for i in range(8)]

        P_buf = h[:, :, :].rearrange("p a (b c) -> p (a b) c", c=S)
        PTf = PT[:, :, :, :].rearrange("p a b c -> p (a b c)")

        def view(base, at, *shape):
            v = base[:, at:at + int(np.prod(shape))]
            if len(shape) == 2:
                v = v.rearrange("p (a b) -> p a b", b=shape[1])
            elif len(shape) == 3:
                v = v.rearrange("p (a b c) -> p a b c", b=shape[1], c=shape[2])
            return v

        def ar(at, *shape):
            return view(arena, at, *shape)

        def col(name, i=0, n=1):
            return cols[:, COLS[name] + i:COLS[name] + i + n]

        qk_raw = ar(0, T, S)
        fv = ar(2048, T, S)
        sf = ar(4096, T, SF_W)
        gate = ar(5152, KD, S)
        sqT = ar(9248, 2, S)
        skT = ar(10272, 2, S)
        q_aug = ar(11296, FOX_H, S)
        k_aug = ar(15392, FOX_H, S)
        sq_tmp = view(PTf, 0, 2, S)
        xp = view(PTf, 1024, 3, S + PAD)
        pooled = view(PTf, 2608, 2, S)
        lf = view(PTf, 3632, 3, T * FOX_H)
        cum = ar(0, 2, S)[0:FOX_H]
        sp = [PT[:, 0, :, :], ar(11296, T, S)]
        az = [PT[:, 1, :, :], ar(13344, T, S)]
        ea = [ar(15392, T, S), ar(17440, T, S)]
        y = ar(0, 4, S)
        u = ar(2048, 2, S + KERNEL - 1)
        sqs = ar(3076, 2, S)
        sq2 = ar(4100, 2, S)
        q2 = ar(5124, T, UQ_W)
        q2T = ar(8196, MLA_H, S)
        k2T = ar(12292, MLA_H, S)
        v2 = ar(16388, T, S)
        lat_q = ar(16388, T, LQ_W)
        lat_kv = ar(5124, T, RANK)
        rope_t = view(PTf, 0, 4, MLA_H * HALF)
        y2 = [ar(5124 + t * D, D) for t in range(T - 1)] + [ar(18436, D)]
        act = ar(0, NF, S)
        sg_t = ar(11264, 2, S)
        emb = ar(12288, T, D)
        pe_raw = ar(0, 2, S)
        post_t = view(PTf, 1024, 2, D)
        gate_t = view(PTf, 3072, 2, S)

        x_in = [sem(f"x_in{t}") for t in range(T)]
        raw_in = [sem(f"raw_in{i}") for i in range(RAW)]
        const_in = sem("const_in")
        g_pre_in, g_post_in = sem("g_pre_in"), sem("g_post_in")
        pt_in = sem("pt_in")
        rows_laid, c_rows_in = sem("rows_laid"), sem("c_rows_in")
        out_stored = sem("out_stored")
        masks_made = sem("masks_made")
        hi_made, hi_shared, w_split, w_used = sem("hi_made"), sem("hi_shared"), sem("w_split"), sem("w_used")
        tile_full = sem("tile_full")
        drained = {"act": sem("drained_act"), "dve": sem("drained_dve"), "dve_last": sem("drained_dve_last")}
        sq_done = sem("sq_done")
        ms_made = sem("ms_made")
        rs_made = sem("rs_made")
        h_made, h_hi = sem("h_made"), sem("h_hi")
        act_step, dve_step = sem("act_step"), sem("dve_step")
        qk_squared, qk_reduced, qk_scaled = sem("qk_squared"), sem("qk_reduced"), sem("qk_scaled")
        gated = sem("gated")
        lf_abs, lf_exp, lf_made, cum_made = sem("lf_abs"), sem("lf_exp"), sem("lf_made"), sem("cum_made")
        pooled_made = sem("pooled_made")
        sines = sem("sines")
        angles = sem("angles")
        scored, maxed, exped, normed = sem("scored"), sem("maxed"), sem("exped"), sem("normed")
        turned, pt_made, pv_done, pv_drained = sem("turned"), sem("pt_made"), sem("pv_done"), sem("pv_drained")
        z_full, z_abs, z_exp, z_ln, sp_made = sem("z_full"), sem("z_abs"), sem("z_exp"), sem("z_ln"), sem("sp_made")
        rest_full, a_made, sb_full, sb_drained = sem("rest_full"), sem("a_made"), sem("sb_full"), sem("sb_drained")
        mix_hi, mix_lo = sem("mix_hi"), sem("mix_lo")
        x_new = sem("x_new")
        lat_scaled, roped, conv_c, conv_y, sq_y = (sem("lat_scaled"), sem("roped"), sem("conv_c"), sem("conv_y"),
                                                   sem("sq_y"))
        sqs_made = sem("sqs_made")
        group_rsqrt, y2_made = sem("group_rsqrt"), sem("y2_made")
        ffn_gate, ffn_act = sem("ffn_gate"), sem("ffn_act")
        stage_hi, staged = sem("stage_hi"), sem("staged")
        p_hi, p_split, emb_made = sem("p_hi"), sem("p_split"), sem("emb_made")
        pgate_made, out_made = sem("pgate_made"), sem("out_made")

        def full(eng, key):
            kind, n = tiles[key][1]
            eng.wait_ge(tile_full if kind == "tile" else w_used, n)

        def tbank(key):
            return bank[tiles[key][0]]

        def z_tile(i, kb):
            start = 0 if kb == 3 else kb * P
            return bank[3 * (i % 2) + (0, 1, 2, 1)[kb]][:, start:start + S - kb * P]

        block = ctx.enter_context(nc.Block())

        @block.sync
        def _(sp_):
            def load_x(t):
                sp_.dma_start(x[:, t, :], x_d[t * P:(t + 1) * P, :]).then_inc(x_in[t], 16)

            def load(c, first, r):
                if not first:
                    sp_.wait_ge(w_split, c - RAW + 1)
                src = w_d[bass.ds(c, 1), :, :].rearrange("a p c -> p (a c)")
                sp_.dma_start(raw[:, r, :], src).then_inc(raw_in[r], 16)

            for t in range(T):
                load_x(t)
                if 0 < t <= RAW:
                    load(t - 1, True, t - 1)
            with sp_.Fori(1, NCH // RAW) as i:
                for r in range(RAW):
                    load(i * RAW + r, False, r)
            for n in range(2 * T):
                g, t = n // T, n % T
                sp_.wait_ge(out_made, n + 1)
                sp_.dma_start(out_d[t * P:(t + 1) * P, g * 512:(g + 1) * 512],
                              x[:, t, g * 512:(g + 1) * 512]).then_inc(out_stored, 16)
            sp_.wait_ge(out_stored, 2 * T * 16)

        @block.gpsimd
        def _(pool):
            nc.gpsimd.memset(ident[:, :], 0.0).then_inc(masks_made, 1)
            nc.gpsimd.memset(ident_b[:, :], 0.0).then_inc(masks_made, 1)
            nc.gpsimd.memset(mask_le[:, :], 0.0).then_inc(masks_made, 1)
            nc.gpsimd.memset(mask_lt[:, :], 0.0).then_inc(masks_made, 1)
            nc.gpsimd.memset(neg_tri[:, :], -1.0).then_inc(masks_made, 1)
            nc.gpsimd.memset(neg_one[:, :], -1.0).then_inc(masks_made, 1)
            nc.gpsimd.memset(ones[:, :], 1.0).then_inc(masks_made, 1)
            nc.gpsimd.memset(xp, 0.0).then_inc(masks_made, 1)
            pool.wait_ge(masks_made, 8)
            for m in (ident, ident_b):
                nc.gpsimd.affine_select(out=m[:, :], in_=m[:, :], compare_op=ALU.not_equal, fill=1.0, base=0,
                                        pattern=[[-1, P]], channel_multiplier=1).then_inc(masks_made, 1)
            nc.gpsimd.affine_select(out=mask_le[:, :], in_=mask_le[:, :], compare_op=ALU.is_ge, fill=NEG, base=0,
                                    pattern=[[-1, P]], channel_multiplier=1).then_inc(masks_made, 1)
            nc.gpsimd.affine_select(out=mask_lt[:, :], in_=mask_lt[:, :], compare_op=ALU.is_gt, fill=NEG, base=0,
                                    pattern=[[1, P]], channel_multiplier=-1).then_inc(masks_made, 1)
            nc.gpsimd.affine_select(out=neg_tri[:, :], in_=neg_tri[:, :], compare_op=ALU.is_ge, fill=0.0, base=0,
                                    pattern=[[-1, P]], channel_multiplier=1).then_inc(masks_made, 1)

            def split(c, s, shared, first=False):
                r = s % RAW
                if not shared:
                    pool.wait_ge(raw_in[r], (c - r) * (16 // RAW) + 16)
                    if not first:
                        pool.wait_ge(w_used, c - SLOTS + 1)
                    nc.gpsimd.tensor_tensor(w_hi[:, s, :], raw[:, r, :], ones[:, :].broadcast_to([P, CW]),
                                            ALU.mult).then_inc(hi_made, 1)
                    pool.wait_ge(hi_made, c + 1)
                else:
                    pool.wait_ge(hi_shared, c + (1 - SHARED))
                nc.gpsimd.tensor_tensor(w_lo[:, s, :], raw[:, r, :], w_hi[:, s, :].bitcast(F32),
                                        ALU.subtract).then_inc(w_split, 1)

            def splits(a, b, shared):
                while a % SLOTS or a < SLOTS:
                    split(a, a % SLOTS, shared, first=(a < SLOTS))
                    a += 1
                with pool.Fori(a // SLOTS, b // SLOTS) as i:
                    for s in range(SLOTS):
                        split(i * SLOTS + s, s, shared)
                for c in range(b // SLOTS * SLOTS, b):
                    split(c, c % SLOTS, shared)

            splits(0, SHARED, False)
            splits(SHARED, NCH, True)

        @block.tensor
        def _(pe):
            mm = nc.tensor.matmul

            def bank_free(key):
                before = tiles[key][2]
                if before is not None:
                    pe.wait_ge(drained[before[0]], before[1])

            def chunk(c):
                pe.wait_ge(w_split, c + 1)
                return w_hi[:, c % SLOTS, :], w_lo[:, c % SLOTS, :]

            def three(out, st_hi, st_lo, mv_hi, mv_lo, start, stop):
                mm(out, st_hi, mv_hi, start=start, stop=False)
                mm(out, st_hi, mv_lo, start=False, stop=False)
                return mm(out, st_lo, mv_hi, start=False, stop=stop)

            def left(k, t):
                return aT_hi[:, k, t * P:(t + 1) * P], aT_lo[:, k, t * P:(t + 1) * P]

            def weights_moving(keys, chunks, width, k0=0, rows=0, ready=None, late=None, before_last=None):
                def step(n, t, parts):
                    c, ks = chunks[n]
                    hi, lo = parts
                    if n == 0:
                        bank_free(keys[t])
                        if ready:
                            ready(t)
                    for kk, k in enumerate(ks):
                        at = slice(kk * width, (kk + 1) * width)
                        st = left(k0 + k, t)
                        end = n == len(chunks) - 1 and kk == len(ks) - 1
                        last = three(tbank(keys[t])[:, 0:width], st[0], st[1], hi[:, at], lo[:, at],
                                     start=(n == 0 and kk == 0), stop=end)
                    if t == T - 1:
                        last.then_inc(w_used, 1)
                    elif n == len(chunks) - 1:
                        last.then_inc(tile_full, 1)

                whole = len(chunks) - rows
                together = T - 1 if late else T
                for n in range(whole):
                    parts = chunk(chunks[n][0])
                    if late and n == whole - 1:
                        late()
                    for t in range(together):
                        step(n, t, parts)
                if late:
                    for n in range(whole):
                        step(n, T - 1, chunk(chunks[n][0]))
                for t in range(T if rows else 0):
                    if before_last and t == T - 1:
                        before_last()
                    for n in range(whole, len(chunks)):
                        step(n, t, chunk(chunks[n][0]))

            def weights_still(key, c):
                hi, lo = chunk(c)
                bank_free(key)
                for k in range(KD):
                    last = three(tbank(key)[:, :], hi[:, k * P:(k + 1) * P], lo[:, k * P:(k + 1) * P],
                                 aT_hi[:, k, :], aT_lo[:, k, :], start=(k == 0), stop=(k == KD - 1))
                last.then_inc(w_used, 1)

            def turn(out, in_):
                return nc.tensor.transpose(out, in_, ident[:, :])

            def turn_rows(name, src, ready, base, tiles_of=range(T)):
                for n in range(2 * tiles_of[0], 2 * tiles_of[-1] + 2):
                    t, half = n // 2, n % 2
                    if half == 0:
                        pe.wait_ge(ready, base + t + 1)
                    bank_free((name, n))
                    for b in range(4):
                        last = turn(tbank((name, n))[:, b * P:(b + 1) * P], src(t, 4 * half + b))
                    last.then_inc(tile_full, 1)

            def h_tile(t, k):
                return h[:, t % 2, k * P:(k + 1) * P]

            split_tiles = [0]

            def left_row():
                base = split_tiles[0]
                split_tiles[0] += 2 * T
                return lambda t: pe.wait_ge(mix_lo, base + 2 * (t + 1))

            def left_ready(n=2 * T):
                split_tiles[0] += n
                pe.wait_ge(mix_lo, split_tiles[0])

            pairs = [(0, (0, 1)), (1, (2, 3)), (2, (4, 5)), (3, (6, 7))]

            def group4(name):
                return [(CH[name] + i, ks) for i, ks in pairs]

            pe.wait_ge(masks_made, 13)
            turn_rows("h1", h_tile, h_made, 0, range(T - 1))
            weights_moving([("fq", t) for t in range(T)], group4("fq"), S, ready=left_row(),
                           late=lambda: turn_rows("h1", h_tile, h_made, 0, range(T - 1, T)))
            weights_moving([("fv", t) for t in range(T)], group4("fv"), S)

            def turn_heads(name, n, width, src, ready, count):
                pe.wait_ge(ready, count)
                for i in range(n):
                    bank_free((name, i))
                    for t in range(T):
                        last = turn(tbank((name, i))[0:width, t * P:(t + 1) * P], src(t, i))
                    last.then_inc(tile_full, 1)

            turn_heads("qT", FOX_H, HD, lambda t, i: qk_raw[:, t, i * HD:(i + 1) * HD], qk_scaled, 1)
            weights_moving([("fk", t) for t in range(T)], group4("fk"), S)
            weights_moving([("sf", t) for t in range(T)],
                           [(CH["sf"], (0, 1, 2)), (CH["sf"] + 1, (3, 4, 5)), (CH["sf"] + 2, (6, 7))], SF_W)
            for i in range(2):
                weights_still(("pg", i), CH["pg"] + i)
            turn_heads("kT", FOX_H, HD, lambda t, i: qk_raw[:, t, i * HD:(i + 1) * HD], qk_scaled, 2)
            pe.wait_ge(lf_made, 1)
            bank_free(("lfT", 0))
            for t in range(T):
                last = turn(tbank(("lfT", 0))[0:FOX_H, t * P:(t + 1) * P], lf[:, 2, t * FOX_H:(t + 1) * FOX_H])
            last.then_inc(tile_full, 1)
            for name, n in (("px", 2), ("fg", 4)):
                for i in range(n):
                    weights_still((name, i), CH[name] + i)
            for i in range(2):
                pe.wait_ge(pooled_made, i + 1)
                bank_free(("y", i))
                mm(tbank(("y", i))[:, :], wpool[:, i, :], pooled[:, i, :], start=True, stop=True).then_inc(tile_full, 1)
            for i in range(2):
                weights_still(("sg", i), CH["sg"] + i)

            LAG = 3

            def softmax_attention(base, heads, width, qT_, kT_, v_, beside, first=None):
                steps = heads * T

                def scores(m):
                    i, qb = m // T, m % T
                    n = base + m
                    if m >= 3:
                        pe.wait_ge(exped, n - 2)
                    elif first:
                        first(m)
                    out = bank[n % 3]
                    kw = (qb + 1) * P
                    mm(out[:, 0:kw], qT_[0:width, i, qb * P:(qb + 1) * P], kT_[0:width, i, 0:kw], start=True,
                       stop=False)
                    mm(out[:, qb * P:kw], ident_b[:, :], mask_le[:, :], start=False, stop=True).then_inc(scored, 1)

                def turn_probs(m):
                    qb = m % T
                    n = base + m
                    pe.wait_ge(normed, n + 1)
                    if m >= 2:
                        pe.wait_ge(pt_made, n - 1)
                    for kb in range(qb + 1):
                        last = turn(bank[3 + n % 2][:, kb * P:(kb + 1) * P], P_buf[:, n % 4, kb * P:(kb + 1) * P])
                    last.then_inc(turned, 1)

                def values(i):
                    pe.wait_ge(pt_made, base + (i + 1) * T)
                    pair = (base // T + i) // 2
                    if i % 2 == 0 and i >= 4:
                        pe.wait_ge(pv_drained, pair - 1)
                    r0 = (i % 2) * HD
                    for kb in range(T):
                        last = mm(bank[6 + pair % 2][r0:r0 + HD, kb * P:S], v_[:, kb, i * HD:(i + 1) * HD],
                                  PT[:, i % 2, kb, kb * P:S], start=(kb == 0), stop=(kb == T - 1),
                                  skip_group_check=True)
                    last.then_inc(pv_done, 1)

                for m in range(steps + LAG + 1):
                    if m < steps:
                        scores(m)
                    if LAG <= m < steps + LAG:
                        turn_probs(m - LAG)
                    if m < steps:
                        beside(m)
                    done = m - LAG - 1
                    if done >= 0 and done % T == T - 1:
                        values(done // T)

            def sqk_piece(m):
                key = (("sq", 0), ("sq", 1), ("sk", 0), ("sk", 1))[m // KD]
                k = m % KD
                hi, lo = chunk(CH["sq"] + m // KD)
                if k == 0:
                    bank_free(key)
                last = three(tbank(key)[:, :], hi[:, k * P:(k + 1) * P], lo[:, k * P:(k + 1) * P], aT_hi[:, k, :],
                             aT_lo[:, k, :], start=(k == 0), stop=(k == KD - 1))
                if k == KD - 1:
                    last.then_inc(w_used, 1)

            pe.wait_ge(drained["act"], tiles["sg", 1][3][1])
            pe.wait_ge(drained["dve"], tiles["y", 1][3][1])
            pe.wait_ge(c_rows_in, 32)
            softmax_attention(0, FOX_H, HD + 2, q_aug, k_aug, fv, sqk_piece)

            pe.wait_ge(exped, FOX_H * T)
            pe.wait_ge(pt_made, FOX_H * T)
            pe.wait_ge(drained["act"], tiles["sk", 1][3][1])

            def z_scores(i):
                for n, kb in enumerate(SB_ORDER):
                    if i >= 2:
                        pe.wait_ge(a_made, (i - 2) * T + (3 if kb in (1, 3) else n + 1))
                    r0, j = (i % 2) * HD, i // 2
                    out = z_tile(i, kb)
                    mm(out, skT[r0:r0 + HD, j, kb * P:(kb + 1) * P], sqT[r0:r0 + HD, j, kb * P:S],
                       start=(kb != 3), stop=False, skip_group_check=True)
                    mm(out[:, 0:P], ident_b[:, :], mask_lt[:, :], start=False, stop=True,
                       skip_group_check=True).then_inc(z_full, 1)

            def rest(i):
                pe.wait_ge(sp_made, (i + 1) * T)
                for kb in SB_ORDER:
                    for jb in range(kb, T):
                        last = mm(z_tile(i, kb)[:, (jb - kb) * P:], (neg_tri if jb == kb else neg_one)[:, :],
                                  sp[i % 2][:, jb, jb * P:S], start=False, stop=(jb == T - 1),
                                  skip_group_check=True)
                    last.then_inc(rest_full, 1)

            def sb_values(i):
                pe.wait_ge(a_made, (i + 1) * T)
                if i == 0:
                    pe.wait_ge(pv_drained, FOX_H // 2)
                if i == 2:
                    pe.wait_ge(sb_drained, 1)
                r0 = (i % 2) * HD
                for kb in range(T):
                    last = mm(bank[6][r0:r0 + HD, kb * P:S], sf[:, kb, i * HD:(i + 1) * HD],
                              az[i % 2][:, kb, kb * P:S], start=(kb == 0), stop=(kb == T - 1),
                              skip_group_check=True)
                last.then_inc(sb_full, 1)

            def out1_step(key, t, n, ks, start, end):
                hi, lo = chunk(CH["out1"] + n)
                if start:
                    bank_free((key, t))
                for kk, k in enumerate(ks):
                    st = left(k, t)
                    at = slice(kk * S, (kk + 1) * S)
                    last = three(tbank((key, t))[:, :], st[0], st[1], hi[:, at], lo[:, at], start=(start and kk == 0),
                                 stop=(end and kk == len(ks) - 1))
                if t == T - 1:
                    last.then_inc(w_used, 1)
                elif end:
                    last.then_inc(tile_full, 1)

            def out1_beside(t):
                if t == 0:
                    left_ready(6)
                    pe.wait_ge(pv_drained, FOX_H // 2)
                for n in range(3):
                    out1_step("out1a", t, n, pairs[n][1], n == 0, n == 2)

            z_scores(0)
            z_scores(1)
            rest(0)
            out1_beside(0)
            z_scores(2)
            sb_values(0)
            rest(1)
            out1_beside(1)
            z_scores(3)
            sb_values(1)
            rest(2)
            rest(3)
            out1_beside(2)
            sb_values(2)
            sb_values(3)
            out1_beside(3)

            pe.wait_ge(a_made, SB_H * T)
            for n in range(2):
                for t in range(T):
                    out1_step("out1c", t, 3 + n, pairs[n][1], n == 0, False)
            left_ready(2)
            pe.wait_ge(sb_drained, SB_H // 2)
            for t in range(T):
                if t == T - 1:
                    turn_rows("h2", h_tile, h_made, T, range(0, 1))
                out1_step("out1c", t, 5, pairs[2][1], False, False)
                out1_step("out1b", t, 6, pairs[3][1], True, True)
                out1_step("out1c", t, 7, pairs[3][1], False, True)

            turn_rows("h2", h_tile, h_made, T, range(1, T - 1))
            weights_moving([("lq", t) for t in range(T)],
                           [(CH["lq"], (0, 1, 2)), (CH["lq"] + 1, (3, 4, 5)), (CH["lq"] + 2, (6, 7))], LQ_W,
                           ready=left_row(), late=lambda: turn_rows("h2", h_tile, h_made, T, range(T - 1, T)))
            weights_moving([("lkv", t) for t in range(T)],
                           [(CH["lkv"], (0, 1, 2, 3)), (CH["lkv"] + 1, (4, 5, 6, 7))], RANK)
            for j in range(4):
                for i, name in enumerate(("c", "xv", "b")):
                    weights_still((name, j), CH["conv"] + 3 * j + i)
            pe.wait_ge(lat_scaled, 1)
            for i in range(4):
                bank_free(("latT", i))
                src = lat_q if i < 2 else lat_kv
                for t in range(T):
                    last = turn(tbank(("latT", i))[:, t * P:(t + 1) * P], src[:, t, (i % 2) * P:(i % 2 + 1) * P])
                last.then_inc(tile_full, 1)
            pe.wait_ge(roped, 1)
            bank_free(("krT", 0))
            for t in range(T):
                last = turn(tbank(("krT", 0))[0:ROPE, t * P:(t + 1) * P], lat_q[:, t, RANK:LQ_W])
            last.then_inc(tile_full, 1)
            for k in range(2):
                left_ready(1)
                hi, lo = chunk(CH["uq"] + k)
                for t in range(T):
                    for g in range(2):
                        key = ("uq", t, g)
                        if k == 0:
                            bank_free(key)
                        st = left(k, t)
                        w = UQ_W // 2
                        last = three(tbank(key)[:, 0:w], st[0], st[1], hi[:, g * w:(g + 1) * w],
                                     lo[:, g * w:(g + 1) * w], start=(k == 0), stop=(k == 1))
                        if (t, g) == (T - 1, 1):
                            last.then_inc(w_used, 1)
                        elif k == 1:
                            last.then_inc(tile_full, 1)
            left_ready(2)
            hi, lo = chunk(CH["uk"])
            for i in range(4):
                bank_free(("uk", i))
                for k in range(2):
                    at = slice(k * 512 + i * P, k * 512 + (i + 1) * P)
                    last = three(tbank(("uk", i))[:, :], hi[:, at], lo[:, at], aT_hi[:, 2 + k, :], aT_lo[:, 2 + k, :],
                                 start=(k == 0), stop=(k == 1))
                last.then_inc(w_used if i == 3 else tile_full, 1)
            pe.wait_ge(sqs_made, 1)
            bank_free(("ssc", 0))
            for t in range(T):
                last = mm(tbank(("ssc", 0))[:, t:t + 1], sqs[:, 1, t * P:(t + 1) * P], ones[:, :], start=True,
                          stop=True)
            last.then_inc(tile_full, 1)
            weights_moving([("uv", t) for t in range(T)], [(CH["uv"], (0, 1))], S, k0=2)
            turn_heads("q2T", MLA_H, QK2, lambda t, i: q2[:, t, i * QK2:(i + 1) * QK2], roped, 2)

            left_ready(4)

            def out2c_piece(m):
                g, t, kk = m // 16, m // 4 % 4, m % 4
                key = ("out2c", g, t)
                hi, lo = chunk(CH["out2c"] + 2 * g + kk // 2)
                if kk == 0:
                    bank_free(key)
                st = left(4 + kk, t)
                at = slice(kk % 2 * 512, (kk % 2 + 1) * 512)
                last = three(tbank(key)[:, :], st[0], st[1], hi[:, at], lo[:, at], start=(kk == 0), stop=(kk == 3))
                if t == T - 1 and kk % 2:
                    last.then_inc(w_used, 1)
                elif kk == 3:
                    last.then_inc(tile_full, 1)

            softmax_attention(FOX_H * T, MLA_H, QK2, q2T, k2T, v2, out2c_piece,
                              first=lambda m: pe.wait_ge(drained["act"], tiles["q2T", m][3][1]))
            pe.wait_ge(exped, (FOX_H + MLA_H) * T)
            pe.wait_ge(pt_made, (FOX_H + MLA_H) * T)
            left_ready(3)

            def out2a_block(t, g, k):
                key = ("out2a", t, g)
                if k == 0:
                    bank_free(key)
                hi, lo = chunk(CH["out2a"] + 2 * g + k // 2)
                st = left(k, t)
                at = slice(k % 2 * 512, (k % 2 + 1) * 512)
                last = three(tbank(key)[:, :], st[0], st[1], hi[:, at], lo[:, at], start=(k == 0), stop=(k == 3))
                if t == T - 1 and k % 2:
                    last.then_inc(w_used, 1)
                elif k == 3:
                    last.then_inc(tile_full, 1)

            for k in range(4):
                if k == 3:
                    left_ready(1)
                    pe.wait_ge(pv_drained, (FOX_H + MLA_H) // 2)
                for g in range(2):
                    out2a_block(0, g, k)
            for t in range(T):
                for g in range(2 if t > 0 else 0):
                    for k in range(4):
                        out2a_block(t, g, k)
                if t == 0:
                    pe.wait_ge(sqs_made, 2)
                    for b in range(T):
                        last = mm(tbank(("ssa", 0))[:, b:b + 1], sqs[:, 0, b * P:(b + 1) * P], ones[:, :],
                                  start=True, stop=True)
                    last.then_inc(tile_full, 1)
            pe.wait_ge(p_split, 2)
            for t in range(T):
                for g in range(2):
                    hi, lo = chunk(CH["ple"] + g)
                    bank_free(("ple", g, t))
                    for k in range(2):
                        st = left(4 + k, t)
                        at = slice(k * S, (k + 1) * S)
                        last = three(tbank(("ple", g, t))[:, :], st[0], st[1], hi[:, at], lo[:, at], start=(k == 0),
                                     stop=(k == 1))
                    last.then_inc(w_used if t == T - 1 else tile_full, 1)
                if t < 2:
                    turn_rows("h3", h_tile, h_made, 2 * T, range(t, t + 1))

            h3_row = left_row()
            pe.wait_ge(drained["act"], tiles["ple", 1, T - 1][3][1])

            def ffn_first():
                for half in range(2):
                    cols_of = slice(half * 256, (half + 1) * 256)
                    for b in range(4):
                        hi, lo = chunk(CH["ffn"] + b)
                        if b == 0:
                            h3_row(2 * half + 1)
                        if half == 0 and b >= 2:
                            turn_rows("h3", h_tile, h_made, 2 * T, range(b, b + 1))
                        for k in range(KD):
                            at = slice(k * P, (k + 1) * P)
                            last = three(bank[b][:, cols_of], hi[:, at], lo[:, at], aT_hi[:, k, cols_of],
                                         aT_lo[:, k, cols_of], start=(k == 0), stop=(k == KD - 1))
                        if half:
                            last.then_inc(w_used, 1)

            def ffn_block(f, c):
                for b in range(4):
                    s = (CH["ffn"] + b) % SLOTS
                    pe.wait_ge(w_split, c + b + 1)
                    if b % 2 == 0:
                        pe.wait_ge(ffn_act, f + b // 2 - 1)
                    for k in range(KD):
                        at = slice(k * P, (k + 1) * P)
                        last = three(bank[b][:, :], w_hi[:, s, at], w_lo[:, s, at], aT_hi[:, k, :], aT_lo[:, k, :],
                                     start=(k == 0), stop=(k == KD - 1))
                    last.then_inc(w_used, 1)

            ffn_first()
            with pe.Fori(1, NF // 2) as i:
                ffn_block(i * 2, i * 4 + CH["ffn"])

            def down_step(t, slot, first=False, end=False):
                s = (CH["down"] + slot) % SLOTS
                for g in range(2):
                    at = slice(g * 512, (g + 1) * 512)
                    last = three(bank[2 * t + g][:, :], aT_hi[:, slot, t * P:(t + 1) * P],
                                 aT_lo[:, slot, t * P:(t + 1) * P], w_hi[:, s, at], w_lo[:, s, at], start=first,
                                 stop=end)
                    if t == T - 1 and g == 1:
                        last.then_inc(w_used, 1)
                    elif end:
                        last.then_inc(tile_full, 1)

            def down_block(k, slot, first=False):
                pe.wait_ge(staged, k + 1)
                pe.wait_ge(w_split, k + (CH["down"] + 1))
                for t in range(T):
                    down_step(t, slot, first)

            pe.wait_ge(ffn_act, NF)
            for k in range(4):
                down_block(k, k, k == 0)
            rounds = (NF - 4) // 4
            with pe.Fori(1, rounds) as i:
                for j in range(4):
                    down_block(i * 4 + j, j)
            for k in range(4 * rounds, NF - 4):
                down_block(k, k % 4)

            def turn_x(tiles_of):
                turn_rows("xT", lambda t, k: x[:, t, k * P:(k + 1) * P], x_new, 4 * T, tiles_of)

            for t in range(T):
                for k in range(NF - 4, NF):
                    if t == 0:
                        pe.wait_ge(staged, k + 1)
                        pe.wait_ge(w_split, k + CH["down"] + 1)
                    down_step(t, k % 4, end=(k == NF - 1))
                if t == T - 2:
                    turn_x(range(0, 1))

            turn_x(range(1, T - 1))
            weights_moving([("pgate", 0, t) for t in range(T)], group4("pgate"), S, ready=left_row(),
                           late=lambda: turn_x(range(T - 1, T)))
            weights_moving([("pgate", 1, t) for t in range(T)],
                           [(CH["pgate"] + 4 + i, ks) for i, ks in pairs], S, rows=3)

        @block.scalar
        def _(act_):
            A = nc.scalar.activation
            steps, rsq, order, sq = [0], [0], [0], [0]
            junk = PTf[:, 3072:4096]

            def own(ins):
                steps[0] += 1
                ins.then_inc(act_step, 1)
                act_.wait_ge(act_step, steps[0])

            def drain(key, ins):
                order[0] += 1
                assert tiles[key][3] == ("act", order[0]), key
                ins.then_inc(drained["act"], 1)

            def copy(out, in_, scale=1.0):
                return A(out, in_, ACT.Copy, scale=scale)

            def rsqrt(at):
                rsq[0] += 1
                act_.wait_ge(ms_made, rsq[0])
                own(A(stat[:, 2, at], stat[:, 1, at], ACT.Ln))
                A(stat[:, 2, at], stat[:, 2, at], ACT.Exp, scale=-0.5).then_inc(rs_made, 1)

            def squares(in_, at):
                if sq[0]:
                    act_.wait_ge(sq_done, sq[0])
                sq[0] += 1
                A(junk[:, 0:in_.shape[-1]], in_, ACT.Square, accum_out=stat[:, 0, at:at + 1]).then_inc(sq_done, 1)

            def split_hi(out, in_, scale=1.0):
                copy(out, in_, scale).then_inc(mix_hi, 1)

            def norm_rows(name, ready, at0):
                for t in range(T + 1):
                    if t < T:
                        ready(t)
                        squares(x[:, t, :], at0 + t)
                    if t > 0:
                        rsqrt(slice(at0 + t - 1, at0 + t))
                    if t > 1:
                        turned_hi(name, range(t - 2, t - 1))
                turned_hi(name, range(T - 1, T))

            def turned_hi(name, tiles_of=range(T)):
                for n in range(2 * tiles_of[0], 2 * tiles_of[-1] + 2):
                    t, half = n // 2, n % 2
                    full(act_, (name, n))
                    split_hi(aT_hi[:, 4 * half:4 * half + 4, t * P:(t + 1) * P],
                             tbank((name, n))[:, :].rearrange("p (a b) -> p a b", b=P))

            act_.dma_start(g_pre[:, :], gains_d[0, :, :]).then_inc(g_pre_in, 16)
            act_.dma_start(cols[:, :], cols_d).then_inc(const_in, 16)
            act_.dma_start(wpool[:, :, :], wpool_d).then_inc(const_in, 16)
            act_.dma_start(pos_i[:, :], pos_d).then_inc(const_in, 16)

            nc.scalar.preload_act_table_set(LOG_EXP)
            norm_rows("h1", lambda t: act_.wait_ge(x_in[t], 16), 0)

            def qk_rows(name, base):
                for t in range(T):
                    if base and t == 0:
                        act_.wait_ge(tile_full, tiles["qT", FOX_H - 1][1][1])
                    full(act_, (name, t))
                    copy(qk_raw[:, t, :], tbank((name, t))[:, :]).then_inc(act_step, 1)
                    steps[0] += 1
                    n = base + t
                    if n >= 2:
                        act_.wait_ge(qk_reduced, n - 1)
                    A(sq_tmp[:, n % 2, :], tbank((name, t))[:, :], ACT.Square).then_inc(qk_squared, 1)
                    act_.wait_ge(qk_squared, n + 1)
                    order[0] += 1
                    nc.scalar.sem_inc(drained["act"], 1)

            def heads_out(name, n, width, dst, scale=None):
                for i in range(n):
                    full(act_, (name, i))
                    drain((name, i), copy(dst[0:width, i, :], tbank((name, i))[0:width, :],
                                          1.0 if scale is None else scale))

            act_.wait_ge(const_in, 48)
            qk_rows("fq", 0)
            act_.dma_start(g_post[:, :], gains_d[3, :, :]).then_inc(g_post_in, 16)
            rsqrt(slice(16, 48))
            for t in range(T):
                full(act_, ("fv", t))
                drain(("fv", t), copy(fv[:, t, :], tbank(("fv", t))[:, :]))
            heads_out("qT", FOX_H, HD, q_aug, col("gq")[0:HD])
            qk_rows("fk", T)
            rsqrt(slice(16, 48))
            for t in range(T):
                full(act_, ("sf", t))
                drain(("sf", t), copy(sf[:, t, :], tbank(("sf", t))[:, 0:SF_W]))
            act_.wait_ge(lf_abs, 1)
            own(A(lf[:, 1, :], lf[:, 1, :], ACT.Exp, scale=-1.0))
            A(lf[:, 1, :], lf[:, 1, :], ACT.Ln, bias=1.0).then_inc(lf_exp, 1)
            act_.wait_ge(angles, 1)
            A(cs[:, 0, :, :], cs[:, 0, :, :], ACT.Sin).then_inc(sines, 1)
            A(cs[:, 1, :, :], cs[:, 1, :, :], ACT.Sin).then_inc(sines, 1)

            def gate_rows(name, n, b0):
                for i in range(n):
                    full(act_, (name, i))
                    drain((name, i), A(gate[:, b0 + i, :], tbank((name, i))[:, :], ACT.Silu))

            gate_rows("pg", 2, 4)
            heads_out("kT", FOX_H, HD, k_aug, col("gk")[0:HD])
            gate_rows("fg", 4, 0)
            act_.wait_ge(rows_laid, 2)
            act_.wait_ge(cum_made, 1)
            act_.dma_start(q_aug[HD:HD + 1, :, :], cum[:, 0, :]).then_inc(c_rows_in, 16)
            act_.dma_start(k_aug[HD + 1:HD + 2, :, :], cum[:, 1, :]).then_inc(c_rows_in, 16)
            gate_rows("sg", 2, 6)

            def softmax_attention(base, heads, pair_out, beside):
                steps_ = heads * T
                for m in range(steps_ + 3):
                    beside(m)
                    if m < steps_:
                        n = base + m
                        kw = (m % T + 1) * P
                        act_.wait_ge(maxed, n + 1)
                        if m >= 4:
                            act_.wait_ge(turned, n - 3)
                        A(P_buf[:, n % 4, 0:kw], bank[n % 3][:, 0:kw], ACT.Exp, bias=negmax[:, n % 8:n % 8 + 1],
                          accum_out=esum[:, n % 8:n % 8 + 1]).then_inc(exped, 1)
                    if m >= 3:
                        n, i, qb = base + m - 3, (m - 3) // T, (m - 3) % T
                        act_.wait_ge(turned, n + 1)
                        if qb == 0 and i >= 2:
                            act_.wait_ge(pv_done, base // T + i - 1)
                        copy(PT[:, i % 2, 0:qb + 1, qb * P:(qb + 1) * P],
                             bank[3 + n % 2][:, 0:(qb + 1) * P].rearrange("p (a b) -> p a b", b=P))\
                            .then_inc(pt_made, 1)
                        if pair_out is not None and qb == 1 and i >= 2 and i % 2 == 0:
                            pair_out(i // 2 - 1)
                if pair_out is not None:
                    pair_out(heads // 2 - 1)

            nc.scalar.preload_act_table_set(LOG_EXP)
            act_.wait_ge(pooled_made, 2)
            act_.wait_ge(tile_full, tiles["y", 1][1][1])

            def sqk_out(m):
                if m % KD == 0 and 0 < m <= 4 * KD:
                    i = m // KD - 1
                    key = ("sq" if i < 2 else "sk", i % 2)
                    full(act_, key)
                    drain(key, copy((sqT if i < 2 else skT)[:, i % 2, :], tbank(key)[:, :],
                                    HD ** -0.5 if i < 2 else 1.0))

            softmax_attention(0, FOX_H, None, sqk_out)

            act_.wait_ge(pv_done, FOX_H)

            def sb_logs(i):
                for n, kb in enumerate(SB_ORDER, i * T):
                    e = ea[i % 2][:, kb, kb * P:S]
                    act_.wait_ge(z_abs, n + 1)
                    own(A(e, e, ACT.Exp))
                    A(e, e, ACT.Ln, bias=1.0).then_inc(z_ln, 1)

            def sb_weights(i):
                for n, kb in enumerate(SB_ORDER, i * T):
                    act_.wait_ge(rest_full, n + (2 if kb == 1 else 1))
                    if kb == 0 and i >= 2:
                        act_.wait_ge(sb_full, i - 1)
                    A(az[i % 2][:, kb, kb * P:S], z_tile(i, kb), ACT.Exp).then_inc(a_made, 1)

            def mix_high(blocks):
                for b in blocks:
                    split_hi(aT_hi[:, b, :], gate[:, b, :])

            sb_logs(0)
            act_.wait_ge(gated, 1)
            act_.wait_ge(w_used, CH["sk"] + 2)
            mix_high(range(6))
            sb_logs(1)
            for i in range(SB_H):
                sb_weights(i)
                if i + 2 < SB_H:
                    sb_logs(i + 2)
            act_.wait_ge(gated, 2)
            mix_high(range(6, KD))

            act_.wait_ge(h_made, T)
            act_.dma_start(g_pre[:, :], gains_d[1, :, :]).then_inc(g_pre_in, 16)
            norm_rows("h2", lambda t: act_.wait_ge(x_new, T + 2 * (t + 1)), 4)
            for name, dst, w, at0 in (("lq", lat_q, LQ_W, 48), ("lkv", lat_kv, RANK, 52)):
                for t in range(T):
                    full(act_, (name, t))
                    own(copy(dst[:, t, :], tbank((name, t))[:, 0:w]))
                    drain((name, t), A(PTf[:, 3072:3072 + RANK], tbank((name, t))[:, 0:RANK], ACT.Square,
                                       accum_out=stat[:, 0, at0 + t:at0 + t + 1]))
            rsqrt(slice(48, 56))
            for j in range(4):
                full(act_, ("c", j))
                if j >= 2:
                    act_.wait_ge(conv_y, j - 1)
                drain(("c", j), copy(u[:, j % 2, KERNEL - 1:], tbank(("c", j))[:, :]))
                act_.wait_ge(conv_y, j + 1)
                A(sqs[:, 1, :] if j == 0 else sq2[:, j % 2, :], y[:, j, :], ACT.Square).then_inc(sq_y, 1)
            for i in range(4):
                full(act_, ("latT", i))
                split_hi(aT_hi[:, i, :], tbank(("latT", i))[:, :], col("gq2", i) if i < 2 else col("gkv2", i - 2))
            full(act_, ("krT", 0))
            own(copy(k2T[HD:QK2, 0, :], tbank(("krT", 0))[0:ROPE, :]))
            order[0] += 1
            assert tiles["krT", 0][3] == ("act", order[0])
            nc.scalar.sem_inc(drained["act"], 1)
            act_.wait_ge(w_used, CH["conv"] + 12)
            for j in range(4):
                split_hi(aT_hi[:, 4 + j, :], y[:, j, :], col("gc", j))
            for t in range(T):
                for g in range(2):
                    full(act_, ("uq", t, g))
                    drain(("uq", t, g), copy(q2[:, t, g * 384:(g + 1) * 384], tbank(("uq", t, g))[:, 0:384],
                                             QK2 ** -0.5))
            own(copy(k2T[HD:QK2, 1:, :], k2T[HD:QK2, 0:1, :].broadcast_to([ROPE, MLA_H - 1, S])))
            for i in range(4):
                full(act_, ("uk", i))
                own(copy(k2T[0:HD, 2 * i, :], tbank(("uk", i))[0:HD, :]))
                drain(("uk", i), copy(k2T[0:HD, 2 * i + 1, :], tbank(("uk", i))[HD:P, :]))
            rsqrt(slice(60, 64))
            for t in range(T):
                full(act_, ("uv", t))
                drain(("uv", t), copy(v2[:, t, :], tbank(("uv", t))[:, :]))
            heads_out("q2T", MLA_H, QK2, q2T)

            def pair_out(pair):
                act_.wait_ge(pv_done, FOX_H + 2 * pair + 2)
                out = bank[6 + pair % 2][:, :]
                split_hi(aT_hi[:, pair, :], out, col("ga", pair))
                A(sqs[:, 0, :] if pair == 0 else sq2[:, pair % 2, :], out, ACT.Square).then_inc(sq_y, 1)

            def out2c_out(m):
                if m % 4 == 0 and 0 < m <= 32:
                    g, t = (m // 4 - 1) // T, (m // 4 - 1) % T
                    if m == 4:
                        act_.wait_ge(group_rsqrt, 1)
                    full(act_, ("out2c", g, t))
                    drain(("out2c", g, t), copy(y2[t][:, g * 512:(g + 1) * 512], tbank(("out2c", g, t))[:, :],
                                                stat[:, 3, 60 + t:61 + t]))

            act_.wait_ge(mix_lo, 4 * T + KD + 8)
            act_.dma_start(pe_raw, pt_d).then_inc(pt_in, 16)
            softmax_attention(FOX_H * T, MLA_H, pair_out, out2c_out)
            act_.wait_ge(h_made, 2 * T)
            act_.dma_start(g_pre[:, :], gains_d[2, :, :]).then_inc(g_pre_in, 16)
            rsqrt(slice(56, 60))

            act_.wait_ge(pt_in, 16)
            act_.wait_ge(w_used, CH["out2c"] + 4)
            for k in range(2):
                copy(aT_hi[:, 4 + k, :], pe_raw[:, k, :]).then_inc(p_hi, 1)

            def weights_hi(c, s, used=None):
                act_.wait_ge(raw_in[s % RAW], (c - s % RAW) * (16 // RAW) + 16)
                if used is not None:
                    act_.wait_ge(w_used, used)
                copy(w_hi[:, s, :], raw[:, s % RAW, :]).then_inc(hi_shared, 1)

            def next_hi(c):
                weights_hi(c, c % SLOTS, used=c - 3)

            def ple_out(t):
                for g in range(2):
                    full(act_, ("ple", g, t))
                    drain(("ple", g, t), copy(emb[:, t, g * 512:(g + 1) * 512], tbank(("ple", g, t))[:, :]))

            def squares_x(t):
                act_.wait_ge(x_new, 3 * T + t + 1)
                squares(x[:, t, :], 9 + 2 * (t + 1))

            def squares_y(t):
                act_.wait_ge(y2_made, 2 * (t + 1))
                squares(y2[t], 8 + 2 * t)

            squares_y(0)
            rsqrt(slice(8, 9))
            squares_x(0)
            squares_y(1)
            rsqrt(slice(10, 12))
            next_hi(CH["ple"])
            next_hi(CH["ple"] + 1)
            squares_x(1)
            squares_y(2)
            rsqrt(slice(12, 14))
            next_hi(CH["ffn"])
            ple_out(0)
            turned_hi("h3", range(0, 1))
            next_hi(CH["ffn"] + 1)
            squares_x(2)
            ple_out(1)
            squares_y(3)
            turned_hi("h3", range(1, 2))
            rsqrt(slice(14, 16))
            ple_out(2)
            ple_out(3)
            next_hi(CH["ffn"] + 2)
            next_hi(CH["ffn"] + 3)
            squares_x(3)
            rsqrt(slice(17, 18))
            turned_hi("h3", range(2, T))

            act_.wait_ge(x_new, 4 * T)
            act_.dma_start(g_post[:, :], gains_d[5, :, :]).then_inc(g_post_in, 16)
            for t in range(T):
                squares(emb[:, t, :], 40 + t)
            rsqrt(slice(40, 44))
            def ffn_silu(f, slot, c, first):
                if not (first and slot == 0):
                    weights_hi(c + 3, (CH["ffn"] + 2 * slot + 3) % SLOTS, used=c)
                act_.wait_ge(w_used, c + 1)
                weights_hi(c + 4, (CH["ffn"] + 2 * slot + 4) % SLOTS)
                if not first:
                    act_.wait_ge(ffn_act, f - 1)
                A(sg_t[:, slot, :], bank[2 * slot][:, :], ACT.Silu).then_inc(ffn_gate, 1)

            for f in range(2):
                ffn_silu(f, f, CH["ffn"] + 2 * f, True)
            act_.wait_ge(emb_made, 1)
            act_.dma_start(g_post[:, :], gains_d[4, :, :]).then_inc(g_post_in, 16)
            with act_.Fori(1, NF // 2) as i:
                for f in range(2):
                    ffn_silu(i * 2 + f, f, i * 4 + (CH["ffn"] + 2 * f), False)

            def stage(k, slot, used):
                act_.wait_ge(w_used, used)
                copy(aT_hi[:, slot, :].unsqueeze(1), act[:, bass.ds(k, 1), :]).then_inc(stage_hi, 1)

            def down_weights(k, slot):
                c = k + (CH["down"] + 3)
                weights_hi(c, (CH["down"] + 3 + slot) % SLOTS, used=c - 3)

            act_.wait_ge(ffn_act, NF)
            for k in range(4):
                stage(k, k, CH["down"])
            for k in range(4):
                down_weights(k, k)
            rounds = (NF - 4) // 4
            with act_.Fori(1, rounds) as i:
                for j in range(4):
                    stage(i * 4 + j, j, i * 4 + (CH["down"] + j - 3))
                    down_weights(i * 4 + j, j)
            for k in range(4 * rounds, NF - 3):
                stage(k, k % 4, CH["down"] + k - 3)
                down_weights(k, k % 4)
            for k in range(NF - 3, NF):
                stage(k, k % 4, CH["down"] + k - 3)

            nc.scalar.preload_act_table_set(LOG_EXP)
            for t in range(T):
                if t == T - 1:
                    turned_hi("xT", range(0, 1))
                    for k in range(NF - 3, NF - 1):
                        down_weights(k, k % 4)
                for g in range(2):
                    full(act_, ("down", t, g))
                    squares(tbank(("down", t, g))[:, :], 16 + 2 * t + g)
                if t == T - 1:
                    turned_hi("xT", range(1, 2))
                rsqrt(slice(24 + t, 25 + t))
            turned_hi("xT", range(2, T - 1))
            for k in range(NF - 1, NF + 1):
                down_weights(k, k % 4)
            turned_hi("xT", range(T - 1, T))
            for g in range(2):
                for t in range(T):
                    n = g * T + t
                    if (g, t) == (0, T - 1):
                        for k in range(NF + 1, NF + 4):
                            down_weights(k, k % 4)
                    full(act_, ("pgate", g, t))
                    if n >= 2:
                        act_.wait_ge(out_made, n - 1)
                    A(gate_t[:, n % 2, :], tbank(("pgate", g, t))[:, :], ACT.Sigmoid).then_inc(pgate_made, 1)
                    if (g, t) == (0, T - 1):
                        down_weights(NF + 4, (NF + 4) % 4)

        @block.vector
        def _(dve):
            V = nc.vector
            steps, rsq, order, lows, sqn, hn, xn = [0], [0], [0], [0], [0], [0], [0]

            def own(ins):
                steps[0] += 1
                ins.then_inc(dve_step, 1)
                dve.wait_ge(dve_step, steps[0])

            def drain(key, ins):
                order[0] += 1
                assert tiles[key][3] == ("dve", order[0]), (key, order[0])
                ins.then_inc(drained["dve"], 1)

            def stt(out, in0, scalar, in1, op0, op1):
                return V.scalar_tensor_tensor(out=out, in0=in0, scalar=scalar, in1=in1, op0=op0, op1=op1)

            def rsqrt(at, width, ss=None):
                rsq[0] += 1
                V.tensor_scalar(stat[:, 1, at], stat[:, 0, at] if ss is None else ss, 1.0 / width, EPS, ALU.mult,
                                ALU.add).then_inc(ms_made, 1)
                dve.wait_ge(rs_made, rsq[0])
                own(V.tensor_tensor(stat[:, 3, at], stat[:, 2, at], stat[:, 2, at], ALU.mult))
                own(stt(stat[:, 3, at], stat[:, 3, at], -0.5, stat[:, 1, at], ALU.mult, ALU.mult))
                own(stt(stat[:, 3, at], stat[:, 3, at], 1.5, stat[:, 2, at], ALU.add, ALU.mult))

            def split_lo(key, out, in_, hi, scale=None):
                lows[0] += 1
                dve.wait_ge(mix_hi, lows[0])
                if scale is None:
                    ins = V.tensor_tensor(out, in_, hi, ALU.subtract)
                else:
                    ins = stt(out, in_, scale, hi, ALU.mult, ALU.subtract)
                ins.then_inc(mix_lo, 1)
                if key is not None:
                    order[0] += 1
                    assert tiles[key][3] == ("dve", order[0]), key
                    dve.wait_ge(mix_lo, lows[0])
                    V.sem_inc(drained["dve"], 1)

            def norm_row(name, at0, t):
                sqn[0] += 1
                dve.wait_ge(sq_done, sqn[0])
                rsqrt(slice(at0 + t, at0 + t + 1), D)
                if t >= 2:
                    full(dve, (name, 2 * (t - 2) + 1))
                stt(h[:, t % 2, :], x[:, t, :], stat[:, 3, at0 + t:at0 + t + 1], g_pre[:, :], ALU.mult,
                    ALU.mult).then_inc(h_made, 1)

            def turned_lo(name, tiles_of=range(T)):
                for n in range(2 * tiles_of[0], 2 * tiles_of[-1] + 2):
                    t, half = n // 2, n % 2
                    at = (slice(None), slice(4 * half, 4 * half + 4), slice(t * P, (t + 1) * P))
                    split_lo((name, n), aT_lo[at], tbank((name, n))[:, :].rearrange("p (a b) -> p a b", b=P),
                             aT_hi[at].bitcast(F32))

            dve.wait_ge(g_pre_in, 16)
            for t in range(T):
                norm_row("h1", 0, t)
                if t > 0:
                    turned_lo("h1", range(t - 1, t))
            turned_lo("h1", range(T - 1, T))
            dve.wait_ge(const_in, 48)
            own(V.tensor_copy(pos_f[:, :], pos_i[:, :]))
            for t in range(T):
                own(V.tensor_scalar(cs[:, 0, t, :], col("invf", 0, HALF), pos_f[:, t:t + 1], None, ALU.mult))
            ang = cs[:, 0, :, :].rearrange("p a b -> p (a b)")
            trn = cs[:, 1, :, :].rearrange("p a b -> p (a b)")
            own(V.tensor_scalar(trn, ang, float(1 / (2 * np.pi)), ROUND, ALU.mult, ALU.add))
            own(V.tensor_scalar(trn, trn, -ROUND, None, ALU.add))
            for part in (PI_A, PI_B, PI_C):
                own(stt(ang, trn, -part, ang, ALU.mult, ALU.add))
            own(V.tensor_scalar(ang, ang, 3.1415925, -3.1415925, ALU.min, ALU.max))
            own(stt(trn, ang, -1.0, ang, ALU.mult, ALU.max))
            V.tensor_scalar(trn, trn, -1.0, float(np.pi / 2), ALU.mult, ALU.add).then_inc(angles, 1)

            own(V.tensor_scalar(col("gq"), col("gq"), HD ** -0.5, None, ALU.mult))
            V.memset(q_aug[HD:HD + 2, :, :], 1.0).then_inc(rows_laid, 1)
            V.memset(k_aug[HD:HD + 2, :, :], 1.0).then_inc(rows_laid, 1)

            def qk_norm(base):
                for t in range(T):
                    n = base + t
                    dve.wait_ge(qk_squared, n + 1)
                    V.reduce_sum(stat[:, 0, 16 + 8 * t:24 + 8 * t],
                                 sq_tmp[:, n % 2, :].rearrange("p (a b) -> p a b", b=HD), axis=AX_X)\
                        .then_inc(qk_reduced, 1)
                dve.wait_ge(qk_reduced, base + T)
                rsqrt(slice(16, 48), HD)
                v = qk_raw.rearrange("p a (b c) -> p (a b) c", c=HD)
                V.tensor_tensor(v, v, stat[:, 3, 16:48].unsqueeze(2).broadcast_to([P, T * FOX_H, HD]), ALU.mult)\
                    .then_inc(qk_scaled, 1)

            qk_norm(0)
            qk_norm(T)
            dve.wait_ge(drained["act"], tiles["sf", T - 1][3][1])
            v0 = lf[:, 0, :].rearrange("p (t h) -> p t h", h=FOX_H)
            own(V.tensor_tensor(v0, sf[:, :, SB_H * HD:SF_W],
                                col("bf", 0, FOX_H).unsqueeze(1).broadcast_to([P, T, FOX_H]), ALU.add))
            stt(lf[:, 1, :], lf[:, 0, :], -1.0, lf[:, 0, :], ALU.mult, ALU.max).then_inc(lf_abs, 1)
            dve.wait_ge(lf_exp, 1)
            stt(lf[:, 2, :], lf[:, 0, :], 0.0, lf[:, 1, :], ALU.min, ALU.subtract).then_inc(lf_made, 1)

            full(dve, ("lfT", 0))
            one_row = xp[0:FOX_H, 2, 0:S]
            own(V.memset(one_row, 1.0))
            ins = V.tensor_tensor_scan(cum[:, 0, :], one_row, tbank(("lfT", 0))[0:FOX_H, :], 0.0, ALU.mult, ALU.add)
            drain(("lfT", 0), ins)
            dve.wait_ge(drained["dve"], order[0])
            V.tensor_scalar(cum[:, 1, :], cum[:, 0, :], -1.0, None, ALU.mult).then_inc(cum_made, 1)
            for i in range(2):
                full(dve, ("px", i))
                if i:
                    dve.wait_ge(pooled_made, i)
                a, b, c = xp[:, 0, :], xp[:, 1, :], xp[:, 2, :]
                ins = V.tensor_copy(a[:, PAD:], tbank(("px", i))[:, :])
                drain(("px", i), ins)
                dve.wait_ge(drained["dve"], order[0])
                src, dst, reach = a, b, 0
                w = 1
                halves = (WINDOWS[2 * i], WINDOWS[2 * i + 1])
                while w < halves[1]:
                    lo_p = 0 if w < halves[0] else HD
                    at = reach + w
                    own(V.tensor_tensor(dst[lo_p:, at:], src[lo_p:, at:], src[lo_p:, at - w:S + PAD - w], ALU.add))
                    if 2 * w == halves[0]:
                        own(V.tensor_copy(pooled[0:HD, i, :], dst[0:HD, PAD:]))
                    reach = at
                    w *= 2
                    src, dst = dst, (c if dst is b else b)
                own(V.tensor_copy(pooled[HD:, i, :], src[HD:, PAD:]))
                own(V.tensor_tensor(xp[:, 1, 0:PAD], pooled[:, i, 0:PAD], col("rc", i * PAD, PAD), ALU.mult))
                own(stt(pooled[:, i, :], pooled[:, i, :], col("invw", i), a[:, PAD:], ALU.mult, ALU.subtract))
                V.tensor_tensor(pooled[:, i, 0:PAD], xp[:, 1, 0:PAD], a[:, PAD:2 * PAD], ALU.subtract)\
                    .then_inc(pooled_made, 1)
            dve.wait_ge(drained["act"], tiles["pg", 1][3][1])
            for i in range(2):
                full(dve, ("y", i))
                drain(("y", i), stt(gate[:, 4 + i, :], tbank(("y", i))[:, :], col("ps", i), gate[:, 4 + i, :],
                                    ALU.mult, ALU.mult))

            def softmax_attention(base, heads, pair_out):
                steps_ = heads * T
                for m in range(steps_ + 1):
                    if m < steps_:
                        n = base + m
                        kw = (m % T + 1) * P
                        dve.wait_ge(scored, n + 1)
                        V.tensor_reduce(negmax[:, n % 8:n % 8 + 1], bank[n % 3][:, 0:kw], AX_X, ALU.max, negate=True)\
                            .then_inc(maxed, 1)
                    if m > 0:
                        n = base + m - 1
                        kw = ((m - 1) % T + 1) * P
                        dve.wait_ge(exped, n + 1)
                        own(V.reciprocal(erec[:, n % 8:n % 8 + 1], esum[:, n % 8:n % 8 + 1]))
                        V.tensor_scalar(P_buf[:, n % 4, 0:kw], P_buf[:, n % 4, 0:kw], erec[:, n % 8:n % 8 + 1],
                                        None, ALU.mult).then_inc(normed, 1)
                    if m % (2 * T) == T + 1 and m > 2 * T:
                        pair_out(m // (2 * T) - 1)
                pair_out(heads // 2 - 1)

            def fox_pair(pair):
                dve.wait_ge(pv_done, 2 * pair + 2)
                V.tensor_tensor(gate[:, pair, :], bank[6 + pair % 2][:, :], gate[:, pair, :], ALU.mult)\
                    .then_inc(pv_drained, 1)

            softmax_attention(0, FOX_H, fox_pair)
            dve.wait_ge(pv_drained, FOX_H // 2)

            def sb_abs(i):
                for n, kb in enumerate(SB_ORDER, i * T):
                    dve.wait_ge(z_full, n + (2 if kb == 1 else 1))
                    if kb == 0 and i >= 2:
                        dve.wait_ge(rest_full, (i - 1) * T)
                    r, z = sp[i % 2][:, kb, kb * P:S], z_tile(i, kb)
                    own(V.tensor_scalar(r, z, 0.0, None, ALU.max))
                    stt(ea[i % 2][:, kb, kb * P:S], r, -2.0, z, ALU.mult, ALU.add).then_inc(z_abs, 1)

            def sb_softplus(i):
                for n, kb in enumerate(SB_ORDER, i * T):
                    dve.wait_ge(z_ln, n + 1)
                    r = sp[i % 2][:, kb, kb * P:S]
                    V.tensor_tensor(r, r, ea[i % 2][:, kb, kb * P:S], ALU.add).then_inc(sp_made, 1)

            def sb_out(pair):
                dve.wait_ge(sb_full, 2 * pair + 2)
                V.tensor_tensor(gate[:, 6 + pair, :], bank[6][:, :], gate[:, 6 + pair, :], ALU.mult)\
                    .then_inc(sb_drained, 1)

            def mix_low(blocks):
                for b in blocks:
                    split_lo(None, aT_lo[:, b, :], gate[:, b, :], aT_hi[:, b, :].bitcast(F32))

            def add_out1(key, half, t):
                full(dve, (key, t))
                at = x[:, t, half * 512:(half + 1) * 512]
                xn[0] += 1
                V.tensor_tensor(at, at, tbank((key, t))[:, :], ALU.add).then_inc(x_new, 1)
                dve.wait_ge(x_new, xn[0])
                order[0] += 1
                assert tiles[key, t][3] == ("dve", order[0]), key
                V.sem_inc(drained["dve"], 1)

            dve.wait_ge(pv_done, FOX_H)
            dve.wait_ge(drained["dve"], order[0])
            V.sem_inc(gated, 1)
            sb_abs(0)
            sb_softplus(0)
            mix_low(range(6))
            sb_abs(1)
            sb_softplus(1)
            add_out1("out1a", 0, 0)
            sb_abs(2)
            sb_softplus(2)
            add_out1("out1a", 0, 1)
            sb_abs(3)
            sb_softplus(3)
            sb_out(0)
            add_out1("out1a", 0, 2)
            sb_out(1)
            dve.wait_ge(sb_drained, SB_H // 2)
            V.sem_inc(gated, 1)
            mix_low(range(6, KD))
            add_out1("out1a", 0, 3)
            dve.wait_ge(g_pre_in, 32)
            for t in range(T + 1):
                if t < T:
                    add_out1("out1b", 0, t)
                    add_out1("out1c", 1, t)
                if t > 0:
                    norm_row("h2", 4, t - 1)
                if t > 1:
                    turned_lo("h2", range(t - 2, t - 1))
            turned_lo("h2", range(T - 1, T))
            dve.wait_ge(drained["act"], tiles["lkv", T - 1][3][1])
            rsqrt(slice(48, 56), RANK)
            for t in range(T):
                own(V.tensor_scalar(lat_q[:, t, 0:RANK], lat_q[:, t, 0:RANK], stat[:, 3, 48 + t:49 + t], None,
                                    ALU.mult))
                own(V.tensor_scalar(lat_kv[:, t, :], lat_kv[:, t, :], stat[:, 3, 52 + t:53 + t], None, ALU.mult))
            V.sem_inc(lat_scaled, 1)

            def rotate(t1, t2, sn, cn, w):
                own(V.tensor_tensor(w[0], t1, cn, ALU.mult))
                own(V.tensor_tensor(w[1], t2, sn, ALU.mult))
                own(V.tensor_tensor(w[2], t2, cn, ALU.mult))
                own(V.tensor_tensor(w[3], t1, sn, ALU.mult))
                own(V.tensor_tensor(t1, w[0], w[1], ALU.subtract))
                own(V.tensor_tensor(t2, w[2], w[3], ALU.add))

            dve.wait_ge(sines, 2)
            w = [rope_t[:, j, 0:T * HALF].rearrange("p (a b) -> p a b", b=HALF) for j in range(4)]
            rotate(lat_q[:, :, RANK:RANK + HALF], lat_q[:, :, RANK + HALF:LQ_W], cs[:, 0, :, :], cs[:, 1, :, :], w)
            V.sem_inc(roped, 1)

            own(V.memset(u[:, :, 0:KERNEL - 1], 0.0))
            for j in range(4):
                dve.wait_ge(drained["act"], tiles["c", j][3][1])
                full(dve, ("xv", j))
                uj = u[:, j % 2, :]
                ins = V.tensor_tensor(uj[:, KERNEL - 1:], uj[:, KERNEL - 1:], tbank(("xv", j))[:, :], ALU.mult)
                drain(("xv", j), ins)
                dve.wait_ge(drained["dve"], order[0])
                own(V.tensor_scalar(y[:, j, :], uj[:, KERNEL - 1:], col("conv", j * KERNEL), None, ALU.mult))
                for tap in range(1, KERNEL):
                    own(stt(y[:, j, :], uj[:, KERNEL - 1 - tap:KERNEL - 1 - tap + S], col("conv", j * KERNEL + tap),
                            y[:, j, :], ALU.mult, ALU.add))
                full(dve, ("b", j))
                ins = V.tensor_tensor(y[:, j, :], y[:, j, :], tbank(("b", j))[:, :], ALU.mult)
                drain(("b", j), ins)
                dve.wait_ge(drained["dve"], order[0])
                V.sem_inc(conv_y, 1)
                dve.wait_ge(sq_y, j + 1)
                if j > 0:
                    own(V.tensor_tensor(sqs[:, 1, :], sqs[:, 1, :], sq2[:, j % 2, :], ALU.add))
            V.sem_inc(sqs_made, 1)
            for i in range(4):
                split_lo(("latT", i), aT_lo[:, i, :], tbank(("latT", i))[:, :], aT_hi[:, i, :].bitcast(F32),
                         col("gq2", i) if i < 2 else col("gkv2", i - 2))
            for j in range(4):
                split_lo(None, aT_lo[:, 4 + j, :], y[:, j, :], aT_hi[:, 4 + j, :].bitcast(F32), col("gc", j))
            dve.wait_ge(drained["act"], tiles["uq", T - 1, 1][3][1])
            for t in range(T):
                qt = q2[:, t, :].rearrange("p (h c) -> p h c", c=QK2)
                w = [rope_t[:, j, :].rearrange("p (a b) -> p a b", b=HALF) for j in range(4)]
                sn, cn = (cs[:, j, t, :].unsqueeze(1).broadcast_to([P, MLA_H, HALF]) for j in (0, 1))
                rotate(qt[:, :, HD:HD + HALF], qt[:, :, HD + HALF:], sn, cn, w)
            V.sem_inc(roped, 1)

            def group_rms(key, at):
                full(dve, (key, 0))
                rsqrt(at, 512, ss=tbank((key, 0))[:, 0:T])
                order[0] += 1
                assert tiles[key, 0][3] == ("dve", order[0]), key
                V.sem_inc(drained["dve"], 1)
                V.sem_inc(group_rsqrt, 1)

            group_rms("ssc", slice(60, 64))

            def mla_pair(pair):
                out = bank[6 + pair % 2][:, :]
                dve.wait_ge(sq_y, 4 + pair + 1)
                split_lo(None, aT_lo[:, pair, :], out, aT_hi[:, pair, :].bitcast(F32), col("ga", pair))
                if pair > 0:
                    own(V.tensor_tensor(sqs[:, 0, :], sqs[:, 0, :], sq2[:, pair % 2, :], ALU.add))
                dve.wait_ge(mix_lo, lows[0])
                V.sem_inc(pv_drained, 1)

            softmax_attention(FOX_H * T, MLA_H, mla_pair)
            V.sem_inc(sqs_made, 1)

            def add_post(t, halves, at):
                for n, (lo_c, hi_c, value) in enumerate(halves):
                    w = post_t[:, t % 2, lo_c:hi_c]
                    own(stt(w, value, stat[:, 3, at:at + 1], g_post[:, lo_c:hi_c], ALU.mult, ALU.mult))
                xn[0] += 1
                V.tensor_tensor(x[:, t, :], x[:, t, :], post_t[:, t % 2, :], ALU.add).then_inc(x_new, 1)

            def out2_row(t):
                for g in range(2):
                    key = ("out2a", t, g)
                    full(dve, key)
                    at = y2[t][:, g * 512:(g + 1) * 512]
                    if (t, g) == (0, 0):
                        full(dve, ("ssa", 0))
                        rsqrt(slice(56, 60), 512, ss=tbank(("ssa", 0))[:, 0:T])
                    stt(at, tbank(key)[:, :], stat[:, 3, 56 + t:57 + t], at, ALU.mult, ALU.add).then_inc(y2_made, 1)
                    dve.wait_ge(y2_made, 2 * t + g + 1)
                    if t < T - 1:
                        order[0] += 1
                        assert tiles[key][3] == ("dve", order[0]), key
                    V.sem_inc(drained[tiles[key][3][0]], 1)
                if t == 0:
                    order[0] += 1
                    V.sem_inc(drained["dve"], 1)

            def h3_row(t):
                if t >= 2:
                    full(dve, ("h3", 2 * (t - 2) + 1))
                at = 9 + 2 * (t + 1)
                stt(h[:, t % 2, :], x[:, t, :], stat[:, 3, at:at + 1], g_pre[:, :], ALU.mult, ALU.mult)\
                    .then_inc(h_made, 1)

            dve.wait_ge(g_post_in, 16)
            dve.wait_ge(g_pre_in, 48)
            for t in range(T + 1):
                if t < T:
                    out2_row(t)
                if t == 0:
                    for k in range(2):
                        dve.wait_ge(p_hi, k + 1)
                        V.tensor_tensor(aT_lo[:, 4 + k, :], pe_raw[:, k, :], aT_hi[:, 4 + k, :].bitcast(F32),
                                        ALU.subtract).then_inc(p_split, 1)
                if t == 3:
                    turned_lo("h3", range(1, 2))
                sqn[0] += 1 if t in (0, T) else 2
                dve.wait_ge(sq_done, sqn[0])
                rsqrt(slice(8 + 2 * t + (t == T), 9 + 2 * t + (t > 0)), D)
                if t < T:
                    add_post(t, [(0, D, y2[t])], 8 + 2 * t)
                if t > 0:
                    h3_row(t - 1)
                if t == 2:
                    turned_lo("h3", range(0, 1))

            turned_lo("h3", range(T - 2, T))
            dve.wait_ge(g_post_in, 32)
            sqn[0] += T
            dve.wait_ge(sq_done, sqn[0])
            rsqrt(slice(40, 44), D)
            for t in range(T):
                own(stt(emb[:, t, :], emb[:, t, :], stat[:, 3, 40 + t:41 + t], g_post[:, :], ALU.mult, ALU.mult))
            V.sem_inc(emb_made, 1)

            def ffn_rows(f, slot, c):
                dve.wait_ge(ffn_gate, f + 1)
                dve.wait_ge(w_used, c + 2)
                V.tensor_tensor(act[:, bass.ds(f, 1), :], sg_t[:, slot, :].unsqueeze(1),
                                bank[2 * slot + 1][:, :].unsqueeze(1), ALU.mult).then_inc(ffn_act, 1)

            for f in range(2):
                ffn_rows(f, f, CH["ffn"] + 2 * f)
            with dve.Fori(1, NF // 2) as i:
                for f in range(2):
                    ffn_rows(i * 2 + f, f, i * 4 + (CH["ffn"] + 2 * f))

            def stage(k, slot):
                dve.wait_ge(stage_hi, k + 1)
                V.tensor_tensor(aT_lo[:, slot, :].unsqueeze(1), act[:, bass.ds(k, 1), :],
                                aT_hi[:, slot, :].bitcast(F32).unsqueeze(1), ALU.subtract).then_inc(staged, 1)

            dve.wait_ge(ffn_act, NF)
            for k in range(4):
                stage(k, k)
            with dve.Fori(1, NF // 4) as i:
                for j in range(4):
                    stage(i * 4 + j, j)
            for k in range(NF // 4 * 4, NF):
                stage(k, k % 4)

            dve.wait_ge(g_post_in, 48)
            for t in range(T):
                if t == T - 1:
                    turned_lo("xT", range(0, 1))
                sqn[0] += 2
                dve.wait_ge(sq_done, sqn[0])
                own(V.tensor_tensor(stat[:, 0, 24 + t:25 + t], stat[:, 0, 16 + 2 * t:17 + 2 * t],
                                    stat[:, 0, 17 + 2 * t:18 + 2 * t], ALU.add))
                rsqrt(slice(24 + t, 25 + t), D)
                if t == T - 1:
                    turned_lo("xT", range(1, T - 1))
                add_post(t, [(g * 512, (g + 1) * 512, tbank(("down", t, g))[:, :]) for g in range(2)], 24 + t)
                for g in range(2):
                    if t < T - 1:
                        order[0] += 1
                    V.sem_inc(drained[tiles["down", t, g][3][0]], 1)

            turned_lo("xT", range(T - 1, T))
            for g in range(2):
                for t in range(T):
                    n = g * T + t
                    dve.wait_ge(pgate_made, n + 1)
                    s = gate_t[:, n % 2, :]
                    own(V.tensor_tensor(s, s, emb[:, t, g * 512:(g + 1) * 512], ALU.mult))
                    at = x[:, t, g * 512:(g + 1) * 512]
                    V.tensor_tensor(at, at, s, ALU.add).then_inc(out_made, 1)


def cut_moving(w, ks, at=slice(None)):
    c = np.concatenate([w[k * P:(k + 1) * P, at] for k in ks], axis=1)
    return np.pad(c, ((0, 0), (0, CW - c.shape[1])))


def cut_still(w, at):
    return w[:, at].reshape(KD, P, P).transpose(1, 0, 2).reshape(P, CW)


def lay_out_weights(w_in, w_out, w_in2, w_uq, w_ukv, w_out2, w_gate, w_up, w_down, w_ple, w_pgate):
    c = []
    pairs = [(0, 1), (2, 3), (4, 5), (6, 7)]
    threes = [(0, 1, 2), (3, 4, 5), (6, 7)]
    fq, fk, fv, fg, ff, px, pg, sq, sk, sv, sg = (
        0, 512, 1024, 1536, 2048, 2056, 2312, 2568, 2824, 3080, 3336)

    def moving(w, at, groups):
        c.extend(cut_moving(w, ks, at) for ks in groups)

    def still(w, at, n):
        c.extend(cut_still(w, slice(at + i * P, at + (i + 1) * P)) for i in range(n))

    for at in (fq, fv, fk):
        moving(w_in, slice(at, at + S), pairs)
    moving(np.concatenate([w_in[:, sv:sv + SB_H * HD], w_in[:, ff:ff + FOX_H]], axis=1), slice(None), threes)
    for at, n in ((pg, 2), (px, 2), (fg, 4), (sg, 2), (sq, 2), (sk, 2)):
        still(w_in, at, n)
    for half in (pairs[:3], pairs[3:]):
        for g in range(2):
            moving(w_out, slice(g * 512, (g + 1) * 512), half)
    kr, cb, cc, cx = 2 * RANK, 2 * RANK + ROPE, 2 * RANK + ROPE + 512, 2 * RANK + ROPE + 1024
    moving(np.concatenate([w_in2[:, :RANK], w_in2[:, kr:kr + ROPE]], axis=1), slice(None), threes)
    moving(w_in2, slice(RANK, 2 * RANK), [(0, 1, 2, 3), (4, 5, 6, 7)])
    for j in range(4):
        for at in (cc, cx, cb):
            still(w_in2, at + j * P, 1)
    moving(w_uq, slice(None), [(0,), (1,)])
    by_head = w_ukv.reshape(RANK, MLA_H, 2, HD)
    for part in range(2):
        moving(by_head[:, :, part, :].reshape(RANK, 512), slice(None), [(0, 1)])
    for half in (pairs[2:], pairs[:2]):
        for g in range(2):
            moving(w_out2, slice(g * 512, (g + 1) * 512), half)
    for g in range(2):
        moving(w_ple, slice(g * 512, (g + 1) * 512), [(0, 1)])
    for f in range(NF):
        still(w_gate, f * P, 1)
        still(w_up, f * P, 1)
    moving(w_down, slice(None), [(k,) for k in range(NF)])
    for g in range(2):
        moving(w_pgate, slice(g * 512, (g + 1) * 512), pairs)
    return np.ascontiguousarray(np.stack(c))


def by_partition(v):
    return v.reshape(-1, P).T


def kernel(**inputs):
    import concourse.bacc as _bacc
    from concourse.bass_utils import run_bass_kernel_spmd as _run

    a = {k: np.asarray(v) for k, v in inputs.items()}
    w = lay_out_weights(a["w_in"][0], a["w_out"][0], a["w_in_2"][0], a["w_uq_2"][0], a["w_ukv_2"][0], a["w_out_2"][0],
                        a["w_gate_2"][0], a["w_up_2"][0], a["w_down_2"][0], a["w_ple_proj_2"][0], a["w_ple_gate_2"][0])
    f32 = np.float32
    halves = np.repeat(np.array(WINDOWS, f32).reshape(2, 2), HD, axis=1)
    rc = 1 / np.minimum(np.arange(1, PAD + 1, dtype=f32)[None, None, :], halves[:, :, None])
    invf = (1.0 / (f32(10000.0) ** (np.arange(HALF, dtype=f32) / f32(HALF)))).astype(f32)
    cols = np.concatenate([
        np.tile(a["q_norm_g"][0], 2)[:, None], np.tile(a["k_norm_g"][0], 2)[:, None],
        by_partition(a["q_norm_2"][0]), by_partition(a["kv_norm_2"][0]),
        a["conv_w_2"][0].reshape(KERNEL, 4, P).transpose(2, 1, 0).reshape(P, 4 * KERNEL),
        by_partition(a["attn_group_norm_2"][0]), by_partition(a["conv_group_norm_2"][0]),
        by_partition(a["pool_scale"][0]),
        np.broadcast_to(a["b_f"][0][None, :], (P, FOX_H)), np.broadcast_to(invf[None, :], (P, HALF)),
        rc.transpose(1, 0, 2).reshape(P, 2 * PAD).astype(f32), (1 / halves).T.astype(f32),
    ], axis=1)
    pos = a["positions_2"].reshape(T, P).T
    wpool = np.zeros((P, 2, P), f32)
    for g in range(4):
        r = slice((g % 2) * HD, (g % 2 + 1) * HD)
        wpool[r, g // 2, r] = a["w_pool"][0, g]
    pt = a["p_2"][0, 0].T.reshape(2, P, S).transpose(1, 0, 2)
    gains = np.stack([np.broadcast_to(a[n][0][None, :], (P, D)) for n in (
        "norm_g", "mix_pre_norm_2", "ffn_pre_norm_2", "mix_post_norm_2", "ffn_post_norm_2", "ple_norm_2")])
    arrays = {"x": a["x"].reshape(S, D), "weights": w, "cols": cols, "pos": pos, "wpool": wpool, "pt": pt,
              "gains": gains}
    arrays = {k: np.ascontiguousarray(v) for k, v in arrays.items()}
    nc = _bacc.Bacc("TRN2", target_bir_lowering=False, num_devices=1)
    args = [nc.dram_tensor("in_" + k, v.shape, mybir.dt.from_np(v.dtype), kind="ExternalInput").ap() for k, v in arrays.items()]
    out = nc.dram_tensor("y_out", (S, D), F32, kind="ExternalOutput").ap()
    hybrid_kernel(nc, *args, out)
    r = _run(nc, [{"in_" + k: v for k, v in arrays.items()}], core_ids=[0])
    return r.results[0]["y_out"].reshape(1, S, D)
```
